# Optimizing a Trainium2 kernel written in Bass

```python
import jax, jax.numpy as jnp
from jax import lax
import numpy as np

D_MODEL = 1024
BATCH = 1
SEQ = 512
DEPTH = 1
DEC_BATCH = 8
DEC_SEQ = 4
PAST_LEN = 4096
PAGE_SIZE = 128

CHUNK = 128
D_A = D_MODEL
H_A = 4
DH_A = D_A // H_A
D_RNN = D_MODEL
H_B = 8
BLK_B = D_RNN // H_B
CONV_W = 4
LRU_C = 8.0
N_GROUPS = 4
E_PER_GROUP = 8
N_EXPERTS = N_GROUPS * E_PER_GROUP
D_EXPERT = 256
TOP_K_INNER = 2
EPS = 1e-6
D_IN = 2 * D_A + D_RNN + 2 * D_MODEL
SPLITS = (D_A, 2 * D_A, 2 * D_A + D_RNN, 2 * D_A + D_RNN + D_MODEL)

kernel_name = 'hybrid_gmlp_rglru_hmoe_step'

def rms_norm(x, g):
    xf = x.astype(jnp.float32)
    y = xf * lax.rsqrt(jnp.mean(xf * xf, axis=-1, keepdims=True) + EPS)
    return (y * g.astype(jnp.float32)).astype(x.dtype)

def layer_norm(x, g, b):
    xf = x.astype(jnp.float32)
    xc = xf - jnp.mean(xf, axis=-1, keepdims=True)
    var = jnp.mean(xc * xc, axis=-1, keepdims=True)
    return (xc * lax.rsqrt(var + EPS) * g.astype(jnp.float32) + b.astype(jnp.float32)).astype(x.dtype)

def chunk_spatial_gating(u, v, w_s, b_s):
    n, s, _ = v.shape
    n_chunks = -(-s // CHUNK)
    pad = n_chunks * CHUNK - s
    vc = jnp.pad(v, ((0, 0), (0, pad), (0, 0))).reshape(n, n_chunks, CHUNK, H_A, DH_A)
    causal = jnp.tril(jnp.ones((CHUNK, CHUNK), dtype=bool))
    w = jnp.where(causal, w_s, jnp.zeros_like(w_s)).astype(v.dtype)
    z = jnp.einsum('hts,bcshk->bcthk', w, vc) + jnp.transpose(b_s).astype(v.dtype)[None, None, :, :, None]
    z = z.reshape(n, n_chunks * CHUNK, D_A)[:, :s]
    return u * z

def causal_depthwise_conv(x, buf, w, b):
    s = x.shape[1]
    xp = jnp.concatenate([buf.astype(x.dtype), x], axis=1)
    y = b.astype(x.dtype) + xp[:, 0:s] * w[0]
    for k in range(1, CONV_W):
        y = y + xp[:, k:k + s] * w[k]
    return y, xp[:, s:]

def block_diag_linear(x, w, b):
    xb = x.reshape(x.shape[:-1] + (H_B, BLK_B))
    y = jnp.einsum('bshi,hij->bshj', xb, w) + b
    return y.reshape(x.shape)

def rg_lru(x, h0, lam, w_a, b_a, w_x, b_x):
    r = jax.nn.sigmoid(block_diag_linear(x, w_a, b_a)).astype(jnp.float32)
    i = jax.nn.sigmoid(block_diag_linear(x, w_x, b_x))
    log_a = -LRU_C * r * jax.nn.softplus(-lam.astype(jnp.float32))
    a = jnp.exp(log_a)
    mult = jnp.sqrt(-jnp.expm1(2.0 * log_a))
    if h0 is None:
        mult = mult.at[:, 0].set(1.0)
    bt = mult * (i * x).astype(jnp.float32)
    if h0 is not None:
        bt = bt.at[:, 0].add(a[:, 0] * h0.astype(jnp.float32))

    def combine(left, right):
        a1, b1 = left
        a2, b2 = right
        return a1 * a2, a2 * b1 + b2

    _, h = lax.associative_scan(combine, (a, bt), axis=1)
    return h.astype(x.dtype), h[:, -1].astype(x.dtype)

def mixer_sublayer(x, h0, conv_buf, norm_g, w_in, ln_g, ln_b, w_s, b_s, conv_w, conv_b,
                   lam, w_a, b_a, w_x, b_x, w_out):
    s = x.shape[1]
    xn = rms_norm(x, norm_g)
    proj = xn @ w_in
    u, v, xr, g_a, g_b = jnp.split(proj, SPLITS, axis=-1)
    u = jax.nn.gelu(u)
    v = layer_norm(jax.nn.gelu(v), ln_g, ln_b)
    y_a = chunk_spatial_gating(u, v, w_s, b_s)
    if conv_buf is None:
        conv_buf = jnp.zeros((x.shape[0], CONV_W - 1, D_RNN), x.dtype)
    xc, new_buf = causal_depthwise_conv(xr, conv_buf, conv_w, conv_b)
    y_b, h_last = rg_lru(xc, h0, lam, w_a, b_a, w_x, b_x)
    merged = jax.nn.sigmoid(g_a) * y_a + jax.nn.sigmoid(g_b) * y_b
    v_rows = v[:, ((s - 1) // CHUNK) * CHUNK:]
    return x + merged @ w_out, h_last, new_buf, v_rows

def hier_moe(x, w_rg, b_rg, w_re, b_re, w_gate, w_up, w_down):
    shp = x.shape
    xf = x.reshape(-1, D_MODEL)
    pg = jax.nn.softmax((xf @ w_rg + b_rg).astype(jnp.float32), axis=-1)
    pg_top, g_idx = lax.top_k(pg, 1)
    e_logits = (xf @ w_re + b_re).astype(jnp.float32).reshape(-1, N_GROUPS, E_PER_GROUP)
    e_in = jnp.take_along_axis(e_logits, g_idx[:, :, None], axis=1)[:, 0]
    pe = jax.nn.softmax(e_in, axis=-1)
    pe_top, e_idx = lax.top_k(pe, TOP_K_INNER)
    w = pg_top * pe_top / jnp.sum(pe_top, axis=-1, keepdims=True)
    expert = g_idx * E_PER_GROUP + e_idx
    gates = jnp.sum(jax.nn.one_hot(expert, N_EXPERTS, dtype=jnp.float32) * w[..., None], axis=1)
    h = jax.nn.silu(jnp.einsum('td,edf->tef', xf, w_gate)) * jnp.einsum('td,edf->tef', xf, w_up)
    h = h * gates.astype(h.dtype)[..., None]
    y = jnp.einsum('tef,efd->td', h, w_down)
    return y.reshape(shp)

def setup_inputs(seed: int = 0) -> dict:
    key = jax.random.key(seed)
    ks = jax.random.split(key, 32)
    f32 = jnp.float32
    nrm = lambda k, shape, scale: jax.random.normal(k, shape, f32) * scale
    a_c = jax.random.uniform(ks[10], (DEPTH, D_RNN), f32, 0.9, 0.999)
    a0 = a_c ** (1.0 / LRU_C)
    return {
        'x_prompt': nrm(ks[0], (BATCH, SEQ, D_MODEL), 1.0),
        'x_sample': nrm(ks[1], (DEC_BATCH, DEC_SEQ, D_MODEL), 1.0),
        'state_lru_h': nrm(ks[2], (DEPTH, DEC_BATCH, D_RNN), 0.5),
        'state_conv': nrm(ks[3], (DEPTH, DEC_BATCH, CONV_W - 1, D_RNN), 1.0),
        'norm1': 1.0 + nrm(ks[4], (DEPTH, D_MODEL), 0.05),
        'w_in': nrm(ks[5], (DEPTH, D_MODEL, D_IN), D_MODEL ** -0.5),
        'ln_g': 1.0 + nrm(ks[6], (DEPTH, D_A), 0.05),
        'ln_b': nrm(ks[7], (DEPTH, D_A), 0.05),
        'w_s': nrm(ks[8], (DEPTH, H_A, CHUNK, CHUNK), CHUNK ** -0.5),
        'b_s': 1.0 + nrm(ks[9], (DEPTH, H_A, CHUNK), 0.1),
        'conv_w': nrm(ks[11], (DEPTH, CONV_W, D_RNN), CONV_W ** -0.5),
        'conv_b': nrm(ks[12], (DEPTH, D_RNN), 0.02),
        'lru_lambda': jnp.log(a0) - jnp.log1p(-a0),
        'w_rg_a': nrm(ks[13], (DEPTH, H_B, BLK_B, BLK_B), BLK_B ** -0.5),
        'b_rg_a': nrm(ks[14], (DEPTH, H_B, BLK_B), 0.02),
        'w_rg_x': nrm(ks[15], (DEPTH, H_B, BLK_B, BLK_B), BLK_B ** -0.5),
        'b_rg_x': nrm(ks[16], (DEPTH, H_B, BLK_B), 0.02),
        'w_out': nrm(ks[17], (DEPTH, D_MODEL, D_MODEL), D_MODEL ** -0.5),
        'norm2': 1.0 + nrm(ks[18], (DEPTH, D_MODEL), 0.05),
        'w_route_group': nrm(ks[19], (DEPTH, D_MODEL, N_GROUPS), D_MODEL ** -0.5),
        'b_route_group': nrm(ks[20], (DEPTH, N_GROUPS), 0.01),
        'w_route_expert': nrm(ks[21], (DEPTH, D_MODEL, N_EXPERTS), D_MODEL ** -0.5),
        'b_route_expert': nrm(ks[22], (DEPTH, N_EXPERTS), 0.01),
        'w_gate': nrm(ks[23], (DEPTH, N_EXPERTS, D_MODEL, D_EXPERT), D_MODEL ** -0.5),
        'w_up': nrm(ks[24], (DEPTH, N_EXPERTS, D_MODEL, D_EXPERT), D_MODEL ** -0.5),
        'w_down': nrm(ks[25], (DEPTH, N_EXPERTS, D_EXPERT, D_MODEL), D_EXPERT ** -0.5),
        'norm_f': 1.0 + nrm(ks[26], (D_MODEL,), 0.05),
    }

def reference(x_prompt, x_sample, state_lru_h, state_conv, norm1, w_in, ln_g, ln_b, w_s, b_s,
              conv_w, conv_b, lru_lambda, w_rg_a, b_rg_a, w_rg_x, b_rg_x, w_out, norm2,
              w_route_group, b_route_group, w_route_expert, b_route_expert,
              w_gate, w_up, w_down, norm_f):
    yp, ys = x_prompt, x_sample
    hp, cp, vp, hs, cs, vs = [], [], [], [], [], []
    for l in range(DEPTH):
        mix_w = (norm1[l], w_in[l], ln_g[l], ln_b[l], w_s[l], b_s[l], conv_w[l], conv_b[l],
                 lru_lambda[l], w_rg_a[l], b_rg_a[l], w_rg_x[l], b_rg_x[l], w_out[l])
        moe_w = (w_route_group[l], b_route_group[l], w_route_expert[l], b_route_expert[l],
                 w_gate[l], w_up[l], w_down[l])
        yp, h, c, v = mixer_sublayer(yp, None, None, *mix_w)
        hp.append(h)
        cp.append(c)
        vp.append(v)
        ys, h, c, v = mixer_sublayer(ys, state_lru_h[l], state_conv[l], *mix_w)
        hs.append(h)
        cs.append(c)
        vs.append(v)
        yp = yp + hier_moe(rms_norm(yp, norm2[l]), *moe_w)
        ys = ys + hier_moe(rms_norm(ys, norm2[l]), *moe_w)
    yp = rms_norm(yp, norm_f)
    ys = rms_norm(ys, norm_f)
    return (yp, ys, jnp.stack(hp), jnp.stack(cp), jnp.stack(vp), jnp.stack(hs), jnp.stack(cs), jnp.stack(vs))


_drawn_inputs = setup_inputs


def setup_inputs(seed=0):
    import zlib

    import numpy as np

    out = dict(_drawn_inputs(seed))
    spreads = {}
    factors = {'b_rg_a': 5.34, 'b_rg_x': 5.368, 'b_route_group': 8.0, 'b_route_expert': 3.867}
    for name, (base, spread) in spreads.items():
        noise = np.random.default_rng([zlib.crc32(name.encode()), seed]).standard_normal(out[name].shape)
        drawn = base * np.exp(spread * noise) if base else spread * noise
        out[name] = __import__('jax').numpy.asarray(drawn.astype(out[name].dtype))
    for name, factor in factors.items():
        out[name] = (out[name] * factor).astype(out[name].dtype)
    return out
```

```python
from contextlib import ExitStack

import concourse.bass as bass
from concourse import mybir

P = 128
D = 1024
KT = D // P
SEQ = 512
NT = SEQ // P
DB, DS = 8, 4
S = DB * DS
TA = SEQ + S
TILES = NT + 1
HEADS = 4
TAPS = 4
NG, EG = 4, 8
NE = NG * EG
NL = NG + NE
FE = 256
CAP = 64
PAIRS = NE // 2
SLOTROWS = NE * CAP
MAXPASS = -(-TA // CAP)
EPS = 1e-6
UNITS_V, UNITS_J, UNITS_O = 8, 32, 8
RAW = 4
OUTC = 36
(C_G1, C_W0, C_CB, C_LAM, C_BA, C_BX, C_H0, C_ST) = (0, 1, 5, 6, 7, 8, 9, 17)
NCH = 41
OUT_OF_RANGE = 4096.0
FIRST = 1

F32 = mybir.dt.float32
F32R = mybir.dt.float32r
BF16 = mybir.dt.bfloat16
I32 = mybir.dt.int32
U32 = mybir.dt.uint32
ALU = mybir.AluOpType
ACT = mybir.ActivationFunctionType
AX = mybir.AxisListType.X

GELU_K = 0.7978845608028654
GELU_C = 0.044715


class Steps:

    def __init__(self, eng, sem):
        self.eng, self.sem, self.base, self.n = eng, sem, 0, 0

    def then(self, ins):
        self.n += 1
        ins.then_inc(self.sem, 1)
        self.eng.wait_ge(self.sem, self.base + self.n)

    def enter(self, i, per):
        self.start, self.per = self.base + self.n, per
        self.base, self.n = self.start + i * per, 0

    def leave(self, times):
        assert self.n == self.per, (self.n, self.per)
        self.base, self.n = self.start + times * self.per, 0


def build(nc, x, wmix, wgate, chan, wst, bs, rows, wr, br, wmoe, y, vp, vs, st):
    xsort = nc.dram_tensor("xsort", (SLOTROWS, D), F32, kind="Internal").ap()
    ysort = nc.dram_tensor("ysort", (SLOTROWS, D), F32, kind="Internal").ap()

    def at(name, offset, shape, dt=F32):
        return nc.alloc_sbuf_tensor_at(name, shape, dt, offset=BASE + offset)

    K = 1024
    BASE = -(-nc.sbuf_base // 64) * 64
    EW = 6144
    wslot = [at(f"wslot{s}", s * 24 * K, [P, EW]) for s in range(4)]
    xh = at("xh", 48 * K, [P, KT, SEQ], F32R)
    xl = at("xl", 64 * K, [P, KT, SEQ], F32R)
    zT = at("zT", 80 * K, [P, KT, TA])
    R_V = 97 * K
    v = at("v", R_V, [P, TILES, D])
    x1 = at("x1", R_V, [P, TILES, D])
    tw = TA * 4
    XRW = 3 + SEQ + DB * 7
    (XC, A, TR, TI, M, U, U1, GA) = [at(n, R_V + i * tw, [P, TA]) for i, n in
                                     enumerate(("xc", "a", "tr", "ti", "m", "u", "u1", "ga"))]
    XR = at("xr", R_V + 8 * tw, [P, XRW])
    R_M = 117 * K
    mh = at("mh", R_M, [P, KT, SEQ], F32R)
    ml = at("ml", R_M + 16 * K, [P, KT, SEQ], F32R)
    xt = at("xt", R_M, [P, TILES, D])
    lng = at("lng", R_M + 20 * K, [P, D])
    lnb = at("lnb", R_M + 24 * K, [P, D])
    junk = at("junk", R_M + 28 * K, [P, D])
    xn2 = at("xn2", R_M, [P, TILES, D])
    xg = at("xg", R_M + 20 * K, [P, 2, D])
    nf = at("nf", R_M + 28 * K, [P, D])
    R_W = 149 * K
    raw = at("raw", R_W, [P, RAW, KT, P])
    wh = at("wh", R_W + 16 * K, [P, 2, D], F32R)
    wl = at("wl", R_W + 24 * K, [P, 2, D], F32R)
    xn2T = at("xn2T", R_W, [P, KT, TA])
    g2 = at("g2", R_W + 17 * K, [P, D])
    junk2 = at("junk2", R_W + 21 * K, [P, D])
    xgT = at("xgT", R_W, [P, 2, KT, P])
    yo = at("yo", R_W + 8 * K, [P, 2, D])
    hs = at("hs", R_W + 16 * K, [P, 2, FE])
    hm = at("hm", R_W + 18 * K, [P, 2, FE])
    hT = at("hT", R_W + 20 * K, [P, 2, 2, P])
    gy = at("gy", R_W + 22 * K, [P, 2, D])
    top = [181 * K]

    def small(name, shape, dt=F32):
        size = 4
        for n in shape[1:]:
            size *= n
        t = at(name, top[0], shape, dt)
        top[0] += -(-size // 32) * 32
        return t

    ch = small("ch", [P, KT, NCH])
    ident = small("ident", [P, P])
    ones = small("ones", [P, P], F32)
    upper = small("upper", [P, P], F32)
    fold = small("fold", [P, S])
    wsT = small("wsT", [P, HEADS, P])
    bdiag = small("bdiag", [S, HEADS, S])
    bsh = small("bsh", [P, HEADS, P])
    gw = small("gw", [P, 2, P])
    xs = small("xs", [P, KT, S])
    ms = small("ms", [P, KT, S])
    sp = small("sp", [P, 512])
    sq = small("sq", [P, 4, S])
    gbs = small("gbs", [P, S])
    so = small("so", [P, KT, OUTC])
    zero = small("zero", [P, D // 4])
    wrt = small("wrt", [P, KT, NL])
    brt = small("brt", [NL, 1])
    ss = small("ss", [P, TILES])
    rstd = small("rstd", [P, TILES])
    bnst = small("bnst", [P, 2, 6])
    bnag = small("bnag", [P, TILES, 2])
    csp = small("csp", [P, KT, 2])
    hb = small("hb", [P, KT, 2])
    t8 = small("t8", [P, 5, KT])
    lgT = small("lgT", [NL, TA])
    lg = small("lg", [P, TILES, NL])
    r4 = small("r4", [P, TILES, NG])
    oh = small("oh", [P, TILES, NG])
    r1 = small("r1", [P, 8, TILES])
    ein = small("ein", [P, TILES, EG])
    e8 = small("e8", [P, TILES, EG])
    o8 = small("o8", [P, 2, TILES, EG])
    big = small("big", [P, TILES, NE])
    ohe = small("ohe", [P, 2, TILES, NE])
    mcnt = small("mcnt", [P, TILES, NE])
    rank = small("rank", [P, TILES, NE])
    first = small("first", [P, EG])
    ebase = small("ebase", [P, NE])
    thr = small("thr", [P, MAXPASS])
    gate = small("gate", [P, 2, TILES])
    rk = small("rk", [P, 2, TILES])
    bp = small("bp", [P, 2, TILES])
    gk = small("gk", [P, 2, TILES])
    pk = small("pk", [P, 2, TILES])
    pf = small("pf", [P, 2, TILES])
    pidx = small("pidx", [P, 2, TILES], U32)
    npf = small("npf", [P, 2])
    npi = small("npi", [1, 1], I32)
    assert BASE + top[0] <= nc.sbuf_usable_end, top[0] / K

    with ExitStack() as ctx:
        ps = ctx.enter_context(nc.psum_tensor("ps", [P, 8, 512], F32))

        def sem(name):
            return ctx.enter_context(nc.semaphore(name))

        x_in = [sem(f"x_in{t}") for t in range(TILES)]
        const_in = sem("const_in")
        raw_in = [sem(f"raw_in{s}") for s in range(RAW)]
        slot_in = [sem(f"slot_in{s}") for s in range(4)]
        gw_in = sem("gw_in")
        xres_in = sem("xres_in")
        bd_in = sem("bd_in")
        masks = sem("masks")
        zeroed = sem("zeroed")
        xg_in = [sem("xg_in0"), sem("xg_in1")]
        scattered = sem("scattered")
        gathered = [sem("gathered0"), sem("gathered1")]
        y_out = [sem("y_out0"), sem("y_out1")]
        v_stored = sem("v_stored")
        done_out = sem("done_out")

        held = sem("held")
        act_s = sem("act_s")
        dve_s = sem("dve_s")
        pool_s = sem("pool_s")

        ss_ready = sem("ss_ready")
        ms_ready = sem("ms_ready")
        sq_ready = sem("sq_ready")
        xn_ready = sem("xn_ready")
        xT_ready = sem("xT_ready")
        xh_ready = sem("xh_ready")
        xl_ready = sem("xl_ready")
        xs_ready = sem("xs_ready")
        hi_ready = sem("hi_ready")
        lo_ready = sem("lo_ready")
        unit_done = sem("unit_done")
        vsum = sem("vsum")
        vfold = sem("vfold")
        v_gelu = sem("v_gelu")
        v_ready = sem("v_ready")
        z_mm = sem("z_mm")
        z_ready = sem("z_ready")
        sproj = sem("sproj")
        sproj_sb = sem("sproj_sb")
        sproj_T = sem("sproj_T")
        sq_sb = sem("sq_sb")
        xr_ev = sem("xr_ev")
        u_ev = sem("u_ev")
        ga_ev = sem("ga_ev")
        gb_ev = sem("gb_ev")
        u_sq = sem("u_sq")
        u_poly = sem("u_poly")
        u_tanh = sem("u_tanh")
        u_free = sem("u_free")
        conv_done = sem("conv_done")
        gates_mm = sem("gates_mm")
        gates_ev = sem("gates_ev")
        a_ready = sem("a_ready")
        m_poly = sem("m_poly")
        m_sqrt = sem("m_sqrt")
        ya_done = sem("ya_done")
        merged = sem("merged")
        x1_ready = sem("x1_ready")
        n2_ms = sem("n2_ms")
        n2_sq = sem("n2_sq")
        xn2_ready = sem("xn2_ready")
        xn2T_mm = sem("xn2T_mm")
        xn2T_sb = [sem("xn2T_even"), sem("xn2T_odd")]
        lg_mm = sem("lg_mm")
        lg_sb = sem("lg_sb")
        lgt_mm = sem("lgt_mm")
        ex_in = sem("ex_in")
        ex_out = sem("ex_out")
        cnt_in = sem("cnt_in")
        rank_mm = sem("rank_mm")
        passes_ready = sem("passes_ready")
        pidx_ready = sem("pidx_ready")
        xgT_mm = sem("xgT_mm")
        xgT_sb = sem("xgT_sb")
        gu_mm = sem("gu_mm")
        silu_done = sem("silu_done")
        hm_ready = sem("hm_ready")
        hT_mm = sem("hT_mm")
        hT_sb = sem("hT_sb")
        pair_mm = sem("pair_mm")
        yo_sb = sem("yo_sb")
        comb = sem("comb")
        fin_ms = sem("fin_ms")
        fin_sq = sem("fin_sq")
        fin_ready = sem("fin_ready")
        so_ready = sem("so_ready")

        block = ctx.enter_context(nc.Block())

        def rowsof(t):
            return S if t == NT else P

        xp_tiles = [x[t * P:t * P + rowsof(t), :] for t in range(TILES)]
        y_tiles = [y[t * P:t * P + rowsof(t), :] for t in range(TILES)]
        NCONST = 16 * 9

        def v_banks(half):
            return ([0, 1, 2, 3], 4, 6) if half == 0 else ([5, 7, 0, 1], 2, 3)

        @block.sync
        def _(sp_):
            e = sp_
            for t in range(TILES):
                e.dma_start(xt[0:rowsof(t), t, :], xp_tiles[t]).then_inc(x_in[t], 16)
            e.dma_start(ch[:], chan).then_inc(const_in, 16)
            for n in range(4):
                e.dma_start(raw[:, n, :, :], wmix[n]).then_inc(raw_in[n], 16)
            e.dma_start(lng[:], rows[0:1, :].broadcast_to([P, D])).then_inc(const_in, 16)
            e.dma_start(lnb[:], rows[1:2, :].broadcast_to([P, D])).then_inc(const_in, 16)
            e.dma_start(wsT[:], wst).then_inc(const_in, 16)
            e.dma_start(bsh[:], bs.broadcast_to([P, HEADS * P]).rearrange("p (h t) -> p h t", h=HEADS)).then_inc(const_in, 16)
            e.dma_start(wrt[:], wr).then_inc(const_in, 16)
            e.dma_start(brt[:], br).then_inc(const_in, 16)
            e.wait_ge(masks, 1)
            for b in range(DB):
                e.dma_start(bdiag[4 * b:4 * b + 4, :, 4 * b:4 * b + 4],
                            wst[0:4, :, 0:4]).then_inc(bd_in, 16)
            for n in range(4, 12):
                e.wait_ge(lo_ready, n - 3)
                e.wait_ge(unit_done, n - 3)
                e.dma_start(raw[:, n % RAW, :, :], wmix[n]).then_inc(raw_in[n % RAW], 16)
            for s in range(2):
                e.dma_start(wslot[s][:], wmoe[s]).then_inc(slot_in[s], 16)
            with e.Fori(0, KT) as j:
                for p in range(4):
                    e.wait_ge(lo_ready, j * 4 + (8 + p + 1))
                    e.sem_inc(held, 1)
                    e.wait_ge(sproj, j + 1)
                    e.sem_inc(held, 1)
                    e.dma_start(raw[:, p, :, :], wmix[bass.ds(j * 4 + (12 + p), 1)].rearrange("a p k c -> (a p) k c")).then_inc(raw_in[p], 16)
            e.wait_ge(merged, FIRST + KT)
            for t in range(TILES):
                e.dma_start(x1[0:rowsof(t), t, :], xp_tiles[t]).then_inc(xres_in, 16)
            for n in range(44, 48):
                e.wait_ge(lo_ready, n - 3)
                e.wait_ge(unit_done, n - 3)
                e.dma_start(raw[:, n % RAW, :, :], wmix[n]).then_inc(raw_in[n % RAW], 16)
            for s in range(2, 4):
                e.dma_start(wslot[s][:], wmoe[s]).then_inc(slot_in[s], 16)
            e.wait_ge(unit_done, 48)
            e.wait_ge(lo_ready, 48)
            e.dma_start(g2[:], rows[2:3, :].broadcast_to([P, D])).then_inc(const_in, 16)
            e.dma_start(nf[:], rows[3:4, :].broadcast_to([P, D])).then_inc(const_in, 16)
            with e.Fori(0, PAIRS // 2 - 1) as i:
                for q in range(2):
                    e.wait_ge(pair_mm, i * 2 + (q + 1))
                    e.sem_inc(held, 1)
                    for s in (2 * q, 2 * q + 1):
                        e.dma_start(wslot[s][:], wmoe[bass.ds(i * 4 + (4 + s), 1)].rearrange("a p c -> (a p) c")).then_inc(slot_in[s], 16)
            e.wait_ge(passes_ready, 1)
            np_ = e.value_load(npi[0:1, 0:1], min_val=1, max_val=MAXPASS)
            with e.If(np_ > 1):
                with e.Fori(1, np_) as k:
                    with e.Fori(0, PAIRS // 2) as i:
                        for q in range(2):
                            e.wait_ge(pair_mm, k * PAIRS + i * 2 + (q - 1))
                            e.sem_inc(held, 1)
                            for s in (2 * q, 2 * q + 1):
                                e.dma_start(wslot[s][:], wmoe[bass.ds(i * 4 + s, 1)].rearrange("a p c -> (a p) c")).then_inc(slot_in[s], 16)
            e.wait_ge(v_stored, 32)
            e.wait_ge(done_out, 16 * (TILES + 1))

        @block.gpsimd
        def _(g):
            own = Steps(g, pool_s)
            g.memset(bdiag[:], 0.0).then_inc(masks, 1)
            own.then(g.memset(ident[:], 0.0))
            g.affine_select(out=ident[:], in_=ident[:], compare_op=ALU.not_equal, fill=1.0, base=0,
                            pattern=[[-1, P]], channel_multiplier=1).then_inc(masks, 1)
            own.then(g.memset(fold[:], 0.0))
            for q in range(4):
                i = g.affine_select(out=fold[:], in_=fold[:], compare_op=ALU.not_equal, fill=1.0,
                                    base=-S * q, pattern=[[-1, S]], channel_multiplier=1)
                if q < 3:
                    own.then(i)
            i.then_inc(masks, 1)
            g.memset(ones[:], 1.0).then_inc(masks, 1)
            own.then(g.memset(upper[:], 1.0))
            g.affine_select(out=upper[:], in_=upper[:], compare_op=ALU.is_gt, fill=0.0, base=0,
                            pattern=[[1, P]], channel_multiplier=-1).then_inc(masks, 1)
            g.wait_ge(const_in, NCONST - 32)
            g.affine_select(out=wsT[:], in_=wsT[:], compare_op=ALU.is_ge, fill=0.0, base=0,
                            pattern=[[0, HEADS], [1, P]], channel_multiplier=-1).then_inc(masks, 1)
            g.wait_ge(bd_in, 16 * DB)
            g.affine_select(out=bdiag[:], in_=bdiag[:], compare_op=ALU.is_ge, fill=0.0, base=0,
                            pattern=[[0, HEADS], [1, S]], channel_multiplier=-1).then_inc(masks, 1)
            for n in range(EG):
                g.memset(first[:, n:n + 1], float(EG - n))
            for n in range(NE):
                g.memset(ebase[:, n:n + 1], float(n * CAP))
            for n in range(MAXPASS):
                i = g.memset(thr[:, n:n + 1], float(n * CAP))
            i.then_inc(masks, 1)
            g.wait_ge(v_ready, 1 + TILES)
            g.dma_start(vp, v[:, NT - 1, :]).then_inc(v_stored, 16)
            g.dma_start(vs, v[0:S, NT, :]).then_inc(v_stored, 16)
            own.then(g.memset(zero[:], 0.0))
            for n in range(SLOTROWS // P):
                g.dma_start(xsort[n * P:(n + 1) * P, :].rearrange("p (a c) -> p a c", a=4),
                            zero[:].rearrange("p (a c) -> p a c", a=1).broadcast_to([P, 4, D // 4])).then_inc(zeroed, 16)
            with g.Fori(0, KT) as j:
                g.wait_ge(gates_mm, FIRST + j)
                g.dma_start(gw[:], wgate[bass.ds(j, 1)].rearrange("a p w c -> (a p) w c")).then_inc(gw_in, 16)
            g.wait_ge(zeroed, 16 * (SLOTROWS // P))
            g.wait_ge(passes_ready, 1)
            np_ = g.value_load(npi[0:1, 0:1], min_val=1, max_val=MAXPASS)
            with g.Fori(0, np_) as k:
                g.wait_ge(pidx_ready, k + 1)
                g.wait_ge(xn2_ready, TILES)
                g.wait_ge(xgT_mm, FIRST + k * PAIRS)
                g.sem_inc(held, 1)
                for s in range(2):
                    for t in range(TILES):
                        r = rowsof(t)
                        g.indirect_dma_start(
                            out=xsort, out_offset=bass.IndirectOffsetOnAxis(ap=pidx[0:r, s, t:t + 1], axis=0),
                            in_=xn2[0:r, t, :], in_offset=None,
                            bounds_check=SLOTROWS - 1, oob_is_err=False).then_inc(scattered, 16)
                g.wait_ge(scattered, (k + 1) * (16 * 2 * TILES))
                g.sem_inc(held, 1)
                with g.Fori(0, PAIRS // 2) as i:
                    for q in range(2):
                        g.wait_ge(xgT_mm, FIRST + k * PAIRS + i * 2)
                        g.dma_start(xg[:, q, :], xsort[bass.ds(i * (2 * P) + q * P, P), :]).then_inc(
                            xg_in[q], 16)
                for q in range(2):
                    g.wait_ge(y_out[q], FIRST + (k + 1) * (16 * (PAIRS // 2)))
                for s in range(2):
                    for t in range(TILES):
                        r = rowsof(t)
                        n = s * TILES + t
                        g.wait_ge(comb, FIRST + k * (2 * TILES) + max(n - 1, 0))
                        g.sem_inc(held, 1)
                        g.indirect_dma_start(
                            out=gy[0:r, n % 2, :], out_offset=None, in_=ysort,
                            in_offset=bass.IndirectOffsetOnAxis(ap=pidx[0:r, s, t:t + 1], axis=0),
                            bounds_check=SLOTROWS - 1, oob_is_err=False).then_inc(gathered[n % 2], 16)
                g.wait_ge(comb, FIRST + (k + 1) * (2 * TILES))

        @block.scalar
        def _(a):
            own = Steps(a, act_s)
            for first_one in (sproj_sb, xr_ev, u_ev, ga_ev, gates_ev, yo_sb, y_out[0], y_out[1]):
                a.sem_inc(first_one, FIRST)

            def split_hi(n, slot, hslot, count):
                a.wait_ge(raw_in[slot], count)
                if n is not None and n >= 2:
                    a.wait_ge(unit_done, n - 1)
                a.activation(wh[:, hslot, :], raw[:, slot, :, :].rearrange("p k c -> p (k c)"),
                             ACT.Copy).then_inc(hi_ready, 1)

            a.wait_ge(ss_ready, 1)
            for t in range(TILES):
                r = rowsof(t)
                a.wait_ge(x_in[t], 16)
                a.activation(junk[0:r, :], xt[0:r, t, :], ACT.Square, accum_out=ss[0:r, t:t + 1]).then_inc(sq_ready, 1)
                a.wait_ge(sq_ready, t + 1)
            a.wait_ge(ms_ready, 1)
            a.activation(rstd[:], ss[:], ACT.Sqrt).then_inc(sq_ready, 1)
            split_hi(0, 0, 0, 16)
            split_hi(1, 1, 1, 16)
            a.wait_ge(const_in, NCONST - 32)
            for k in range(KT):
                a.wait_ge(xT_ready, k + 1)
                a.activation(xh[:, k, :], ps[:, k % 4, :], ACT.Copy, scale=ch[:, k, C_G1:C_G1 + 1]).then_inc(xh_ready, 1)
            a.wait_ge(v_ready, 1)
            a.activation(t8[:, 1, :], t8[:, 0, :], ACT.Exp, scale=-1.0).then_inc(ex_out, 1)
            for half in range(2):
                banks, sbank, fbank = v_banks(half)
                for u in range(4):
                    n = half * 4 + u
                    a.wait_ge(unit_done, n + 1)
                    split_hi(n + 2, (n + 2) % RAW, n % 2, 16 * ((n + 2) // RAW + 1))
                a.activation(sp[:], ps[:, sbank, :], ACT.Copy).then_inc(vsum, 1)
                c = slice(half * 512, half * 512 + 512)
                for t in range(NT):
                    a.activation(v[:, t, c], ps[:, banks[t], :], ACT.Gelu_apprx_tanh).then_inc(v_gelu, 1)
                a.wait_ge(vfold, half + 1)
                a.activation(v[0:S, NT, c], ps[0:S, fbank, :], ACT.Gelu_apprx_tanh).then_inc(v_gelu, 1)
            a.wait_ge(ms_ready, 2)
            a.activation(rstd[:], ss[:], ACT.Sqrt).then_inc(sq_ready, 1)

            a.wait_ge(z_ready, 2 * KT)
            a.wait_ge(v_stored, 32)
            with a.Fori(0, KT) as j:
                smp = lambda t: t[:, SEQ:TA]
                def raw_count(extra):
                    return j * 16 + 16 * (2 + extra + 1)
                a.wait_ge(sproj, j + 1)
                a.wait_ge(sproj_T, FIRST + j)
                a.activation(sp[:], ps[:, 6, :], ACT.Copy).then_inc(sproj_sb, 1)
                a.wait_ge(unit_done, j * 4 + 9)
                split_hi(None, 2, 0, raw_count(0))
                a.wait_ge(conv_done, FIRST + j)
                a.activation(XR[:, 3:3 + SEQ], ps[:, 0, :], ACT.Copy).then_inc(xr_ev, 1)
                a.wait_ge(sproj_T, FIRST + j + 1)
                a.activation(sq[:].rearrange("p u s -> p (u s)"), ps[:, 7, 0:4 * S], ACT.Copy).then_inc(sq_sb, 1)
                a.wait_ge(sq_sb, j + 1)
                a.activation(XR[:, 3 + SEQ:XRW].rearrange("p (b s) -> p b s", b=DB)[:, :, 3:7],
                             sq[:, 0, :].rearrange("p (b s) -> p b s", b=DB), ACT.Copy).then_inc(xr_ev, 1)
                a.wait_ge(unit_done, j * 4 + 10)
                split_hi(None, 3, 1, raw_count(0))
                a.wait_ge(ya_done, FIRST + j)
                a.activation(U[:, 0:SEQ], ps[:, 1, :], ACT.Copy).then_inc(u_ev, 1)
                a.activation(smp(U), sq[:, 1, :], ACT.Copy).then_inc(u_ev, 1)
                a.wait_ge(u_ev, FIRST + j * 2 + 2)
                a.activation(U1[:], U[:], ACT.Square).then_inc(u_sq, 1)
                a.wait_ge(unit_done, j * 4 + 11)
                split_hi(None, 0, 0, raw_count(1))
                a.wait_ge(merged, FIRST + j)
                a.activation(GA[:, 0:SEQ], ps[:, 2, :], ACT.Tanh, scale=0.5).then_inc(ga_ev, 1)
                a.activation(smp(GA), sq[:, 2, :], ACT.Tanh, scale=0.5).then_inc(ga_ev, 1)
                a.wait_ge(u_poly, j + 1)
                a.activation(U1[:], U1[:], ACT.Tanh, scale=GELU_K).then_inc(u_tanh, 1)
                a.wait_ge(gates_mm, FIRST + j + 1)
                for w, T in ((0, TR), (1, TI)):
                    b = hb[:, bass.ds(j, 1), w]
                    a.activation(T[:, 0:SEQ], ps[:, 4 + w, :], ACT.Tanh, scale=0.5, bias=b).then_inc(gates_ev, 1)
                    a.activation(smp(T), ps[:, 7, (4 + w) * S:(5 + w) * S], ACT.Tanh, scale=0.5, bias=b).then_inc(gates_ev, 1)
                cp, cn = csp[:, bass.ds(j, 1), 0], csp[:, bass.ds(j, 1), 1]
                a.wait_ge(gates_ev, FIRST + j * 4 + 4)
                a.activation(A[:], TR[:], ACT.Exp, scale=cp, bias=cp).then_inc(a_ready, 1)
                a.activation(TR[:], TR[:], ACT.Tanh, scale=cn, bias=cn).then_inc(a_ready, 1)
                a.wait_ge(a_ready, j * 3 + 1)
                a.activation(M[:], A[:], ACT.Square).then_inc(a_ready, 1)
                a.wait_ge(unit_done, j * 4 + 12)
                split_hi(None, 1, 1, raw_count(1))
                a.activation(ps[:, 3, :], ps[:, 3, :], ACT.Tanh, scale=0.5).then_inc(gb_ev, 1)
                a.activation(gbs[:], sq[:, 3, :], ACT.Tanh, scale=0.5).then_inc(gb_ev, 1)
                a.wait_ge(m_poly, j + 1)
                a.activation(M[:], M[:], ACT.Sqrt).then_inc(m_sqrt, 1)

            for half in range(2):
                banks, sbank, fbank = v_banks(half)
                for u in range(4):
                    n = UNITS_V + UNITS_J + half * 4 + u
                    a.wait_ge(unit_done, n + 1)
                    if n + 2 < 48:
                        split_hi(n + 2, (n + 2) % RAW, n % 2, 16 * ((n + 2) // RAW + 1))
                if half:
                    a.wait_ge(vfold, 3)
                a.activation(sp[:], ps[:, sbank, :], ACT.Copy).then_inc(vsum, 1)
            for t in range(TILES):
                r = rowsof(t)
                a.wait_ge(x1_ready, TILES + t + 1)
                a.wait_ge(n2_sq, t)
                a.activation(junk2[0:r, :], x1[0:r, t, :], ACT.Square, accum_out=ss[0:r, t:t + 1]).then_inc(n2_sq, 1)
            a.wait_ge(n2_ms, 1)
            a.activation(rstd[:], ss[:], ACT.Sqrt).then_inc(n2_sq, 1)
            for k in range(0, KT, 2):
                a.wait_ge(xn2T_mm, k + 1)
                a.activation(xn2T[:, k, 0:SEQ], ps[:, k % 4, :], ACT.Copy).then_inc(xn2T_sb[0], 1)
            a.wait_ge(ex_in, 1)
            a.activation(r4[:], r4[:], ACT.Exp).then_inc(ex_out, 1)
            a.wait_ge(ex_in, 2)
            a.activation(r1[:, 3, :], r1[:, 2, :], ACT.Exp).then_inc(ex_out, 1)
            a.wait_ge(passes_ready, 1)
            np_ = a.value_load(npi[0:1, 0:1], min_val=1, max_val=MAXPASS)
            with a.Fori(0, np_) as k:
                with a.Fori(0, PAIRS // 2) as i:
                    for q in range(2):
                        G = k * PAIRS + i * 2 + q
                        a.wait_ge(gu_mm, G + 1)
                        a.activation(hs[:, q, :], ps[:, 2, 0:FE], ACT.Silu).then_inc(silu_done, 1)
                        a.wait_ge(pair_mm, G + 1)
                        a.wait_ge(y_out[q], FIRST + (k * (PAIRS // 2) + i) * 16)
                        a.activation(yo[:, q, :], ps[:, 6:8, :].rearrange("p b c -> p (b c)"), ACT.Copy).then_inc(yo_sb, 1)
                        a.wait_ge(yo_sb, FIRST + G + 1)
                        a.dma_start(ysort[bass.ds(i * (2 * P) + q * P, P), :], yo[:, q, :]).then_inc(y_out[q], 16)
            for t in range(TILES):
                r = rowsof(t)
                a.wait_ge(comb, FIRST + np_ * (2 * TILES))
                a.wait_ge(n2_sq, TILES + 1 + t)
                a.activation(junk2[0:r, :], x1[0:r, t, :], ACT.Square, accum_out=ss[0:r, t:t + 1]).then_inc(n2_sq, 1)
            a.wait_ge(fin_ms, 1)
            a.activation(rstd[:], ss[:], ACT.Sqrt).then_inc(fin_sq, 1)
            for t in range(TILES):
                r = rowsof(t)
                a.wait_ge(fin_ready, t + 1)
                a.dma_start(y_tiles[t], xn2[0:r, t, :]).then_inc(done_out, 16)
            a.wait_ge(so_ready, 1)
            a.dma_start(st, so[:]).then_inc(done_out, 16)

        @block.vector
        def _(d):
            own = Steps(d, dve_s)
            for first_one in (conv_done, ya_done, merged, comb, xgT_sb, hm_ready, hT_sb):
                d.sem_inc(first_one, FIRST)

            def split_lo(hslot, slot, count):
                d.wait_ge(hi_ready, count)
                d.tensor_tensor(wl[:, hslot, :], raw[:, slot, :, :].rearrange("p k c -> p (k c)"),
                                wh[:, hslot, :].bitcast(F32), ALU.subtract).then_inc(lo_ready, 1)

            def rsqrt_steps(wait_sum, sig_ms, sig_val, wait_sq, scale):
                wait_sum()
                d.tensor_scalar(ss[:], ss[:], scale, EPS, ALU.mult, ALU.add).then_inc(sig_ms, 1)
                wait_sq()
                own.then(d.reciprocal(rstd[:], rstd[:]))

            d.memset(ss[:], float(D)).then_inc(ss_ready, 1)
            rsqrt_steps(lambda: d.wait_ge(sq_ready, TILES), ms_ready, 1,
                        lambda: d.wait_ge(sq_ready, TILES + 1), 1.0 / D)
            for t in range(TILES):
                r = rowsof(t)
                d.tensor_scalar(xt[0:r, t, :], xt[0:r, t, :], rstd[0:r, t:t + 1], None, ALU.mult).then_inc(xn_ready, 1)
            split_lo(0, 0, 1)
            split_lo(1, 1, 2)
            d.wait_ge(const_in, NCONST - 32)
            for k in range(KT):
                d.wait_ge(xh_ready, k + 1)
                d.scalar_tensor_tensor(out=xl[:, k, :], in0=ps[:, k % 4, :], scalar=ch[:, k, C_G1:C_G1 + 1],
                                       in1=xh[:, k, :].bitcast(F32), op0=ALU.mult, op1=ALU.subtract).then_inc(xl_ready, 1)
            d.wait_ge(xT_ready, KT + 1)
            d.tensor_tensor(xs[:], ps[:, 4, 0:KT * S].rearrange("p (k s) -> p k s", k=KT),
                            ch[:, :, C_G1:C_G1 + 1].broadcast_to([P, KT, S]), ALU.mult).then_inc(xs_ready, 1)
            own.then(d.tensor_scalar(hb[:], ch[:, :, C_BA:C_BA + 2], 0.5, None, ALU.mult))
            own.then(d.tensor_scalar(bsh[:], bsh[:], 0.5, None, ALU.mult))
            lam = ch[:, :, C_LAM]
            d.scalar_tensor_tensor(out=t8[:, 0, :], in0=lam, scalar=-1.0, in1=lam, op0=ALU.mult, op1=ALU.max).then_inc(v_ready, 1)
            d.wait_ge(ex_out, 1)
            own.then(d.tensor_scalar(t8[:, 2, :], t8[:, 1, :], 2.0, None, ALU.add))
            own.then(d.reciprocal(t8[:, 2, :], t8[:, 2, :]))
            own.then(d.tensor_tensor(t8[:, 1, :], t8[:, 1, :], t8[:, 2, :], ALU.mult))
            own.then(d.tensor_tensor(t8[:, 2, :], t8[:, 1, :], t8[:, 1, :], ALU.mult))
            own.then(d.tensor_scalar(t8[:, 3, :], t8[:, 2, :], 1.0 / 17, 1.0 / 15, ALU.mult, ALU.add))
            for n in (13, 11, 9, 7, 5, 3, 1):
                own.then(d.tensor_tensor(t8[:, 3, :], t8[:, 3, :], t8[:, 2, :], ALU.mult))
                own.then(d.tensor_scalar(t8[:, 3, :], t8[:, 3, :], 1.0 / n, None, ALU.add))
            own.then(d.tensor_tensor(t8[:, 3, :], t8[:, 3, :], t8[:, 1, :], ALU.mult))
            own.then(d.tensor_scalar(t8[:, 4, :], lam, -1.0, 0.0, ALU.mult, ALU.max))
            own.then(d.scalar_tensor_tensor(out=t8[:, 3, :], in0=t8[:, 3, :], scalar=2.0, in1=t8[:, 4, :],
                                            op0=ALU.mult, op1=ALU.add))
            own.then(d.tensor_scalar(csp[:, :, 0], t8[:, 3, :], -4.0, None, ALU.mult))
            own.then(d.tensor_scalar(csp[:, :, 1], t8[:, 3, :], 4.0, None, ALU.mult))
            for n in range(UNITS_V):
                split_lo(n % 2, (n + 2) % RAW, n + 3)
            own.then(d.memset(bnag[:], 1.0))
            for t in range(TILES):
                r = rowsof(t)
                d.wait_ge(v_gelu, TILES + t + 1)
                for h in range(2):
                    own.then(d.bn_stats(bnst[0:r, h, :], v[0:r, t, h * 512:(h + 1) * 512]))
                own.then(d.bn_aggr(bnag[0:r, t, :], bnst[0:r, :, :]))
            d.tensor_scalar(ss[:], bnag[:, :, 1], EPS, None, ALU.add).then_inc(ms_ready, 1)
            d.wait_ge(sq_ready, TILES + 2)
            own.then(d.reciprocal(rstd[:], rstd[:]))
            d.wait_ge(const_in, NCONST - 32)
            for t in range(TILES):
                r = rowsof(t)
                vt = v[0:r, t, :]
                own.then(d.tensor_scalar(vt, vt, bnag[0:r, t, 0:1], rstd[0:r, t:t + 1], ALU.subtract, ALU.mult))
                own.then(d.tensor_tensor(vt, vt, lng[0:r, :], ALU.mult))
                d.tensor_tensor(vt, vt, lnb[0:r, :], ALU.add).then_inc(v_ready, 1)
            for j in range(KT):
                h = j // 2
                d.wait_ge(z_mm, j + 1)
                d.scalar_tensor_tensor(
                    out=zT[:, j, 0:SEQ].rearrange("p (c t) -> p c t", c=NT),
                    in0=ps[:, j % 4, :].rearrange("p (c t) -> p c t", c=NT), scalar=0.5,
                    in1=bsh[:, h:h + 1, :].broadcast_to([P, NT, P]), op0=ALU.mult, op1=ALU.add).then_inc(z_ready, 1)
            for j in range(KT):
                h = j // 2
                d.wait_ge(z_mm, KT + 1)
                d.scalar_tensor_tensor(
                    out=zT[:, j, SEQ:TA].rearrange("p (b s) -> p b s", b=DB),
                    in0=ps[:, 5, j * S:(j + 1) * S].rearrange("p (b s) -> p b s", b=DB), scalar=0.5,
                    in1=bsh[:, h:h + 1, 0:DS].broadcast_to([P, DB, DS]), op0=ALU.mult, op1=ALU.add).then_inc(z_ready, 1)
            d.wait_ge(v_stored, 32)
            own.then(d.memset(XR[:, 0:3], 0.0))
            xrs = XR[:, 3 + SEQ:XRW].rearrange("p (b s) -> p b s", b=DB)
            smp = lambda t: t[:, SEQ:TA].rearrange("p (b s) -> p b s", b=DB)
            with d.Fori(0, KT) as j:
                own.enter(j, 25)
                col = lambda c, n=1: ch[:, bass.ds(j, 1), c:c + n].rearrange("p a c -> p (a c)")
                n0 = UNITS_V
                split_lo(0, 2, j * 4 + (n0 + 3))
                d.wait_ge(gates_mm, FIRST + j)
                own.then(d.tensor_copy(xrs[:, :, 0:3], col(C_ST, 24).rearrange("p (b s) -> p b s", b=DB)))
                d.wait_ge(xr_ev, FIRST + j * 2 + 2)
                own.then(d.tensor_scalar(XC[:, 0:SEQ], XR[:, 3:3 + SEQ], col(C_W0 + 3), col(C_CB), ALU.mult, ALU.add))
                own.then(d.tensor_scalar(smp(XC), xrs[:, :, 3:7], col(C_W0 + 3), col(C_CB), ALU.mult, ALU.add))
                for t in range(3):
                    own.then(d.scalar_tensor_tensor(out=XC[:, 0:SEQ], in0=XR[:, t:t + SEQ], scalar=col(C_W0 + t),
                                                    in1=XC[:, 0:SEQ], op0=ALU.mult, op1=ALU.add))
                    i = d.scalar_tensor_tensor(out=smp(XC), in0=xrs[:, :, t:t + 4], scalar=col(C_W0 + t),
                                               in1=smp(XC), op0=ALU.mult, op1=ALU.add)
                    if t < 2:
                        own.then(i)
                own.then(i)
                sj = so[:, bass.ds(j, 1), :].rearrange("p a c -> p (a c)")
                d.tensor_copy(sj[:, 9:12], XR[:, SEQ:SEQ + 3])
                d.tensor_copy(sj[:, 12:36].rearrange("p (b s) -> p b s", b=DB), xrs[:, :, 4:7]).then_inc(conv_done, 1)
                split_lo(1, 3, j * 4 + (n0 + 4))
                d.wait_ge(u_sq, j + 1)
                own.then(d.tensor_scalar(U1[:], U1[:], GELU_C, 1.0, ALU.mult, ALU.add))
                d.tensor_tensor(U1[:], U1[:], U[:], ALU.mult).then_inc(u_poly, 1)
                split_lo(0, 0, j * 4 + (n0 + 5))
                d.wait_ge(u_tanh, j + 1)
                own.then(d.scalar_tensor_tensor(out=U1[:], in0=U1[:], scalar=1.0, in1=U[:], op0=ALU.add, op1=ALU.mult))
                d.tensor_tensor(U1[:], U1[:], zT[:, bass.ds(j, 1), :].rearrange("p a t -> p (a t)"), ALU.mult).then_inc(u_free, 1)
                d.wait_ge(u_free, j + 1)
                d.wait_ge(ga_ev, FIRST + j * 2 + 2)
                d.scalar_tensor_tensor(out=GA[:], in0=GA[:], scalar=1.0, in1=U1[:], op0=ALU.add, op1=ALU.mult).then_inc(ya_done, 1)
                d.wait_ge(a_ready, j * 3 + 3)
                d.scalar_tensor_tensor(out=M[:], in0=M[:], scalar=1.0, in1=TR[:], op0=ALU.add, op1=ALU.mult).then_inc(m_poly, 1)
                own.then(d.scalar_tensor_tensor(out=TI[:], in0=TI[:], scalar=1.0, in1=XC[:], op0=ALU.add, op1=ALU.mult))
                split_lo(1, 1, j * 4 + (n0 + 6))
                d.wait_ge(m_sqrt, j + 1)
                own.then(d.memset(M[:, 0:1], 1.0))
                own.then(d.scalar_tensor_tensor(out=TI[:], in0=TI[:], scalar=0.5, in1=M[:], op0=ALU.mult, op1=ALU.mult))
                own.then(d.tensor_tensor(TR[:, 0:DB], smp(A)[:, :, 0], col(C_H0, DB), ALU.mult))
                own.then(d.tensor_tensor(smp(TI)[:, :, 0], smp(TI)[:, :, 0], TR[:, 0:DB], ALU.add))
                own.then(d.memset(smp(A)[:, :, 0], 0.0))
                own.then(d.tensor_tensor_scan(XC[:], A[:], TI[:], 0.0, ALU.mult, ALU.add))
                own.then(d.tensor_copy(sj[:, 0:1], XC[:, SEQ - 1:SEQ]))
                own.then(d.tensor_copy(sj[:, 1:9], smp(XC)[:, :, DS - 1]))
                d.wait_ge(gb_ev, j * 2 + 2)
                own.then(d.scalar_tensor_tensor(out=M[:, 0:SEQ], in0=ps[:, 3, :], scalar=1.0, in1=XC[:, 0:SEQ],
                                                op0=ALU.add, op1=ALU.mult))
                own.then(d.scalar_tensor_tensor(out=M[:, SEQ:TA], in0=gbs[:], scalar=1.0, in1=XC[:, SEQ:TA],
                                                op0=ALU.add, op1=ALU.mult))
                own.then(d.tensor_tensor(M[:], M[:], GA[:], ALU.add))
                own.then(d.tensor_copy(mh[:, bass.ds(j, 1), :].rearrange("p a t -> p (a t)"), M[:, 0:SEQ]))
                own.then(d.tensor_copy(ms[:, bass.ds(j, 1), :].rearrange("p a t -> p (a t)"), M[:, SEQ:TA]))
                d.tensor_tensor(ml[:, bass.ds(j, 1), :].rearrange("p a t -> p (a t)"), M[:, 0:SEQ],
                                mh[:, bass.ds(j, 1), :].rearrange("p a t -> p (a t)").bitcast(F32),
                                ALU.subtract).then_inc(merged, 1)
                own.leave(KT)
            d.memset(pf[:], 0.0).then_inc(so_ready, 1)
            for half in range(2):
                banks, sbank, fbank = v_banks(half)
                c = slice(half * 512, half * 512 + 512)
                for u in range(4):
                    n = UNITS_V + UNITS_J + half * 4 + u
                    if n + 2 < 48:
                        split_lo(n % 2, (n + 2) % RAW, n + 3)
                d.wait_ge(unit_done, 44 + 4 * half)
                d.wait_ge(xres_in, 16 * TILES)
                for t in range(NT):
                    d.scalar_tensor_tensor(out=x1[:, t, c], in0=ps[:, banks[t], :], scalar=0.5, in1=x1[:, t, c],
                                           op0=ALU.mult, op1=ALU.add).then_inc(x1_ready, 1)
                d.wait_ge(vfold, 3 + half)
                d.scalar_tensor_tensor(out=x1[0:S, NT, c], in0=ps[0:S, fbank, :], scalar=0.5, in1=x1[0:S, NT, c],
                                       op0=ALU.mult, op1=ALU.add).then_inc(x1_ready, 1)
            rsqrt_steps(lambda: d.wait_ge(n2_sq, TILES), n2_ms, 1, lambda: d.wait_ge(n2_sq, TILES + 1), 1.0 / D)
            d.wait_ge(const_in, NCONST)
            for t in range(TILES):
                r = rowsof(t)
                d.scalar_tensor_tensor(out=xn2[0:r, t, :], in0=x1[0:r, t, :], scalar=rstd[0:r, t:t + 1], in1=g2[0:r, :],
                                       op0=ALU.mult, op1=ALU.mult).then_inc(xn2_ready, 1)
            for k in range(1, KT, 2):
                d.wait_ge(xn2T_mm, k + 1)
                d.tensor_copy(xn2T[:, k, 0:SEQ], ps[:, k % 4, :]).then_inc(xn2T_sb[1], 1)
            d.wait_ge(xn2T_mm, KT + 1)
            d.tensor_copy(xn2T[:, :, SEQ:TA], ps[:, 4, 0:KT * S].rearrange("p (k s) -> p k s", k=KT)).then_inc(xn2T_sb[1], 1)
            d.wait_ge(lg_mm, 1)
            d.tensor_scalar(lgT[:, 0:SEQ], ps[0:NL, 5, :], brt[:], None, ALU.add).then_inc(lg_sb, 1)
            d.tensor_scalar(lgT[:, SEQ:TA], ps[0:NL, 6, 0:S], brt[:], None, ALU.add).then_inc(lg_sb, 1)
            own.then(d.memset(lg[:], 0.0))
            d.wait_ge(lgt_mm, 1)
            for t in range(TILES):
                r = rowsof(t)
                own.then(d.tensor_copy(lg[0:r, t, :], ps[0:r, 7, t * NL:(t + 1) * NL]))

            def bc(t, n):
                return t.rearrange("p (t a) -> p t a", a=1).broadcast_to([P, TILES, n])

            def row(t, n):
                return t.rearrange("p (a n) -> p a n", a=1).broadcast_to([P, TILES, n])

            def first_max(out, keys, maxv, tmp, n, mv):
                own.then(d.reduce_max(maxv, keys, axis=AX))
                own.then(d.tensor_tensor(tmp, keys, bc(maxv, n), ALU.is_ge))
                own.then(d.tensor_tensor(tmp, tmp, row(first[:, 0:n], n), ALU.mult))
                own.then(d.reduce_max(mv, tmp, axis=AX))
                own.then(d.tensor_tensor(out, tmp, bc(mv, n), ALU.is_equal))

            d.wait_ge(masks, 8)
            first_max(oh[:], lg[:, :, 0:NG], r1[:, 0, :], r4[:], NG, r1[:, 1, :])
            d.tensor_tensor(r4[:], lg[:, :, 0:NG], bc(r1[:, 0, :], NG), ALU.subtract).then_inc(ex_in, 1)
            d.wait_ge(ex_out, 2)
            own.then(d.reduce_sum(r1[:, 1, :], r4[:], axis=AX))
            own.then(d.reciprocal(r1[:, 5, :], r1[:, 1, :]))
            b4 = big[:].rearrange("p t (g e) -> p t g e", g=NG)
            ohb = oh[:].rearrange("p t (g a) -> p t g a", a=1).broadcast_to([P, TILES, NG, EG])
            for t in range(TILES):
                own.then(d.tensor_tensor(b4[:, t], lg[:, t, NG:NL].rearrange("p (g e) -> p g e", g=NG), ohb[:, t], ALU.mult))
            for t in range(TILES):
                own.then(d.reduce_sum(ein[:, t, :], b4[:, t].rearrange("p g e -> p e g"), axis=AX))
            first_max(o8[:, 0], ein[:], r1[:, 0, :], e8[:], EG, r1[:, 1, :])
            own.then(d.scalar_tensor_tensor(out=ein[:], in0=o8[:, 0], scalar=-1e30, in1=ein[:], op0=ALU.mult, op1=ALU.add))
            first_max(o8[:, 1], ein[:], r1[:, 4, :], e8[:], EG, r1[:, 1, :])
            d.tensor_tensor(r1[:, 2, :], r1[:, 4, :], r1[:, 0, :], ALU.subtract).then_inc(ex_in, 1)
            d.wait_ge(ex_out, 3)
            own.then(d.tensor_scalar(r1[:, 6, :], r1[:, 3, :], 1.0, None, ALU.add))
            own.then(d.reciprocal(r1[:, 6, :], r1[:, 6, :]))
            own.then(d.tensor_tensor(gate[:, 0, :], r1[:, 6, :], r1[:, 5, :], ALU.mult))
            own.then(d.tensor_tensor(gate[:, 1, :], gate[:, 0, :], r1[:, 3, :], ALU.mult))
            for s in range(2):
                for t in range(TILES):
                    own.then(d.tensor_tensor(
                        ohe[:, s, t].rearrange("p (g e) -> p g e", g=NG), ohb[:, t],
                        o8[:, s, t:t + 1, :].broadcast_to([P, NG, EG]), ALU.mult))
            d.tensor_tensor(mcnt[:], ohe[:, 0], ohe[:, 1], ALU.add).then_inc(cnt_in, 1)
            d.wait_ge(rank_mm, 1)
            own.then(d.memset(rank[:], 0.0))
            for t in range(TILES):
                r = rowsof(t)
                own.then(d.tensor_copy(rank[0:r, t, :], ps[0:r, 0, t * NE:(t + 1) * NE]))
            own.then(d.reduce_max(npf[:, 0:1], ps[:, 0, TILES * NE:(TILES + 1) * NE], axis=AX))
            own.then(d.tensor_scalar(big[:, 0, 0:MAXPASS], thr[:], npf[:, 0:1], None, ALU.is_lt))
            own.then(d.reduce_sum(npf[:, 1:2], big[:, 0, 0:MAXPASS], axis=AX))
            d.tensor_copy(npi[0:1, 0:1], npf[0:1, 1:2]).then_inc(passes_ready, 1)
            for s in range(2):
                own.then(d.tensor_tensor(big[:], ohe[:, s], rank[:], ALU.mult))
                own.then(d.reduce_sum(rk[:, s, :], big[:], axis=AX))
                own.then(d.tensor_tensor(big[:], ohe[:, s], row(ebase[:], NE), ALU.mult))
                own.then(d.reduce_sum(bp[:, s, :], big[:], axis=AX))
            own.then(d.memset(gy[:], 0.0))
            d.wait_ge(passes_ready, 1)
            np_ = d.value_load(npi[0:1, 0:1], min_val=1, max_val=MAXPASS)
            with d.Fori(0, np_) as k:
                own.enter(k, 7)
                d.wait_ge(comb, FIRST + k * (2 * TILES))
                own.then(d.tensor_scalar(gk[:], rk[:], 0.0, None, ALU.is_ge))
                own.then(d.tensor_scalar(pk[:], rk[:], float(CAP), None, ALU.is_lt))
                own.then(d.tensor_tensor(pk[:], pk[:], gk[:], ALU.mult))
                own.then(d.tensor_tensor(gk[:], pk[:], gate[:], ALU.mult))
                own.then(d.scalar_tensor_tensor(out=pf[:], in0=rk[:], scalar=-OUT_OF_RANGE, in1=bp[:], op0=ALU.add, op1=ALU.add))
                own.then(d.tensor_tensor(pf[:], pf[:], pk[:], ALU.mult))
                d.tensor_scalar(pidx[:], pf[:], OUT_OF_RANGE, None, ALU.add).then_inc(pidx_ready, 1)
                own.then(d.tensor_scalar(rk[:], rk[:], float(-CAP), None, ALU.add))
                d.sem_inc(held, 1)
                with d.Fori(0, PAIRS // 2) as i:
                    for q in range(2):
                        G = k * PAIRS + i * 2 + q
                        d.wait_ge(xgT_mm, FIRST + G + 1)
                        d.tensor_copy(xgT[:, q, :, :].rearrange("p k c -> p (k c)"),
                                      ps[:, 0:2, :].rearrange("p b c -> p (b c)")).then_inc(xgT_sb, 1)
                        d.wait_ge(silu_done, G + 1)
                        d.tensor_tensor(hm[:, q, :], hs[:, q, :], ps[:, 2, FE:2 * FE], ALU.mult).then_inc(hm_ready, 1)
                        d.wait_ge(hT_mm, G + 1)
                        d.tensor_copy(hT[:, q, :, :].rearrange("p f c -> p (f c)"), ps[:, 3, 0:2 * P]).then_inc(hT_sb, 1)
                for s in range(2):
                    for t in range(TILES):
                        r = rowsof(t)
                        n = s * TILES + t
                        d.wait_ge(gathered[n % 2], k * (16 * TILES) + 16 * (n // 2 + 1))
                        if s:
                            d.wait_ge(comb, FIRST + k * (2 * TILES) + t + 1)
                        d.scalar_tensor_tensor(out=x1[0:r, t, :], in0=gy[0:r, n % 2, :], scalar=gk[0:r, s, t:t + 1],
                                               in1=x1[0:r, t, :], op0=ALU.mult, op1=ALU.add).then_inc(comb, 1)
                own.leave(np_)
            rsqrt_steps(lambda: d.wait_ge(n2_sq, 2 * TILES + 1), fin_ms, 1, lambda: d.wait_ge(fin_sq, 1), 1.0 / D)
            for t in range(TILES):
                r = rowsof(t)
                d.scalar_tensor_tensor(out=xn2[0:r, t, :], in0=x1[0:r, t, :], scalar=rstd[0:r, t:t + 1], in1=nf[0:r, :],
                                       op0=ALU.mult, op1=ALU.mult).then_inc(fin_ready, 1)

        @block.tensor
        def _(pe):
            for first_one in (sproj_T, gates_mm, xgT_mm):
                pe.sem_inc(first_one, FIRST)
            def product(out, sh, sl, mh_, ml_, start, stop):
                pe.matmul(out, sh, mh_, start=start, stop=False)
                pe.matmul(out, sl, mh_, start=False, stop=False)
                return pe.matmul(out, sh, ml_, start=False, stop=stop)

            def token_rows(base, half, sth, stl, sts):
                banks, sbank, fbank = v_banks(half)
                for u in range(4):
                    n = base + half * 4 + u
                    slot = n % RAW
                    pe.wait_ge(hi_ready, n + 1)
                    pe.wait_ge(lo_ready, n + 1)
                    wr_ = raw[:, slot, :, :].rearrange("p k c -> p (k c)")
                    for t in range(NT):
                        for kk in range(2):
                            k = 2 * u + kk
                            c = slice(kk * 512, kk * 512 + 512)
                            tok = slice(t * P, t * P + P)
                            product(ps[:, banks[t], :], sth[:, k, tok], stl[:, k, tok], wh[:, n % 2, c], wl[:, n % 2, c],
                                    k == 0, k == KT - 1)
                    for kk in range(2):
                        k = 2 * u + kk
                        q = k % 4
                        last = pe.matmul(ps[S * q:S * q + S, sbank, :], sts[:, k, :], wr_[:, kk * 512:kk * 512 + 512],
                                         start=k < 4, stop=k >= 4, tile_position=(0, S * q), skip_group_check=True)
                    last.then_inc(unit_done, 1)

            def fold_rows(half, count):
                pe.wait_ge(vsum, count)
                pe.matmul(ps[0:S, v_banks(half)[2], :], fold[:], sp[:], start=True, stop=True).then_inc(vfold, 1)

            pe.wait_ge(masks, 2)
            pe.wait_ge(xn_ready, TILES)
            for k in range(KT):
                if k >= 4:
                    pe.wait_ge(xl_ready, k - 3)
                for t in range(NT):
                    i = pe.transpose(ps[:, k % 4, t * P:(t + 1) * P], xt[:, t, k * P:(k + 1) * P], ident[:])
                i.then_inc(xT_ready, 1)
            for k in range(KT):
                i = pe.transpose(ps[:, 4, k * S:(k + 1) * S], xt[0:S, NT, k * P:(k + 1) * P], ident[0:S, 0:S])
            i.then_inc(xT_ready, 1)
            pe.wait_ge(xl_ready, KT)
            pe.wait_ge(xh_ready, KT)
            pe.wait_ge(xs_ready, 1)
            pe.wait_ge(masks, 3)
            token_rows(0, 0, xh, xl, xs)
            fold_rows(0, 1)
            pe.wait_ge(v_gelu, NT)
            pe.wait_ge(vsum, 1)
            token_rows(0, 1, xh, xl, xs)
            fold_rows(1, 2)
            pe.wait_ge(masks, 7)
            pe.wait_ge(v_gelu, 2 * TILES)
            pe.wait_ge(v_ready, 1 + TILES)
            for j in range(KT):
                if j >= 4:
                    pe.wait_ge(z_ready, j - 3)
                for c in range(NT):
                    i = pe.matmul(ps[:, j % 4, c * P:(c + 1) * P], v[:, c, j * P:(j + 1) * P], wsT[:, j // 2, :], start=True, stop=True)
                i.then_inc(z_mm, 1)
            for j in range(KT):
                i = pe.matmul(ps[:, 5, j * S:(j + 1) * S], v[0:S, NT, j * P:(j + 1) * P], bdiag[:, j // 2, :],
                              start=True, stop=True)
            i.then_inc(z_mm, 1)
            pe.wait_ge(z_ready, 2 * KT)
            with pe.Fori(0, KT) as j:
                for s in range(RAW):
                    pe.wait_ge(raw_in[s], j * 16 + 48)
                pe.wait_ge(sproj_sb, FIRST + j)
                for k in range(KT):
                    q = k % 4
                    i = pe.matmul(ps[S * q:S * q + S, 6, :].rearrange("p (u c) -> p u c", u=4), xs[:, k, :], raw[:, :, k, :],
                                  start=k < 4, stop=k >= 4, tile_position=(0, S * q), skip_group_check=True)
                i.then_inc(sproj, 1)
                for p, freed in enumerate((xr_ev, u_ev, ga_ev, None)):
                    pe.wait_ge(hi_ready, j * 4 + (UNITS_V + p + 1))
                    pe.wait_ge(lo_ready, j * 4 + (UNITS_V + p + 1))
                    if freed is not None:
                        pe.wait_ge(freed, FIRST + j * 2)
                    else:
                        pe.wait_ge(merged, FIRST + j)
                    for k in range(KT):
                        c = slice(k * P, k * P + P)
                        i = product(ps[:, p, :], wh[:, p % 2, c], wl[:, p % 2, c], xh[:, k, :], xl[:, k, :], k == 0, k == KT - 1)
                    i.then_inc(unit_done, 1)
                    if p == 0:
                        pe.wait_ge(sproj_sb, FIRST + j + 1)
                        pe.wait_ge(gates_ev, FIRST + j * 4)
                        for u in range(4):
                            i = pe.matmul(ps[:, 7, u * S:(u + 1) * S], sp[:, u * P:(u + 1) * P], fold[:], start=True, stop=True)
                        i.then_inc(sproj_T, 1)
                    if p == 2:
                        pe.wait_ge(conv_done, FIRST + j + 1)
                        pe.wait_ge(gw_in, j * 16 + 16)
                        pe.wait_ge(sq_sb, j + 1)
                        pe.wait_ge(gates_ev, FIRST + j * 4)
                        for w in range(2):
                            pe.matmul(ps[:, 4 + w, :], gw[:, w, :], XC[:, 0:SEQ], start=True, stop=True)
                            i = pe.matmul(ps[:, 7, (4 + w) * S:(5 + w) * S], gw[:, w, :], XC[:, SEQ:TA], start=True, stop=True)
                        i.then_inc(gates_mm, 1)
            pe.wait_ge(merged, FIRST + KT)
            pe.wait_ge(gates_ev, FIRST + 4 * KT)
            pe.wait_ge(sproj_sb, FIRST + KT)
            token_rows(UNITS_V + UNITS_J, 0, mh, ml, ms)
            fold_rows(0, 3)
            pe.wait_ge(x1_ready, NT)
            token_rows(UNITS_V + UNITS_J, 1, mh, ml, ms)
            pe.wait_ge(x1_ready, TILES)
            fold_rows(1, 4)
            pe.wait_ge(xn2_ready, TILES)
            for k in range(KT):
                if k >= 4:
                    pe.wait_ge(xn2T_sb[k % 2], (k - 4) // 2 + 1)
                for t in range(NT):
                    i = pe.transpose(ps[:, k % 4, t * P:(t + 1) * P], xn2[:, t, k * P:(k + 1) * P], ident[:])
                i.then_inc(xn2T_mm, 1)
            for k in range(KT):
                i = pe.transpose(ps[:, 4, k * S:(k + 1) * S], xn2[0:S, NT, k * P:(k + 1) * P], ident[0:S, 0:S])
            i.then_inc(xn2T_mm, 1)
            pe.wait_ge(xn2T_sb[0], KT // 2)
            pe.wait_ge(xn2T_sb[1], KT // 2 + 1)
            for k in range(KT):
                pe.matmul(ps[0:NL, 5, :], wrt[:, k, :], xn2T[:, k, 0:SEQ], start=k == 0, stop=k == KT - 1)
            for k in range(KT):
                i = pe.matmul(ps[0:NL, 6, 0:S], wrt[:, k, :], xn2T[:, k, SEQ:TA], start=k == 0, stop=k == KT - 1)
            i.then_inc(lg_mm, 1)
            pe.wait_ge(lg_sb, 2)
            for t in range(TILES):
                r = rowsof(t)
                i = pe.transpose(ps[0:r, 7, t * NL:(t + 1) * NL], lgT[:, t * P:t * P + r], ident[0:NL, 0:NL])
            i.then_inc(lgt_mm, 1)
            pe.wait_ge(cnt_in, 1)
            for t in range(TILES + 1):
                r = rowsof(t) if t < TILES else P
                out = ps[0:r, 0, t * NE:(t + 1) * NE]
                for b in range(min(t, NT) if t < TILES else TILES):
                    rb = rowsof(b)
                    i = pe.matmul(out, ones[0:rb, 0:r], mcnt[0:rb, b, :], start=b == 0, stop=t == TILES and b == NT)
                if t < TILES:
                    i = pe.matmul(out, upper[0:r, 0:r], mcnt[0:r, t, :], start=t == 0, stop=True)
            i.then_inc(rank_mm, 1)
            pe.wait_ge(passes_ready, 1)
            np_ = pe.value_load(npi[0:1, 0:1], min_val=1, max_val=MAXPASS)
            with pe.Fori(0, np_) as k:
                with pe.Fori(0, PAIRS // 2) as i:
                    for q in range(2):
                        G = k * PAIRS + i * 2 + q
                        pe.wait_ge(xg_in[q], (k * (PAIRS // 2) + i + 1) * 16)
                        pe.wait_ge(xgT_sb, FIRST + G)
                        for c in range(KT):
                            l = pe.transpose(ps[:, c // 4, (c % 4) * P:(c % 4 + 1) * P], xg[:, q, c * P:(c + 1) * P], ident[:])
                        l.then_inc(xgT_mm, 1)
                        pe.wait_ge(xgT_sb, FIRST + G + 1)
                        for s in range(2):
                            pe.wait_ge(slot_in[2 * q + s], (k * (PAIRS // 2) + i + 1) * 16)
                        pe.wait_ge(hm_ready, FIRST + G)
                        for c in range(KT):
                            for s in range(2):
                                l = pe.matmul(ps[CAP * s:CAP * s + CAP, 2, :], xgT[:, q, c, CAP * s:CAP * s + CAP],
                                              wslot[2 * q + s][:, c * 512:(c + 1) * 512], start=c == 0, stop=c == KT - 1,
                                              tile_position=(0, CAP * s), skip_group_check=True)
                        l.then_inc(gu_mm, 1)
                        pe.wait_ge(hm_ready, FIRST + G + 1)
                        pe.wait_ge(hT_sb, FIRST + G)
                        for f in range(2):
                            l = pe.transpose(ps[:, 3, f * P:(f + 1) * P], hm[:, q, f * P:(f + 1) * P], ident[:])
                        l.then_inc(hT_mm, 1)
                        pe.wait_ge(hT_sb, FIRST + G + 1)
                        pe.wait_ge(yo_sb, FIRST + G)
                        for f in range(2):
                            for h in range(2):
                                for s in range(2):
                                    o = KT * 512 + f * D + h * 512
                                    l = pe.matmul(ps[CAP * s:CAP * s + CAP, 6 + h, :], hT[:, q, f, CAP * s:CAP * s + CAP],
                                                  wslot[2 * q + s][:, o:o + 512], start=f == 0, stop=f == 1,
                                                  tile_position=(0, CAP * s), skip_group_check=True)
                        l.then_inc(pair_mm, 1)


_INS = ["x", "wmix", "wgate", "chan", "wst", "bs", "rows", "wr", "br", "wmoe"]
_OUTS = [("y", (TA, D)), ("vp", (P, D)), ("vs", (S, D)), ("st", (P, KT, OUTC))]


def lay_out(np, i):
    f = lambda n: np.asarray(i[n])
    cat = np.concatenate
    x = cat([f("x_prompt").reshape(SEQ, D), f("x_sample").reshape(S, D)])
    w_in = f("w_in")[0].reshape(KT, P, 5, D)

    def token_units(w):
        return w.reshape(4, 2, P, 2, 512).transpose(3, 0, 2, 1, 4).reshape(8, P, KT, P)

    order = [2, 0, 3, 4]
    jw = w_in[:, :, order, :].reshape(KT, P, 4, KT, P).transpose(3, 2, 1, 0, 4).reshape(UNITS_J, P, KT, P)
    wmix = cat([token_units(w_in[:, :, 1, :]), jw, token_units(f("w_out")[0].reshape(KT, P, D))])
    wgate = np.stack([f("w_rg_a")[0], f("w_rg_x")[0]], axis=2)
    per = lambda a: a.reshape(-1, KT, P).transpose(2, 1, 0)
    chan = cat([per(f("norm1")[0]), per(f("conv_w")[0]), per(f("conv_b")[0]), per(f("lru_lambda")[0]),
                per(f("b_rg_a")[0].reshape(-1)), per(f("b_rg_x")[0].reshape(-1)), per(f("state_lru_h")[0]),
                per(f("state_conv")[0].reshape(-1, D))], axis=2)
    wst = f("w_s")[0].transpose(2, 0, 1)
    bs = f("b_s")[0].reshape(1, HEADS * P)
    rows = np.stack([f("ln_g")[0], f("ln_b")[0], f("norm2")[0], f("norm_f")])
    wr = cat([f("w_route_group")[0], f("w_route_expert")[0]], axis=1).reshape(KT, P, NL).transpose(1, 0, 2)
    br = cat([f("b_route_group")[0], f("b_route_expert")[0]]).reshape(NL, 1)
    gu = cat([f("w_gate")[0], f("w_up")[0]], axis=2).reshape(NE, KT, P, 512).transpose(0, 2, 1, 3).reshape(NE, P, KT * 512)
    wd = f("w_down")[0].reshape(NE, 2, P, D).transpose(0, 2, 1, 3).reshape(NE, P, 2 * D)
    wmoe = cat([gu, wd], axis=2)
    return dict(x=x, wmix=wmix, wgate=wgate, chan=chan, wst=wst, bs=bs, rows=rows, wr=wr, br=br, wmoe=wmoe)


def kernel(**inputs):
    import numpy as _np
    import concourse.bacc as _bacc
    from concourse.bass_utils import run_bass_kernel_spmd as _run

    nc = _bacc.Bacc("TRN2", target_bir_lowering=False, num_devices=1)
    laid = lay_out(_np, inputs)
    arrays, args = {}, []
    for name in _INS:
        a = _np.ascontiguousarray(laid[name])
        arrays[f"in_{name}"] = a
        args.append(nc.dram_tensor(f"in_{name}", a.shape, mybir.dt.from_np(a.dtype), kind="ExternalInput").ap())
    for name, shape in _OUTS:
        args.append(nc.dram_tensor(f"out_{name}", shape, F32, kind="ExternalOutput").ap())
    build(nc, *args)
    r = _run(nc, [arrays], core_ids=[0])
    y, vp, vs, st = (_np.asarray(r.results[0][f"out_{n}"]) for n, _ in _OUTS)
    st = st.transpose(2, 1, 0).reshape(OUTC, D)
    return (y[:SEQ].reshape(1, SEQ, D), y[SEQ:].reshape(DB, DS, D),
            st[0].reshape(1, 1, D), st[9:12].reshape(1, 1, 3, D), vp.reshape(1, 1, P, D),
            st[1:9].reshape(1, DB, D), st[12:36].reshape(1, DB, 3, D), vs.reshape(1, DB, DS, D))
```

```python
from contextlib import ExitStack

import concourse.bass as bass
from concourse import mybir

P = 128
D = 1024
KT = D // P
SEQ = 512
NT = SEQ // P
DB, DS = 8, 4
S = DB * DS
TA = SEQ + S
TILES = NT + 1
HEADS = 4
TAPS = 4
NG, EG = 4, 8
NE = NG * EG
NL = NG + NE
FE = 256
CAP = 64
PAIRS = NE // 2
MAXCHUNK = -(-TA // CAP)
EXTRA = 2 * TA // CAP
COLS = PAIRS + EXTRA
EPS = 1e-6
UNITS_V, UNITS_J, UNITS_O = 8, 32, 8
RAW = 4
OUTC = 36
(C_G1, C_W0, C_CB, C_LAM, C_BA, C_BX, C_H0, C_ST, C_G2) = (0, 1, 5, 6, 7, 8, 9, 17, 41)
NCH = 42
OUT_OF_RANGE = 8192.0
MASKED = 1e30
FIRST = 1

F32 = mybir.dt.float32
F32R = mybir.dt.float32r
BF16 = mybir.dt.bfloat16
I32 = mybir.dt.int32
U32 = mybir.dt.uint32
ALU = mybir.AluOpType
ACT = mybir.ActivationFunctionType
AX = mybir.AxisListType.X

GELU_K = 0.7978845608028654
GELU_C = 0.044715


class Steps:

    def __init__(self, eng, sem):
        self.eng, self.sem, self.base, self.n = eng, sem, 0, 0

    def then(self, ins):
        self.n += 1
        ins.then_inc(self.sem, 1)
        self.eng.wait_ge(self.sem, self.base + self.n)

    def enter(self, i, per):
        self.start, self.per = self.base + self.n, per
        self.base, self.n = self.start + i * per, 0

    def leave(self, times):
        assert self.n == self.per, (self.n, self.per)
        self.base, self.n = self.start + times * self.per, 0


def build(nc, x, wmix, wgate, chan, wst, bs, rows, wr, br, wmoe, y, vp, vs, st):
    xnd = nc.dram_tensor("xnd", (TA, D), F32, kind="Internal").ap()
    ytok = nc.dram_tensor("ytok", (2 * TA, D), F32, kind="Internal").ap()

    def at(name, offset, shape, dt=F32):
        return nc.alloc_sbuf_tensor_at(name, shape, dt, offset=BASE + offset)

    K = 1024
    BASE = -(-nc.sbuf_base // 64) * 64
    EW = 6144
    wslot = [at(f"wslot{s}", s * 24 * K, [P, EW]) for s in range(4)]
    xh = at("xh", 48 * K, [P, KT, SEQ], F32R)
    xl = at("xl", 64 * K, [P, KT, SEQ], F32R)
    zT = at("zT", 80 * K, [P, KT, TA])
    R_V = 97 * K
    v = at("v", R_V, [P, TILES, D])
    x1 = at("x1", R_V, [P, TILES, D])
    tw = TA * 4
    XRW = 3 + SEQ + DB * 7
    (XC, A, TR, TI, M, U, U1, GA) = [at(n, R_V + i * tw, [P, TA]) for i, n in
                                     enumerate(("xc", "a", "tr", "ti", "m", "u", "u1", "ga"))]
    XR = at("xr", R_V + 8 * tw, [P, XRW])
    R_M = 117 * K
    mh = at("mh", R_M, [P, KT, SEQ], F32R)
    ml = at("ml", R_M + 16 * K, [P, KT, SEQ], F32R)
    xt = at("xt", R_M, [P, TILES, D])
    lng = at("lng", R_M + 20 * K, [P, D])
    lnb = at("lnb", R_M + 24 * K, [P, D])
    junk = at("junk", R_M + 28 * K, [P, D])
    xn2 = at("xn2", R_M, [P, TILES, D])
    xg = at("xg", R_M + 20 * K, [P, 2, D])
    gy = at("gy", 48 * K, [P, 2, TILES, D])
    xn2T = at("xn2T", 79 * K, [P, KT, TA])
    nf = at("nf", R_M + 28 * K, [P, D])
    R_W = 149 * K
    raw = at("raw", R_W, [P, RAW, KT, P])
    wh = at("wh", R_W + 16 * K, [P, 2, D], F32R)
    wl = at("wl", R_W + 24 * K, [P, 2, D], F32R)
    xgT = at("xgT", R_W, [P, 2, KT, P])
    yo = at("yo", R_W + 8 * K, [P, D])
    junk2 = at("junk2", R_W + 12 * K, [P, D])
    hs = at("hs", R_W + 16 * K, [P, 2, FE])
    hm = at("hm", R_W + 18 * K, [P, 2, FE])
    hT = at("hT", R_W + 20 * K, [P, 2, 2, P])
    posh = at("posh", R_W + 22 * K, [P, 2 * TILES, P])
    colh = at("colh", R_W + 27 * K, [P, 2 * TILES, COLS])
    cmp_ = at("cmp", R_W + 29 * K, [P, 2 * TILES * NE])
    top = [181 * K]

    def small(name, shape, dt=F32):
        size = 4
        for n in shape[1:]:
            size *= n
        t = at(name, top[0], shape, dt)
        top[0] += -(-size // 32) * 32
        return t

    ch = small("ch", [P, KT, NCH])
    ident = small("ident", [P, P])
    ones = small("ones", [P, P], F32)
    upper = small("upper", [P, P], F32)
    fold = small("fold", [P, S])
    wsT = small("wsT", [P, HEADS, P])
    bdiag = small("bdiag", [S, HEADS, S])
    bsh = small("bsh", [P, HEADS, P])
    gw = small("gw", [P, 2, P])
    xs = small("xs", [P, KT, S])
    ms = small("ms", [P, KT, S])
    sp = small("sp", [P, 512])
    sq = small("sq", [P, 4, S])
    gbs = small("gbs", [P, S])
    so = small("so", [P, KT, OUTC])
    wrt = small("wrt", [P, KT, NL])
    brt = small("brt", [P, NL])
    ss = small("ss", [P, TILES])
    rstd = small("rstd", [P, TILES])
    ssa = small("ssa", [P, TILES])
    bnst = small("bnst", [P, 2, 6])
    bnag = small("bnag", [P, TILES, 2])
    csp = small("csp", [P, KT, 2])
    hb = small("hb", [P, KT, 2])
    t8 = small("t8", [P, 5, KT])
    lgg = small("lgg", [P, TILES, NG])
    lge = small("lge", [P, TILES, NE])
    r4 = small("r4", [P, TILES, NG])
    oh = small("oh", [P, TILES, NG])
    r1 = small("r1", [P, 8, TILES])
    key = small("key", [P, TILES, NE])
    ohe = small("ohe", [P, 2, TILES, NE])
    mcnt = small("mcnt", [P, TILES, NE])
    cum = small("cum", [P, TILES + 1, NE])
    first = small("first", [P, NE])
    iota = small("iota", [P, P])
    epair = small("epair", [P, NE])
    ehalf = small("ehalf", [P, NE])
    tokv = small("tokv", [P, 2, TILES])
    gate = small("gate", [P, 2, TILES])
    T2 = 2 * TILES
    (rk, chk, epr, ehf, ebx, isx, colv, posv) = [small(n, [P, T2]) for n in
                                                 ("rk", "chk", "epr", "ehf", "ebx", "isx", "colv", "posv")]
    xcnt = small("xcnt", [P, 3, NE])
    tab = small("tab", [P, 3, COLS])
    idxg = small("idxg", [P, COLS], U32)
    idxy = small("idxy", [P, COLS], U32)
    colg = small("colg", [P, 2], U32)
    coly = small("coly", [P, 1], U32)
    nxi = small("nxi", [1, 1 + EXTRA], I32)
    assert BASE + top[0] <= nc.sbuf_usable_end, top[0] / K

    with ExitStack() as ctx:
        ps = ctx.enter_context(nc.psum_tensor("ps", [P, 8, 512], F32))

        def sem(name):
            return ctx.enter_context(nc.semaphore(name))

        x_in = [sem(f"x_in{t}") for t in range(TILES)]
        const_in = sem("const_in")
        raw_in = [sem(f"raw_in{s}") for s in range(RAW)]
        slot_in = [sem(f"slot_in{s}") for s in range(4)]
        down_in = [sem(f"down_in{s}") for s in range(4)]
        gw_in = sem("gw_in")
        xres_in = sem("xres_in")
        bd_in = sem("bd_in")
        masks = sem("masks")
        xg_zero = sem("xg_zero")
        xn_stored = sem("xn_stored")
        xg_in = [sem("xg_in0"), sem("xg_in1")]
        y_out = sem("y_out")
        yo_free = sem("yo_free")
        back_in = [sem(f"back_in{n}") for n in range(TILES)]
        v_stored = sem("v_stored")
        done_out = sem("done_out")

        held = sem("held")
        act_s = sem("act_s")
        dve_s = sem("dve_s")
        pool_s = sem("pool_s")

        ss_ready = sem("ss_ready")
        ms_ready = sem("ms_ready")
        sq_ready = sem("sq_ready")
        xn_ready = sem("xn_ready")
        xT_ready = sem("xT_ready")
        xh_ready = sem("xh_ready")
        xl_ready = sem("xl_ready")
        xs_ready = sem("xs_ready")
        hi_ready = sem("hi_ready")
        lo_ready = sem("lo_ready")
        unit_done = sem("unit_done")
        vsum = sem("vsum")
        vfold = sem("vfold")
        v_gelu = sem("v_gelu")
        v_ready = sem("v_ready")
        z_mm = sem("z_mm")
        z_ready = sem("z_ready")
        sproj = sem("sproj")
        sproj_sb = sem("sproj_sb")
        sproj_T = sem("sproj_T")
        sq_sb = sem("sq_sb")
        xr_ev = sem("xr_ev")
        u_ev = sem("u_ev")
        ga_ev = sem("ga_ev")
        gb_ev = sem("gb_ev")
        u_sq = sem("u_sq")
        u_poly = sem("u_poly")
        u_tanh = sem("u_tanh")
        u_free = sem("u_free")
        conv_done = sem("conv_done")
        gates_mm = sem("gates_mm")
        gates_ev = sem("gates_ev")
        a_ready = sem("a_ready")
        m_poly = sem("m_poly")
        m_sqrt = sem("m_sqrt")
        ya_done = sem("ya_done")
        merged = sem("merged")
        x1_ready = sem("x1_ready")
        n2_ms = sem("n2_ms")
        n2_sq = sem("n2_sq")
        xn2_ready = sem("xn2_ready")
        xn2T_mm = sem("xn2T_mm")
        xn2T_sb = [sem("xn2T_even"), sem("xn2T_odd")]
        lg_mm = sem("lg_mm")
        ex_in = sem("ex_in")
        ex_out = sem("ex_out")
        cnt_in = sem("cnt_in")
        rank_mm = sem("rank_mm")
        pos_ready = sem("pos_ready")
        tab_mm = sem("tab_mm")
        tab_ready = sem("tab_ready")
        extra_ready = sem("extra_ready")
        col_copied = sem("col_copied")
        xgT_mm = sem("xgT_mm")
        xgT_sb = sem("xgT_sb")
        gu_mm = sem("gu_mm")
        silu_done = sem("silu_done")
        hm_ready = sem("hm_ready")
        hT_mm = sem("hT_mm")
        hT_sb = sem("hT_sb")
        pair_mm = sem("pair_mm")
        yo_sb = sem("yo_sb")
        comb = sem("comb")
        fin_ms = sem("fin_ms")
        fin_sq = sem("fin_sq")
        fin_ready = sem("fin_ready")
        so_ready = sem("so_ready")

        block = ctx.enter_context(nc.Block())

        def rowsof(t):
            return S if t == NT else P

        xp_tiles = [x[t * P:t * P + rowsof(t), :] for t in range(TILES)]
        y_tiles = [y[t * P:t * P + rowsof(t), :] for t in range(TILES)]
        NCONST = 16 * 8

        def v_banks(half):
            return ([0, 1, 2, 3], 4, 6) if half == 0 else ([5, 7, 0, 1], 2, 3)

        @block.sync
        def _(sp_):
            e = sp_
            for t in range(TILES):
                e.dma_start(xt[0:rowsof(t), t, :], xp_tiles[t]).then_inc(x_in[t], 16)
            e.dma_start(ch[:], chan).then_inc(const_in, 16)
            for n in range(4):
                e.dma_start(raw[:, n, :, :], wmix[n]).then_inc(raw_in[n], 16)
            e.dma_start(lng[:], rows[0:1, :].broadcast_to([P, D])).then_inc(const_in, 16)
            e.dma_start(lnb[:], rows[1:2, :].broadcast_to([P, D])).then_inc(const_in, 16)
            e.dma_start(wsT[:], wst).then_inc(const_in, 16)
            e.dma_start(bsh[:], bs.broadcast_to([P, HEADS * P]).rearrange("p (h t) -> p h t", h=HEADS)).then_inc(const_in, 16)
            e.dma_start(wrt[:], wr).then_inc(const_in, 16)
            e.dma_start(brt[:], br.broadcast_to([P, NL])).then_inc(const_in, 16)
            e.wait_ge(masks, 1)
            for b in range(DB):
                e.dma_start(bdiag[4 * b:4 * b + 4, :, 4 * b:4 * b + 4],
                            wst[0:4, :, 0:4]).then_inc(bd_in, 16)
            for n in range(4, 12):
                e.wait_ge(lo_ready, n - 3)
                e.wait_ge(unit_done, n - 3)
                e.dma_start(raw[:, n % RAW, :, :], wmix[n]).then_inc(raw_in[n % RAW], 16)
            GU = KT * 512
            for s in range(2):
                e.dma_start(wslot[s][:, 0:GU], wmoe[s][:, 0:GU]).then_inc(slot_in[s], 16)
                e.dma_start(wslot[s][:, GU:EW], wmoe[s][:, GU:EW]).then_inc(down_in[s], 16)
            with e.Fori(0, KT) as j:
                for p in range(4):
                    e.wait_ge(lo_ready, j * 4 + (8 + p + 1))
                    e.sem_inc(held, 1)
                    e.wait_ge(sproj, j + 1)
                    e.sem_inc(held, 1)
                    e.dma_start(raw[:, p, :, :], wmix[bass.ds(j * 4 + (12 + p), 1)].rearrange("a p k c -> (a p) k c")).then_inc(raw_in[p], 16)
            e.wait_ge(merged, FIRST + KT)
            for t in range(TILES):
                e.dma_start(x1[0:rowsof(t), t, :], xp_tiles[t]).then_inc(xres_in, 16)
            for n in range(44, 48):
                e.wait_ge(lo_ready, n - 3)
                e.wait_ge(unit_done, n - 3)
                e.dma_start(raw[:, n % RAW, :, :], wmix[n]).then_inc(raw_in[n % RAW], 16)
            e.dma_start(wslot[2][:, 0:GU], wmoe[2][:, 0:GU]).then_inc(slot_in[2], 16)
            e.dma_start(wslot[2][:, GU:EW], wmoe[2][:, GU:EW]).then_inc(down_in[2], 16)
            e.wait_ge(unit_done, 48)
            e.dma_start(nf[:], rows[2:3, :].broadcast_to([P, D])).then_inc(const_in, 16)
            e.wait_ge(lg_mm, 1)
            e.dma_start(wslot[3][:, 0:GU], wmoe[3][:, 0:GU]).then_inc(slot_in[3], 16)
            e.dma_start(wslot[3][:, GU:EW], wmoe[3][:, GU:EW]).then_inc(down_in[3], 16)
            with e.Fori(0, PAIRS // 2 - 1) as i:
                for q in range(2):
                    for have, lo, hi, into in ((gu_mm, 0, GU, slot_in), (pair_mm, GU, EW, down_in)):
                        e.wait_ge(have, i * 2 + (q + 1))
                        e.sem_inc(held, 1)
                        for s in (2 * q, 2 * q + 1):
                            e.dma_start(wslot[s][:, lo:hi], wmoe[bass.ds(i * 4 + (4 + s), 1), :, lo:hi].rearrange(
                                "a p c -> (a p) c")).then_inc(into[s], 16)
            e.wait_ge(extra_ready, 1)
            nx = e.value_load(nxi[0:1, 0:1], min_val=0, max_val=EXTRA)
            with e.If(nx > 0):
                with e.Fori(0, nx) as m:
                    ex = e.value_load(nxi[0:1, bass.ds(m + 1, 1)], min_val=0, max_val=NE - 1)
                    for have, lo, hi, into in ((gu_mm, 0, GU, slot_in), (pair_mm, GU, EW, down_in)):
                        e.wait_ge(have, m + PAIRS)
                        e.sem_inc(held, 1)
                        e.dma_start(wslot[0][:, lo:hi], wmoe[bass.ds(ex, 1), :, lo:hi].rearrange(
                            "a p c -> (a p) c")).then_inc(into[0], 16)
            e.wait_ge(yo_free, FIRST + nx + PAIRS)
            e.sem_inc(held, 1)
            for t in range(TILES):
                r = rowsof(t)
                for s in range(2):
                    e.dma_start(gy[0:r, s, t, :], ytok[s * TA + t * P:s * TA + t * P + r, :]).then_inc(back_in[t], 16)
            for t in range(TILES):
                e.wait_ge(fin_ready, t + 1)
                e.dma_start(y_tiles[t], xn2[0:rowsof(t), t, :]).then_inc(done_out, 16)
            e.wait_ge(v_stored, 32)
            e.wait_ge(done_out, 16 * (TILES + 1))

        @block.gpsimd
        def _(g):
            own = Steps(g, pool_s)
            g.memset(bdiag[:], 0.0).then_inc(masks, 1)
            own.then(g.memset(ident[:], 0.0))
            g.affine_select(out=ident[:], in_=ident[:], compare_op=ALU.not_equal, fill=1.0, base=0,
                            pattern=[[-1, P]], channel_multiplier=1).then_inc(masks, 1)
            own.then(g.memset(fold[:], 0.0))
            for q in range(4):
                i = g.affine_select(out=fold[:], in_=fold[:], compare_op=ALU.not_equal, fill=1.0,
                                    base=-S * q, pattern=[[-1, S]], channel_multiplier=1)
                if q < 3:
                    own.then(i)
            i.then_inc(masks, 1)
            g.memset(ones[:], 1.0).then_inc(masks, 1)
            own.then(g.memset(upper[:], 1.0))
            g.affine_select(out=upper[:], in_=upper[:], compare_op=ALU.is_gt, fill=0.0, base=0,
                            pattern=[[1, P]], channel_multiplier=-1).then_inc(masks, 1)
            g.wait_ge(const_in, NCONST - 16)
            g.affine_select(out=wsT[:], in_=wsT[:], compare_op=ALU.is_ge, fill=0.0, base=0,
                            pattern=[[0, HEADS], [1, P]], channel_multiplier=-1).then_inc(masks, 1)
            g.wait_ge(bd_in, 16 * DB)
            g.affine_select(out=bdiag[:], in_=bdiag[:], compare_op=ALU.is_ge, fill=0.0, base=0,
                            pattern=[[0, HEADS], [1, S]], channel_multiplier=-1).then_inc(masks, 1)
            for n in range(NE):
                g.memset(first[:, n:n + 1], float(NE - n))
            own.then(g.memset(ehalf[:], 0.0))
            g.memset(ehalf[:].rearrange("p (e a) -> p e a", a=2)[:, :, 1:2], float(CAP)).then_inc(masks, 1)
            g.wait_ge(v_ready, 1 + TILES)
            g.dma_start(vp, v[:, NT - 1, :]).then_inc(v_stored, 16)
            g.dma_start(vs, v[0:S, NT, :]).then_inc(v_stored, 16)
            with g.Fori(0, KT) as j:
                g.wait_ge(gates_mm, FIRST + j)
                g.dma_start(gw[:], wgate[bass.ds(j, 1)].rearrange("a p w c -> (a p) w c")).then_inc(gw_in, 16)
            g.wait_ge(unit_done, 48)
            g.memset(xg[:], 0.0).then_inc(xg_zero, 1)
            g.wait_ge(xn_stored, 16 * TILES)
            g.wait_ge(tab_ready, 1)
            g.wait_ge(xg_zero, 1)

            def gather(q, column, count):
                g.tensor_copy(colg[:, q:q + 1], idxg[:, column]).then_inc(col_copied, 1)
                g.wait_ge(col_copied, count)
                g.sem_inc(held, 1)
                return g.indirect_dma_start(
                    out=xg[:, q, :], out_offset=None, in_=xnd,
                    in_offset=bass.IndirectOffsetOnAxis(ap=colg[:, q:q + 1], axis=0),
                    bounds_check=TA - 1, oob_is_err=False)

            def scatter(column, count):
                g.tensor_copy(coly[:], idxy[:, column]).then_inc(col_copied, 1)
                g.wait_ge(col_copied, count)
                g.sem_inc(held, 1)
                return g.indirect_dma_start(
                    out=ytok, out_offset=bass.IndirectOffsetOnAxis(ap=coly[:, 0:1], axis=0),
                    in_=yo[:, :], in_offset=None, bounds_check=2 * TA - 1, oob_is_err=False)

            for q in range(2):
                gather(q, slice(q, q + 1), q + 1).then_inc(xg_in[q], 16)
            with g.Fori(0, PAIRS // 2 - 1) as i:
                for q in range(2):
                    G = i * 2 + q
                    g.wait_ge(yo_sb, FIRST + G + 1)
                    g.sem_inc(held, 1)
                    scatter(bass.ds(G, 1), G * 2 + 3).then_inc(y_out, 16)
                    gather(q, bass.ds(G + 2, 1), G * 2 + 4).then_inc(xg_in[q], 16)
                    g.wait_ge(y_out, G * 16 + 16)
                    g.sem_inc(yo_free, 1)
            for G in range(PAIRS - 2, PAIRS):
                g.wait_ge(yo_sb, FIRST + G + 1)
                scatter(slice(G, G + 1), PAIRS + G + 1).then_inc(y_out, 16)
                g.wait_ge(y_out, G * 16 + 16)
                g.sem_inc(yo_free, 1)
            g.wait_ge(extra_ready, 1)
            nx = g.value_load(nxi[0:1, 0:1], min_val=0, max_val=EXTRA)
            with g.If(nx > 0):
                with g.Fori(0, nx) as m:
                    g.wait_ge(xgT_mm, FIRST + m + PAIRS)
                    g.sem_inc(held, 1)
                    gather(0, bass.ds(m + PAIRS, 1), m * 2 + (2 * PAIRS + 1)).then_inc(xg_in[0], 16)
                    g.wait_ge(yo_sb, FIRST + m + (PAIRS + 1))
                    g.sem_inc(held, 1)
                    scatter(bass.ds(m + PAIRS, 1), m * 2 + (2 * PAIRS + 2)).then_inc(y_out, 16)
                    g.wait_ge(y_out, m * 16 + (PAIRS * 16 + 16))
                    g.sem_inc(yo_free, 1)

        @block.scalar
        def _(a):
            own = Steps(a, act_s)
            for first_one in (sproj_sb, xr_ev, u_ev, ga_ev, gates_ev, yo_sb, yo_free):
                a.sem_inc(first_one, FIRST)

            def split_hi(n, slot, hslot, count):
                a.wait_ge(raw_in[slot], count)
                if n is not None and n >= 2:
                    a.wait_ge(unit_done, n - 1)
                a.activation(wh[:, hslot, :], raw[:, slot, :, :].rearrange("p k c -> p (k c)"),
                             ACT.Copy).then_inc(hi_ready, 1)

            a.wait_ge(ss_ready, 1)
            for t in range(TILES):
                r = rowsof(t)
                a.wait_ge(x_in[t], 16)
                a.activation(junk[0:r, :], xt[0:r, t, :], ACT.Square, accum_out=ss[0:r, t:t + 1]).then_inc(sq_ready, 1)
                a.wait_ge(sq_ready, t + 1)
            a.wait_ge(ms_ready, 1)
            a.activation(rstd[:], ss[:], ACT.Sqrt).then_inc(sq_ready, 1)
            split_hi(0, 0, 0, 16)
            split_hi(1, 1, 1, 16)
            a.wait_ge(const_in, NCONST - 16)
            for k in range(KT):
                a.wait_ge(xT_ready, k + 1)
                a.activation(xh[:, k, :], ps[:, k % 4, :], ACT.Copy, scale=ch[:, k, C_G1:C_G1 + 1]).then_inc(xh_ready, 1)
            a.wait_ge(v_ready, 1)
            a.activation(t8[:, 1, :], t8[:, 0, :], ACT.Exp, scale=-1.0).then_inc(ex_out, 1)
            for half in range(2):
                banks, sbank, fbank = v_banks(half)
                for u in range(4):
                    n = half * 4 + u
                    a.wait_ge(unit_done, n + 1)
                    split_hi(n + 2, (n + 2) % RAW, n % 2, 16 * ((n + 2) // RAW + 1))
                a.activation(sp[:], ps[:, sbank, :], ACT.Copy).then_inc(vsum, 1)
                c = slice(half * 512, half * 512 + 512)
                for t in range(NT):
                    a.activation(v[:, t, c], ps[:, banks[t], :], ACT.Gelu_apprx_tanh).then_inc(v_gelu, 1)
                a.wait_ge(vfold, half + 1)
                a.activation(v[0:S, NT, c], ps[0:S, fbank, :], ACT.Gelu_apprx_tanh).then_inc(v_gelu, 1)
            a.wait_ge(ms_ready, 2)
            a.activation(rstd[:], ss[:], ACT.Sqrt).then_inc(sq_ready, 1)

            a.wait_ge(z_ready, 2 * KT)
            a.wait_ge(v_stored, 32)
            with a.Fori(0, KT) as j:
                smp = lambda t: t[:, SEQ:TA]
                def raw_count(extra):
                    return j * 16 + 16 * (2 + extra + 1)
                a.wait_ge(sproj, j + 1)
                a.wait_ge(sproj_T, FIRST + j)
                a.activation(sp[:], ps[:, 6, :], ACT.Copy).then_inc(sproj_sb, 1)
                a.wait_ge(unit_done, j * 4 + 9)
                split_hi(None, 2, 0, raw_count(0))
                a.wait_ge(conv_done, FIRST + j)
                a.activation(XR[:, 3:3 + SEQ], ps[:, 0, :], ACT.Copy).then_inc(xr_ev, 1)
                a.wait_ge(sproj_T, FIRST + j + 1)
                a.activation(sq[:].rearrange("p u s -> p (u s)"), ps[:, 7, 0:4 * S], ACT.Copy).then_inc(sq_sb, 1)
                a.wait_ge(sq_sb, j + 1)
                a.activation(XR[:, 3 + SEQ:XRW].rearrange("p (b s) -> p b s", b=DB)[:, :, 3:7],
                             sq[:, 0, :].rearrange("p (b s) -> p b s", b=DB), ACT.Copy).then_inc(xr_ev, 1)
                a.wait_ge(unit_done, j * 4 + 10)
                split_hi(None, 3, 1, raw_count(0))
                a.wait_ge(ya_done, FIRST + j)
                a.activation(U[:, 0:SEQ], ps[:, 1, :], ACT.Copy).then_inc(u_ev, 1)
                a.activation(smp(U), sq[:, 1, :], ACT.Copy).then_inc(u_ev, 1)
                a.wait_ge(u_ev, FIRST + j * 2 + 2)
                a.activation(U1[:], U[:], ACT.Square).then_inc(u_sq, 1)
                a.wait_ge(unit_done, j * 4 + 11)
                split_hi(None, 0, 0, raw_count(1))
                a.wait_ge(merged, FIRST + j)
                a.activation(GA[:, 0:SEQ], ps[:, 2, :], ACT.Tanh, scale=0.5).then_inc(ga_ev, 1)
                a.activation(smp(GA), sq[:, 2, :], ACT.Tanh, scale=0.5).then_inc(ga_ev, 1)
                a.wait_ge(u_poly, j + 1)
                a.activation(U1[:], U1[:], ACT.Tanh, scale=GELU_K).then_inc(u_tanh, 1)
                a.wait_ge(gates_mm, FIRST + j + 1)
                for w, T in ((0, TR), (1, TI)):
                    b = hb[:, bass.ds(j, 1), w]
                    a.activation(T[:, 0:SEQ], ps[:, 4 + w, :], ACT.Tanh, scale=0.5, bias=b).then_inc(gates_ev, 1)
                    a.activation(smp(T), ps[:, 7, (4 + w) * S:(5 + w) * S], ACT.Tanh, scale=0.5, bias=b).then_inc(gates_ev, 1)
                cp, cn = csp[:, bass.ds(j, 1), 0], csp[:, bass.ds(j, 1), 1]
                a.wait_ge(gates_ev, FIRST + j * 4 + 4)
                a.activation(A[:], TR[:], ACT.Exp, scale=cp, bias=cp).then_inc(a_ready, 1)
                a.activation(TR[:], TR[:], ACT.Tanh, scale=cn, bias=cn).then_inc(a_ready, 1)
                a.wait_ge(a_ready, j * 3 + 1)
                a.activation(M[:], A[:], ACT.Square).then_inc(a_ready, 1)
                a.wait_ge(unit_done, j * 4 + 12)
                split_hi(None, 1, 1, raw_count(1))
                a.activation(ps[:, 3, :], ps[:, 3, :], ACT.Tanh, scale=0.5).then_inc(gb_ev, 1)
                a.activation(gbs[:], sq[:, 3, :], ACT.Tanh, scale=0.5).then_inc(gb_ev, 1)
                a.wait_ge(m_poly, j + 1)
                a.activation(M[:], M[:], ACT.Sqrt).then_inc(m_sqrt, 1)

            for half in range(2):
                banks, sbank, fbank = v_banks(half)
                for u in range(4):
                    n = UNITS_V + UNITS_J + half * 4 + u
                    a.wait_ge(unit_done, n + 1)
                    if n + 2 < 48:
                        split_hi(n + 2, (n + 2) % RAW, n % 2, 16 * ((n + 2) // RAW + 1))
                if half:
                    a.wait_ge(vfold, 3)
                a.activation(sp[:], ps[:, sbank, :], ACT.Copy).then_inc(vsum, 1)
            for h in range(2):
                acc = (ssa, ss)[h]
                for t in range(TILES):
                    r = rowsof(t)
                    a.wait_ge(x1_ready, h * TILES + t + 1)
                    a.wait_ge(n2_sq, h * TILES + t)
                    a.activation(junk2[0:r, 0:512], x1[0:r, t, h * 512:h * 512 + 512], ACT.Square,
                                 accum_out=acc[0:r, t:t + 1]).then_inc(n2_sq, 1)
            a.wait_ge(n2_ms, 1)
            a.activation(rstd[:], ss[:], ACT.Sqrt).then_inc(n2_sq, 1)
            for k in range(0, KT, 2):
                a.wait_ge(xn2T_mm, k + 1)
                a.activation(xn2T[:, k, 0:SEQ], ps[:, k % 4, :], ACT.Copy, scale=ch[:, k, C_G2:C_G2 + 1]).then_inc(xn2T_sb[0], 1)
            a.wait_ge(n2_ms, 2)
            for t in range(TILES):
                r = rowsof(t)
                a.activation(xn2[0:r, t, :], x1[0:r, t, :], ACT.Copy, scale=rstd[0:r, t:t + 1]).then_inc(xn2_ready, 1)
                a.wait_ge(xn2_ready, t + 1)
                a.dma_start(xnd[t * P:t * P + r, :], xn2[0:r, t, :]).then_inc(xn_stored, 16)
            a.wait_ge(ex_in, 1)
            a.activation(r4[:], r4[:], ACT.Exp).then_inc(ex_out, 1)
            a.wait_ge(ex_in, 2)
            a.activation(r1[:, 3, :], r1[:, 2, :], ACT.Exp).then_inc(ex_out, 1)

            def pair(G, q):
                a.wait_ge(gu_mm, G + 1)
                a.activation(hs[:, q, :], ps[:, 2, 0:FE], ACT.Silu).then_inc(silu_done, 1)
                a.wait_ge(pair_mm, G + 1)
                a.wait_ge(yo_free, FIRST + G)
                a.activation(yo[:], ps[:, 6:8, :].rearrange("p b c -> p (b c)"), ACT.Copy).then_inc(yo_sb, 1)

            with a.Fori(0, PAIRS // 2) as i:
                for q in range(2):
                    pair(i * 2 + q, q)
            a.wait_ge(extra_ready, 1)
            nx = a.value_load(nxi[0:1, 0:1], min_val=0, max_val=EXTRA)
            with a.If(nx > 0):
                with a.Fori(0, nx) as m:
                    pair(m + PAIRS, 0)
            a.dma_start(st, so[:]).then_inc(done_out, 16)
            for t in range(TILES):
                r = rowsof(t)
                a.wait_ge(comb, 2 * t + 2)
                a.wait_ge(n2_sq, 2 * TILES + 1 + t)
                a.activation(junk2[0:r, :], x1[0:r, t, :], ACT.Square, accum_out=ss[0:r, t:t + 1]).then_inc(n2_sq, 1)
            a.wait_ge(fin_ms, 1)
            a.activation(rstd[:], ss[:], ACT.Sqrt).then_inc(fin_sq, 1)

        @block.vector
        def _(d):
            own = Steps(d, dve_s)
            for first_one in (conv_done, ya_done, merged, xgT_sb, hm_ready, hT_sb):
                d.sem_inc(first_one, FIRST)

            def split_lo(hslot, slot, count):
                d.wait_ge(hi_ready, count)
                d.tensor_tensor(wl[:, hslot, :], raw[:, slot, :, :].rearrange("p k c -> p (k c)"),
                                wh[:, hslot, :].bitcast(F32), ALU.subtract).then_inc(lo_ready, 1)

            def rsqrt_steps(wait_sum, sig_ms, sig_val, wait_sq, scale):
                wait_sum()
                d.tensor_scalar(ss[:], ss[:], scale, EPS, ALU.mult, ALU.add).then_inc(sig_ms, 1)
                wait_sq()
                own.then(d.reciprocal(rstd[:], rstd[:]))

            d.memset(ss[:], float(D)).then_inc(ss_ready, 1)
            rsqrt_steps(lambda: d.wait_ge(sq_ready, TILES), ms_ready, 1,
                        lambda: d.wait_ge(sq_ready, TILES + 1), 1.0 / D)
            for t in range(TILES):
                r = rowsof(t)
                d.tensor_scalar(xt[0:r, t, :], xt[0:r, t, :], rstd[0:r, t:t + 1], None, ALU.mult).then_inc(xn_ready, 1)
            split_lo(0, 0, 1)
            split_lo(1, 1, 2)
            d.wait_ge(const_in, NCONST - 16)
            for k in range(KT):
                d.wait_ge(xh_ready, k + 1)
                d.scalar_tensor_tensor(out=xl[:, k, :], in0=ps[:, k % 4, :], scalar=ch[:, k, C_G1:C_G1 + 1],
                                       in1=xh[:, k, :].bitcast(F32), op0=ALU.mult, op1=ALU.subtract).then_inc(xl_ready, 1)
            d.wait_ge(xT_ready, KT + 1)
            d.tensor_tensor(xs[:], ps[:, 4, 0:KT * S].rearrange("p (k s) -> p k s", k=KT),
                            ch[:, :, C_G1:C_G1 + 1].broadcast_to([P, KT, S]), ALU.mult).then_inc(xs_ready, 1)
            own.then(d.tensor_scalar(hb[:], ch[:, :, C_BA:C_BA + 2], 0.5, None, ALU.mult))
            own.then(d.tensor_scalar(bsh[:], bsh[:], 0.5, None, ALU.mult))
            lam = ch[:, :, C_LAM]
            d.scalar_tensor_tensor(out=t8[:, 0, :], in0=lam, scalar=-1.0, in1=lam, op0=ALU.mult, op1=ALU.max).then_inc(v_ready, 1)
            d.wait_ge(ex_out, 1)
            own.then(d.tensor_scalar(t8[:, 2, :], t8[:, 1, :], 2.0, None, ALU.add))
            own.then(d.reciprocal(t8[:, 2, :], t8[:, 2, :]))
            own.then(d.tensor_tensor(t8[:, 1, :], t8[:, 1, :], t8[:, 2, :], ALU.mult))
            own.then(d.tensor_tensor(t8[:, 2, :], t8[:, 1, :], t8[:, 1, :], ALU.mult))
            own.then(d.tensor_scalar(t8[:, 3, :], t8[:, 2, :], 1.0 / 17, 1.0 / 15, ALU.mult, ALU.add))
            for n in (13, 11, 9, 7, 5, 3, 1):
                own.then(d.tensor_tensor(t8[:, 3, :], t8[:, 3, :], t8[:, 2, :], ALU.mult))
                own.then(d.tensor_scalar(t8[:, 3, :], t8[:, 3, :], 1.0 / n, None, ALU.add))
            own.then(d.tensor_tensor(t8[:, 3, :], t8[:, 3, :], t8[:, 1, :], ALU.mult))
            own.then(d.tensor_scalar(t8[:, 4, :], lam, -1.0, 0.0, ALU.mult, ALU.max))
            own.then(d.scalar_tensor_tensor(out=t8[:, 3, :], in0=t8[:, 3, :], scalar=2.0, in1=t8[:, 4, :],
                                            op0=ALU.mult, op1=ALU.add))
            own.then(d.tensor_scalar(csp[:, :, 0], t8[:, 3, :], -4.0, None, ALU.mult))
            own.then(d.tensor_scalar(csp[:, :, 1], t8[:, 3, :], 4.0, None, ALU.mult))
            for n in range(UNITS_V):
                split_lo(n % 2, (n + 2) % RAW, n + 3)
            own.then(d.memset(bnag[:], 1.0))
            for t in range(TILES):
                r = rowsof(t)
                d.wait_ge(v_gelu, TILES + t + 1)
                for h in range(2):
                    own.then(d.bn_stats(bnst[0:r, h, :], v[0:r, t, h * 512:(h + 1) * 512]))
                own.then(d.bn_aggr(bnag[0:r, t, :], bnst[0:r, :, :]))
            d.tensor_scalar(ss[:], bnag[:, :, 1], EPS, None, ALU.add).then_inc(ms_ready, 1)
            d.wait_ge(sq_ready, TILES + 2)
            own.then(d.reciprocal(rstd[:], rstd[:]))
            d.wait_ge(const_in, NCONST - 16)
            for t in range(TILES):
                r = rowsof(t)
                vt = v[0:r, t, :]
                own.then(d.tensor_scalar(vt, vt, bnag[0:r, t, 0:1], rstd[0:r, t:t + 1], ALU.subtract, ALU.mult))
                own.then(d.tensor_tensor(vt, vt, lng[0:r, :], ALU.mult))
                d.tensor_tensor(vt, vt, lnb[0:r, :], ALU.add).then_inc(v_ready, 1)
            for j in range(KT):
                h = j // 2
                d.wait_ge(z_mm, j + 1)
                d.scalar_tensor_tensor(
                    out=zT[:, j, 0:SEQ].rearrange("p (c t) -> p c t", c=NT),
                    in0=ps[:, j % 4, :].rearrange("p (c t) -> p c t", c=NT), scalar=0.5,
                    in1=bsh[:, h:h + 1, :].broadcast_to([P, NT, P]), op0=ALU.mult, op1=ALU.add).then_inc(z_ready, 1)
            for j in range(KT):
                h = j // 2
                d.wait_ge(z_mm, KT + 1)
                d.scalar_tensor_tensor(
                    out=zT[:, j, SEQ:TA].rearrange("p (b s) -> p b s", b=DB),
                    in0=ps[:, 5, j * S:(j + 1) * S].rearrange("p (b s) -> p b s", b=DB), scalar=0.5,
                    in1=bsh[:, h:h + 1, 0:DS].broadcast_to([P, DB, DS]), op0=ALU.mult, op1=ALU.add).then_inc(z_ready, 1)
            d.wait_ge(v_stored, 32)
            own.then(d.memset(XR[:, 0:3], 0.0))
            xrs = XR[:, 3 + SEQ:XRW].rearrange("p (b s) -> p b s", b=DB)
            smp = lambda t: t[:, SEQ:TA].rearrange("p (b s) -> p b s", b=DB)
            with d.Fori(0, KT) as j:
                own.enter(j, 25)
                col = lambda c, n=1: ch[:, bass.ds(j, 1), c:c + n].rearrange("p a c -> p (a c)")
                n0 = UNITS_V
                split_lo(0, 2, j * 4 + (n0 + 3))
                d.wait_ge(gates_mm, FIRST + j)
                own.then(d.tensor_copy(xrs[:, :, 0:3], col(C_ST, 24).rearrange("p (b s) -> p b s", b=DB)))
                d.wait_ge(xr_ev, FIRST + j * 2 + 2)
                own.then(d.tensor_scalar(XC[:, 0:SEQ], XR[:, 3:3 + SEQ], col(C_W0 + 3), col(C_CB), ALU.mult, ALU.add))
                own.then(d.tensor_scalar(smp(XC), xrs[:, :, 3:7], col(C_W0 + 3), col(C_CB), ALU.mult, ALU.add))
                for t in range(3):
                    own.then(d.scalar_tensor_tensor(out=XC[:, 0:SEQ], in0=XR[:, t:t + SEQ], scalar=col(C_W0 + t),
                                                    in1=XC[:, 0:SEQ], op0=ALU.mult, op1=ALU.add))
                    i = d.scalar_tensor_tensor(out=smp(XC), in0=xrs[:, :, t:t + 4], scalar=col(C_W0 + t),
                                               in1=smp(XC), op0=ALU.mult, op1=ALU.add)
                    if t < 2:
                        own.then(i)
                own.then(i)
                sj = so[:, bass.ds(j, 1), :].rearrange("p a c -> p (a c)")
                d.tensor_copy(sj[:, 9:12], XR[:, SEQ:SEQ + 3])
                d.tensor_copy(sj[:, 12:36].rearrange("p (b s) -> p b s", b=DB), xrs[:, :, 4:7]).then_inc(conv_done, 1)
                split_lo(1, 3, j * 4 + (n0 + 4))
                d.wait_ge(u_sq, j + 1)
                own.then(d.tensor_scalar(U1[:], U1[:], GELU_C, 1.0, ALU.mult, ALU.add))
                d.tensor_tensor(U1[:], U1[:], U[:], ALU.mult).then_inc(u_poly, 1)
                split_lo(0, 0, j * 4 + (n0 + 5))
                d.wait_ge(u_tanh, j + 1)
                own.then(d.scalar_tensor_tensor(out=U1[:], in0=U1[:], scalar=1.0, in1=U[:], op0=ALU.add, op1=ALU.mult))
                d.tensor_tensor(U1[:], U1[:], zT[:, bass.ds(j, 1), :].rearrange("p a t -> p (a t)"), ALU.mult).then_inc(u_free, 1)
                d.wait_ge(u_free, j + 1)
                d.wait_ge(ga_ev, FIRST + j * 2 + 2)
                d.scalar_tensor_tensor(out=GA[:], in0=GA[:], scalar=1.0, in1=U1[:], op0=ALU.add, op1=ALU.mult).then_inc(ya_done, 1)
                d.wait_ge(a_ready, j * 3 + 3)
                d.scalar_tensor_tensor(out=M[:], in0=M[:], scalar=1.0, in1=TR[:], op0=ALU.add, op1=ALU.mult).then_inc(m_poly, 1)
                own.then(d.scalar_tensor_tensor(out=TI[:], in0=TI[:], scalar=1.0, in1=XC[:], op0=ALU.add, op1=ALU.mult))
                split_lo(1, 1, j * 4 + (n0 + 6))
                d.wait_ge(m_sqrt, j + 1)
                own.then(d.memset(M[:, 0:1], 1.0))
                own.then(d.scalar_tensor_tensor(out=TI[:], in0=TI[:], scalar=0.5, in1=M[:], op0=ALU.mult, op1=ALU.mult))
                own.then(d.tensor_tensor(TR[:, 0:DB], smp(A)[:, :, 0], col(C_H0, DB), ALU.mult))
                own.then(d.tensor_tensor(smp(TI)[:, :, 0], smp(TI)[:, :, 0], TR[:, 0:DB], ALU.add))
                own.then(d.memset(smp(A)[:, :, 0], 0.0))
                own.then(d.tensor_tensor_scan(XC[:], A[:], TI[:], 0.0, ALU.mult, ALU.add))
                own.then(d.tensor_copy(sj[:, 0:1], XC[:, SEQ - 1:SEQ]))
                own.then(d.tensor_copy(sj[:, 1:9], smp(XC)[:, :, DS - 1]))
                d.wait_ge(gb_ev, j * 2 + 2)
                own.then(d.scalar_tensor_tensor(out=M[:, 0:SEQ], in0=ps[:, 3, :], scalar=1.0, in1=XC[:, 0:SEQ],
                                                op0=ALU.add, op1=ALU.mult))
                own.then(d.scalar_tensor_tensor(out=M[:, SEQ:TA], in0=gbs[:], scalar=1.0, in1=XC[:, SEQ:TA],
                                                op0=ALU.add, op1=ALU.mult))
                own.then(d.tensor_tensor(M[:], M[:], GA[:], ALU.add))
                own.then(d.tensor_copy(mh[:, bass.ds(j, 1), :].rearrange("p a t -> p (a t)"), M[:, 0:SEQ]))
                own.then(d.tensor_copy(ms[:, bass.ds(j, 1), :].rearrange("p a t -> p (a t)"), M[:, SEQ:TA]))
                d.tensor_tensor(ml[:, bass.ds(j, 1), :].rearrange("p a t -> p (a t)"), M[:, 0:SEQ],
                                mh[:, bass.ds(j, 1), :].rearrange("p a t -> p (a t)").bitcast(F32),
                                ALU.subtract).then_inc(merged, 1)
                own.leave(KT)
            d.wait_ge(masks, 8)
            own.then(d.tensor_tensor_scan(iota[:], ones[:], ones[:], 0.0, ALU.mult, ALU.add))
            own.then(d.tensor_scalar(iota[:], iota[:], -1.0, None, ALU.add))
            own.then(d.reduce_sum(r1[:, 7, 0:1], upper[:], axis=AX))
            for s in range(2):
                for t in range(TILES):
                    own.then(d.tensor_scalar(tokv[:, s, t:t + 1], r1[:, 7, 0:1], -1.0, float(P + s * TA + t * P), ALU.mult, ALU.add))
            own.then(d.tensor_copy(epair[:].rearrange("p (e a) -> p e a", a=2),
                                   iota[:, 0:PAIRS].rearrange("p (e a) -> p e a", a=1).broadcast_to([P, PAIRS, 2])))
            own.then(d.memset(cum[:, 0, :], 0.0))
            own.then(d.memset(mcnt[:], 0.0))
            d.memset(ssa[:], float(D) / 2).then_inc(so_ready, 1)
            for half in range(2):
                banks, sbank, fbank = v_banks(half)
                c = slice(half * 512, half * 512 + 512)
                for u in range(4):
                    n = UNITS_V + UNITS_J + half * 4 + u
                    if n + 2 < 48:
                        split_lo(n % 2, (n + 2) % RAW, n + 3)
                d.wait_ge(unit_done, 44 + 4 * half)
                d.wait_ge(xres_in, 16 * TILES)
                for t in range(NT):
                    d.scalar_tensor_tensor(out=x1[:, t, c], in0=ps[:, banks[t], :], scalar=0.5, in1=x1[:, t, c],
                                           op0=ALU.mult, op1=ALU.add).then_inc(x1_ready, 1)
                d.wait_ge(vfold, 3 + half)
                d.scalar_tensor_tensor(out=x1[0:S, NT, c], in0=ps[0:S, fbank, :], scalar=0.5, in1=x1[0:S, NT, c],
                                       op0=ALU.mult, op1=ALU.add).then_inc(x1_ready, 1)
            d.wait_ge(so_ready, 1)
            d.wait_ge(n2_sq, 2 * TILES)
            own.then(d.tensor_tensor(ss[:], ss[:], ssa[:], ALU.add))
            d.tensor_scalar(ss[:], ss[:], 1.0 / D, EPS, ALU.mult, ALU.add).then_inc(n2_ms, 1)
            d.wait_ge(n2_sq, 2 * TILES + 1)
            d.reciprocal(rstd[:], rstd[:]).then_inc(n2_ms, 1)
            for k in range(1, KT, 2):
                d.wait_ge(xn2T_mm, k + 1)
                d.tensor_scalar(xn2T[:, k, 0:SEQ], ps[:, k % 4, :], ch[:, k, C_G2:C_G2 + 1], None, ALU.mult).then_inc(xn2T_sb[1], 1)
            d.wait_ge(xn2T_mm, KT + 1)
            d.tensor_tensor(xn2T[:, :, SEQ:TA], ps[:, 4, 0:KT * S].rearrange("p (k s) -> p k s", k=KT),
                            ch[:, :, C_G2:C_G2 + 1].broadcast_to([P, KT, S]), ALU.mult).then_inc(xn2T_sb[1], 1)

            def bc(t, n):
                return t.rearrange("p (t a) -> p t a", a=1).broadcast_to([P, t.shape[1], n])

            def row(t, m):
                return t.rearrange("p (a n) -> p a n", a=1).broadcast_to([P, m, t.shape[1]])

            def first_max(out, keys, maxv, n, mv):
                own.then(d.reduce_max(maxv, keys, axis=AX))
                own.then(d.tensor_tensor(out, keys, bc(maxv, n), ALU.is_ge))
                own.then(d.tensor_tensor(out, out, row(first[:, 0:n], TILES), ALU.mult))
                own.then(d.reduce_max(mv, out, axis=AX))
                own.then(d.tensor_tensor(out, out, bc(mv, n), ALU.is_equal))

            d.wait_ge(lg_mm, 1)
            d.wait_ge(n2_ms, 2)
            lps = ps[:, 5, 0:TILES * NL].rearrange("p (t n) -> p t n", t=TILES)
            own.then(d.tensor_tensor(lgg[:], lps[:, :, 0:NG], bc(rstd[:], NG), ALU.mult))
            own.then(d.tensor_tensor(lge[:], lps[:, :, NG:NL], bc(rstd[:], NE), ALU.mult))
            own.then(d.tensor_tensor(lgg[:], lgg[:], row(brt[:, 0:NG], TILES), ALU.add))
            own.then(d.tensor_tensor(lge[:], lge[:], row(brt[:, NG:NL], TILES), ALU.add))
            first_max(oh[:], lgg[:], r1[:, 0, :], NG, r1[:, 1, :])
            d.tensor_tensor(r4[:], lgg[:], bc(r1[:, 0, :], NG), ALU.subtract).then_inc(ex_in, 1)
            own.then(d.tensor_scalar(oh[:], oh[:], MASKED, -MASKED, ALU.mult, ALU.add))
            own.then(d.tensor_tensor(lge[:].rearrange("p t (g e) -> p (t g) e", e=EG), lge[:].rearrange("p t (g e) -> p (t g) e", e=EG),
                                     bc(oh[:].rearrange("p t g -> p (t g)"), EG), ALU.add))
            first_max(ohe[:, 0], lge[:], r1[:, 0, :], NE, r1[:, 1, :])
            own.then(d.scalar_tensor_tensor(out=key[:], in0=ohe[:, 0], scalar=-2 * MASKED, in1=lge[:], op0=ALU.mult, op1=ALU.add))
            first_max(ohe[:, 1], key[:], r1[:, 4, :], NE, r1[:, 1, :])
            d.tensor_tensor(mcnt[:, 0:NT, :], ohe[:, 0, 0:NT, :], ohe[:, 1, 0:NT, :], ALU.add)
            own.then(d.tensor_tensor(mcnt[0:S, NT, :], ohe[0:S, 0, NT, :], ohe[0:S, 1, NT, :], ALU.add))
            for t in range(TILES):
                i = d.tensor_tensor(cum[:, t + 1, :], cum[:, t, :], mcnt[:, t, :], ALU.add)
                if t < NT:
                    own.then(i)
            i.then_inc(cnt_in, 1)
            oh10 = ohe[:].rearrange("p s t e -> p (s t) e")
            pick = cmp_[:].rearrange("p (t e) -> p t e", e=NE)

            def choose(out, values):
                own.then(d.tensor_tensor(pick, oh10, values, ALU.mult))
                own.then(d.reduce_sum(out, pick, axis=AX))

            choose(epr[:], row(epair[:], T2))
            choose(ehf[:], row(ehalf[:], T2))
            d.tensor_tensor(r1[:, 2, :], r1[:, 4, :], r1[:, 0, :], ALU.subtract).then_inc(ex_in, 1)
            d.wait_ge(rank_mm, 1)
            total = ps[:, 0, TILES * NE:(TILES + 1) * NE]
            nck = MAXCHUNK - 1
            caps = tab[:, 0, 0:nck]
            own.then(d.tensor_scalar(caps, iota[:, 1:MAXCHUNK], float(CAP), None, ALU.mult))
            c8 = cmp_[:, 0:NE * nck].rearrange("p (e c) -> p e c", c=nck)
            own.then(d.tensor_tensor(c8, bc(total, nck), row(caps, NE), ALU.is_gt))
            own.then(d.reduce_sum(xcnt[:, 0, :], c8, axis=AX))
            own.then(d.tensor_tensor_scan(xcnt[:, 1, :], ones[:, 0:NE], xcnt[:, 0, :], 0.0, ALU.mult, ALU.add))
            own.then(d.scalar_tensor_tensor(out=xcnt[:, 2, :], in0=xcnt[:, 1, :], scalar=float(PAIRS - 1), in1=xcnt[:, 0, :],
                                            op0=ALU.add, op1=ALU.subtract))
            choose(ebx[:], row(xcnt[:, 2, :], T2))
            own.then(d.tensor_tensor(cmp_[:].rearrange("p (s n) -> p s n", s=2), ohe[:].rearrange("p s t e -> p s (t e)"),
                                     row(ps[:, 0, 0:TILES * NE], 2), ALU.mult))
            own.then(d.reduce_sum(rk[:], pick, axis=AX))
            c10 = cmp_[:, 0:T2 * nck].rearrange("p (e c) -> p e c", c=nck)
            own.then(d.tensor_tensor(c10, bc(rk[:], nck), row(caps, T2), ALU.is_ge))
            own.then(d.reduce_sum(chk[:], c10, axis=AX))
            own.then(d.tensor_scalar(isx[:], chk[:], 1.0, None, ALU.is_ge))
            own.then(d.tensor_tensor(ebx[:], ebx[:], chk[:], ALU.add))
            own.then(d.tensor_tensor(ebx[:], ebx[:], epr[:], ALU.subtract))
            own.then(d.tensor_tensor(ebx[:], ebx[:], isx[:], ALU.mult))
            own.then(d.tensor_tensor(colv[:], ebx[:], epr[:], ALU.add))
            own.then(d.scalar_tensor_tensor(out=posv[:], in0=chk[:], scalar=-float(CAP), in1=rk[:], op0=ALU.mult, op1=ALU.add))
            own.then(d.tensor_scalar(isx[:], isx[:], -1.0, 1.0, ALU.mult, ALU.add))
            own.then(d.tensor_tensor(ehf[:], ehf[:], isx[:], ALU.mult))
            own.then(d.tensor_tensor(posv[:], posv[:], ehf[:], ALU.add))
            own.then(d.tensor_tensor(colh[:], row(iota[:, 0:COLS], T2), bc(colv[:], COLS), ALU.is_equal))
            own.then(d.tensor_tensor(colh[:], colh[:], bc(tokv[:].rearrange("p s t -> p (s t)"), COLS), ALU.mult))
            d.tensor_tensor(posh[:], row(iota[:], T2), bc(posv[:], P), ALU.is_equal).then_inc(pos_ready, 1)
            own.then(d.tensor_copy(nxi[0:1, 0:1], xcnt[0:1, 1, NE - 1:NE]))
            for m in range(EXTRA):
                own.then(d.tensor_scalar(cmp_[0:1, 0:NE], xcnt[0:1, 1, :], float(m), None, ALU.is_le))
                own.then(d.reduce_sum(tab[0:1, 1, m:m + 1], cmp_[0:1, 0:NE], axis=AX))
            d.tensor_copy(nxi[0:1, 1:1 + EXTRA], tab[0:1, 1, 0:EXTRA]).then_inc(extra_ready, 1)
            d.wait_ge(tab_mm, 1)
            own.then(d.tensor_scalar(tab[:, 0, :], ps[:, 1, 0:COLS], 0.5, OUT_OF_RANGE, ALU.is_lt, ALU.mult))
            own.then(d.tensor_scalar(tab[:, 1, :], ps[:, 1, 0:COLS], TA + 0.5, float(-TA), ALU.is_gt, ALU.mult))
            own.then(d.scalar_tensor_tensor(out=tab[:, 2, :], in0=tab[:, 0, :], scalar=-1.0, in1=ps[:, 1, 0:COLS], op0=ALU.add, op1=ALU.add))
            own.then(d.tensor_copy(idxy[:], tab[:, 2, :]))
            d.tensor_tensor(idxg[:], tab[:, 2, :], tab[:, 1, :], ALU.add).then_inc(tab_ready, 1)
            d.wait_ge(ex_out, 3)
            own.then(d.reduce_sum(r1[:, 1, :], r4[:], axis=AX))
            own.then(d.reciprocal(r1[:, 5, :], r1[:, 1, :]))
            own.then(d.tensor_scalar(r1[:, 6, :], r1[:, 3, :], 1.0, None, ALU.add))
            own.then(d.reciprocal(r1[:, 6, :], r1[:, 6, :]))
            own.then(d.tensor_tensor(gate[:, 0, :], r1[:, 6, :], r1[:, 5, :], ALU.mult))
            own.then(d.tensor_tensor(gate[:, 1, :], gate[:, 0, :], r1[:, 3, :], ALU.mult))

            def pair(G, q):
                d.wait_ge(xgT_mm, FIRST + G + 1)
                d.tensor_tensor(xgT[:, q, :, :], ps[:, 0:2, :].rearrange("p b (k c) -> p (b k) c", c=P),
                                ch[:, :, C_G2:C_G2 + 1].broadcast_to([P, KT, P]), ALU.mult).then_inc(xgT_sb, 1)
                d.wait_ge(silu_done, G + 1)
                d.tensor_tensor(hm[:, q, :], hs[:, q, :], ps[:, 2, FE:2 * FE], ALU.mult).then_inc(hm_ready, 1)
                d.wait_ge(hT_mm, G + 1)
                d.tensor_copy(hT[:, q, :, :].rearrange("p f c -> p (f c)"), ps[:, 3, 0:2 * P]).then_inc(hT_sb, 1)

            with d.Fori(0, PAIRS // 2) as i:
                for q in range(2):
                    pair(i * 2 + q, q)
            nx = d.value_load(nxi[0:1, 0:1], min_val=0, max_val=EXTRA)
            with d.If(nx > 0):
                with d.Fori(0, nx) as m:
                    pair(m + PAIRS, 0)
            for t in range(TILES):
                r = rowsof(t)
                d.wait_ge(back_in[t], 32)
                for s in range(2):
                    d.scalar_tensor_tensor(out=x1[0:r, t, :], in0=gy[0:r, s, t, :], scalar=gate[0:r, s, t:t + 1],
                                           in1=x1[0:r, t, :], op0=ALU.mult, op1=ALU.add).then_inc(comb, 1)
                    if s == 0:
                        d.wait_ge(comb, 2 * t + 1)
            rsqrt_steps(lambda: d.wait_ge(n2_sq, 3 * TILES + 1), fin_ms, 1, lambda: d.wait_ge(fin_sq, 1), 1.0 / D)
            d.wait_ge(const_in, NCONST)
            for t in range(TILES):
                r = rowsof(t)
                d.scalar_tensor_tensor(out=xn2[0:r, t, :], in0=x1[0:r, t, :], scalar=rstd[0:r, t:t + 1], in1=nf[0:r, :],
                                       op0=ALU.mult, op1=ALU.mult).then_inc(fin_ready, 1)

        @block.tensor
        def _(pe):
            for first_one in (sproj_T, gates_mm, xgT_mm):
                pe.sem_inc(first_one, FIRST)
            def product(out, sh, sl, mh_, ml_, start, stop):
                pe.matmul(out, sh, mh_, start=start, stop=False)
                pe.matmul(out, sl, mh_, start=False, stop=False)
                return pe.matmul(out, sh, ml_, start=False, stop=stop)

            def token_rows(base, half, sth, stl, sts):
                banks, sbank, fbank = v_banks(half)
                for u in range(4):
                    n = base + half * 4 + u
                    slot = n % RAW
                    pe.wait_ge(hi_ready, n + 1)
                    pe.wait_ge(lo_ready, n + 1)
                    wr_ = raw[:, slot, :, :].rearrange("p k c -> p (k c)")
                    for t in range(NT):
                        for kk in range(2):
                            k = 2 * u + kk
                            c = slice(kk * 512, kk * 512 + 512)
                            tok = slice(t * P, t * P + P)
                            product(ps[:, banks[t], :], sth[:, k, tok], stl[:, k, tok], wh[:, n % 2, c], wl[:, n % 2, c],
                                    k == 0, k == KT - 1)
                    for kk in range(2):
                        k = 2 * u + kk
                        q = k % 4
                        last = pe.matmul(ps[S * q:S * q + S, sbank, :], sts[:, k, :], wr_[:, kk * 512:kk * 512 + 512],
                                         start=k < 4, stop=k >= 4, tile_position=(0, S * q), skip_group_check=True)
                    last.then_inc(unit_done, 1)

            def fold_rows(half, count):
                pe.wait_ge(vsum, count)
                pe.matmul(ps[0:S, v_banks(half)[2], :], fold[:], sp[:], start=True, stop=True).then_inc(vfold, 1)

            pe.wait_ge(masks, 2)
            pe.wait_ge(xn_ready, TILES)
            for k in range(KT):
                if k >= 4:
                    pe.wait_ge(xl_ready, k - 3)
                for t in range(NT):
                    i = pe.transpose(ps[:, k % 4, t * P:(t + 1) * P], xt[:, t, k * P:(k + 1) * P], ident[:])
                i.then_inc(xT_ready, 1)
            for k in range(KT):
                i = pe.transpose(ps[:, 4, k * S:(k + 1) * S], xt[0:S, NT, k * P:(k + 1) * P], ident[0:S, 0:S])
            i.then_inc(xT_ready, 1)
            pe.wait_ge(xl_ready, KT)
            pe.wait_ge(xh_ready, KT)
            pe.wait_ge(xs_ready, 1)
            pe.wait_ge(masks, 3)
            token_rows(0, 0, xh, xl, xs)
            fold_rows(0, 1)
            pe.wait_ge(v_gelu, NT)
            pe.wait_ge(vsum, 1)
            token_rows(0, 1, xh, xl, xs)
            fold_rows(1, 2)
            pe.wait_ge(masks, 7)
            pe.wait_ge(v_gelu, 2 * TILES)
            pe.wait_ge(v_ready, 1 + TILES)
            for j in range(KT):
                if j >= 4:
                    pe.wait_ge(z_ready, j - 3)
                for c in range(NT):
                    i = pe.matmul(ps[:, j % 4, c * P:(c + 1) * P], v[:, c, j * P:(j + 1) * P], wsT[:, j // 2, :], start=True, stop=True)
                i.then_inc(z_mm, 1)
            for j in range(KT):
                i = pe.matmul(ps[:, 5, j * S:(j + 1) * S], v[0:S, NT, j * P:(j + 1) * P], bdiag[:, j // 2, :],
                              start=True, stop=True)
            i.then_inc(z_mm, 1)
            pe.wait_ge(z_ready, 2 * KT)
            with pe.Fori(0, KT) as j:
                for s in range(RAW):
                    pe.wait_ge(raw_in[s], j * 16 + 48)
                pe.wait_ge(sproj_sb, FIRST + j)
                for k in range(KT):
                    q = k % 4
                    i = pe.matmul(ps[S * q:S * q + S, 6, :].rearrange("p (u c) -> p u c", u=4), xs[:, k, :], raw[:, :, k, :],
                                  start=k < 4, stop=k >= 4, tile_position=(0, S * q), skip_group_check=True)
                i.then_inc(sproj, 1)
                for p, freed in enumerate((xr_ev, u_ev, ga_ev, None)):
                    pe.wait_ge(hi_ready, j * 4 + (UNITS_V + p + 1))
                    pe.wait_ge(lo_ready, j * 4 + (UNITS_V + p + 1))
                    if freed is not None:
                        pe.wait_ge(freed, FIRST + j * 2)
                    else:
                        pe.wait_ge(merged, FIRST + j)
                    for k in range(KT):
                        c = slice(k * P, k * P + P)
                        i = product(ps[:, p, :], wh[:, p % 2, c], wl[:, p % 2, c], xh[:, k, :], xl[:, k, :], k == 0, k == KT - 1)
                    i.then_inc(unit_done, 1)
                    if p == 0:
                        pe.wait_ge(sproj_sb, FIRST + j + 1)
                        pe.wait_ge(gates_ev, FIRST + j * 4)
                        for u in range(4):
                            i = pe.matmul(ps[:, 7, u * S:(u + 1) * S], sp[:, u * P:(u + 1) * P], fold[:], start=True, stop=True)
                        i.then_inc(sproj_T, 1)
                    if p == 2:
                        pe.wait_ge(conv_done, FIRST + j + 1)
                        pe.wait_ge(gw_in, j * 16 + 16)
                        pe.wait_ge(sq_sb, j + 1)
                        pe.wait_ge(gates_ev, FIRST + j * 4)
                        for w in range(2):
                            pe.matmul(ps[:, 4 + w, :], gw[:, w, :], XC[:, 0:SEQ], start=True, stop=True)
                            i = pe.matmul(ps[:, 7, (4 + w) * S:(5 + w) * S], gw[:, w, :], XC[:, SEQ:TA], start=True, stop=True)
                        i.then_inc(gates_mm, 1)
            pe.wait_ge(merged, FIRST + KT)
            pe.wait_ge(gates_ev, FIRST + 4 * KT)
            pe.wait_ge(sproj_sb, FIRST + KT)
            token_rows(UNITS_V + UNITS_J, 0, mh, ml, ms)
            fold_rows(0, 3)
            pe.wait_ge(x1_ready, NT)
            token_rows(UNITS_V + UNITS_J, 1, mh, ml, ms)
            pe.wait_ge(x1_ready, TILES)
            fold_rows(1, 4)
            pe.wait_ge(x1_ready, 2 * TILES)
            for k in range(KT):
                if k >= 4:
                    pe.wait_ge(xn2T_sb[k % 2], (k - 4) // 2 + 1)
                for t in range(NT):
                    i = pe.transpose(ps[:, k % 4, t * P:(t + 1) * P], x1[:, t, k * P:(k + 1) * P], ident[:])
                i.then_inc(xn2T_mm, 1)
            for k in range(KT):
                i = pe.transpose(ps[:, 4, k * S:(k + 1) * S], x1[0:S, NT, k * P:(k + 1) * P], ident[0:S, 0:S])
            i.then_inc(xn2T_mm, 1)
            pe.wait_ge(xn2T_sb[0], KT // 2)
            pe.wait_ge(xn2T_sb[1], KT // 2 + 1)
            for t in range(TILES):
                r = rowsof(t)
                for k in range(KT):
                    i = pe.matmul(ps[0:r, 5, t * NL:(t + 1) * NL], xn2T[:, k, t * P:t * P + r], wrt[:, k, :],
                                  start=k == 0, stop=k == KT - 1)
            i.then_inc(lg_mm, 1)
            pe.wait_ge(cnt_in, 1)
            pe.matmul(ps[:, 0, 0:(TILES + 1) * NE], ones[:], cum[:].rearrange("p t e -> p (t e)"), start=True, stop=False)
            pe.matmul(ps[:, 0, 0:TILES * NE], upper[:], mcnt[:].rearrange("p t e -> p (t e)"), start=False, stop=True).then_inc(rank_mm, 1)
            pe.wait_ge(pos_ready, 1)
            for n in range(2 * TILES):
                r = rowsof(n % TILES)
                i = pe.matmul(ps[:, 1, 0:COLS], posh[0:r, n, :], colh[0:r, n, :], start=n == 0, stop=n == 2 * TILES - 1)
            i.then_inc(tab_mm, 1)

            def pair(G, q, halves, rows_in, weights_in):
                pe.wait_ge(xg_in[q], rows_in)
                pe.wait_ge(xgT_sb, FIRST + G)
                for c in range(KT):
                    l = pe.transpose(ps[:, c // 4, (c % 4) * P:(c % 4 + 1) * P], xg[:, q, c * P:(c + 1) * P], ident[:])
                l.then_inc(xgT_mm, 1)
                pe.wait_ge(xgT_sb, FIRST + G + 1)
                for s in halves:
                    pe.wait_ge(slot_in[2 * q + s], weights_in)
                pe.wait_ge(hm_ready, FIRST + G)
                for c in range(KT):
                    for s in halves:
                        l = pe.matmul(ps[CAP * s:CAP * s + CAP, 2, :], xgT[:, q, c, CAP * s:CAP * s + CAP],
                                      wslot[2 * q + s][:, c * 512:(c + 1) * 512], start=c == 0, stop=c == KT - 1,
                                      tile_position=(0, CAP * s), skip_group_check=True)
                l.then_inc(gu_mm, 1)
                pe.wait_ge(hm_ready, FIRST + G + 1)
                pe.wait_ge(hT_sb, FIRST + G)
                for f in range(2):
                    l = pe.transpose(ps[:, 3, f * P:(f + 1) * P], hm[:, q, f * P:(f + 1) * P], ident[:])
                l.then_inc(hT_mm, 1)
                pe.wait_ge(hT_sb, FIRST + G + 1)
                for s in halves:
                    pe.wait_ge(down_in[2 * q + s], weights_in)
                pe.wait_ge(yo_sb, FIRST + G)
                for f in range(2):
                    for h in range(2):
                        for s in halves:
                            o = KT * 512 + f * D + h * 512
                            l = pe.matmul(ps[CAP * s:CAP * s + CAP, 6 + h, :], hT[:, q, f, CAP * s:CAP * s + CAP],
                                          wslot[2 * q + s][:, o:o + 512], start=f == 0, stop=f == 1,
                                          tile_position=(0, CAP * s), skip_group_check=True)
                l.then_inc(pair_mm, 1)

            with pe.Fori(0, PAIRS // 2) as i:
                for q in range(2):
                    pair(i * 2 + q, q, (0, 1), (i + 1) * 16, (i + 1) * 16)
            pe.wait_ge(extra_ready, 1)
            nx = pe.value_load(nxi[0:1, 0:1], min_val=0, max_val=EXTRA)
            with pe.If(nx > 0):
                with pe.Fori(0, nx) as m:
                    have = m * 16 + (PAIRS // 2 + 1) * 16
                    pair(m + PAIRS, 0, (0,), have, have)


_INS = ["x", "wmix", "wgate", "chan", "wst", "bs", "rows", "wr", "br", "wmoe"]
_OUTS = [("y", (TA, D)), ("vp", (P, D)), ("vs", (S, D)), ("st", (P, KT, OUTC))]


def lay_out(np, i):
    f = lambda n: np.asarray(i[n])
    cat = np.concatenate
    x = cat([f("x_prompt").reshape(SEQ, D), f("x_sample").reshape(S, D)])
    w_in = f("w_in")[0].reshape(KT, P, 5, D)

    def token_units(w):
        return w.reshape(4, 2, P, 2, 512).transpose(3, 0, 2, 1, 4).reshape(8, P, KT, P)

    order = [2, 0, 3, 4]
    jw = w_in[:, :, order, :].reshape(KT, P, 4, KT, P).transpose(3, 2, 1, 0, 4).reshape(UNITS_J, P, KT, P)
    wmix = cat([token_units(w_in[:, :, 1, :]), jw, token_units(f("w_out")[0].reshape(KT, P, D))])
    wgate = np.stack([f("w_rg_a")[0], f("w_rg_x")[0]], axis=2)
    per = lambda a: a.reshape(-1, KT, P).transpose(2, 1, 0)
    chan = cat([per(f("norm1")[0]), per(f("conv_w")[0]), per(f("conv_b")[0]), per(f("lru_lambda")[0]),
                per(f("b_rg_a")[0].reshape(-1)), per(f("b_rg_x")[0].reshape(-1)), per(f("state_lru_h")[0]),
                per(f("state_conv")[0].reshape(-1, D)),
                per(f("norm2")[0])], axis=2)
    wst = f("w_s")[0].transpose(2, 0, 1)
    bs = f("b_s")[0].reshape(1, HEADS * P)
    rows = np.stack([f("ln_g")[0], f("ln_b")[0], f("norm_f")])
    wr = cat([f("w_route_group")[0], f("w_route_expert")[0]], axis=1).reshape(KT, P, NL).transpose(1, 0, 2)
    br = cat([f("b_route_group")[0], f("b_route_expert")[0]]).reshape(1, NL)
    gu = cat([f("w_gate")[0], f("w_up")[0]], axis=2).reshape(NE, KT, P, 512).transpose(0, 2, 1, 3).reshape(NE, P, KT * 512)
    wd = f("w_down")[0].reshape(NE, 2, P, D).transpose(0, 2, 1, 3).reshape(NE, P, 2 * D)
    wmoe = cat([gu, wd], axis=2)
    return dict(x=x, wmix=wmix, wgate=wgate, chan=chan, wst=wst, bs=bs, rows=rows, wr=wr, br=br, wmoe=wmoe)


def kernel(**inputs):
    import numpy as _np
    import concourse.bacc as _bacc
    from concourse.bass_utils import run_bass_kernel_spmd as _run

    nc = _bacc.Bacc("TRN2", target_bir_lowering=False, num_devices=1)
    laid = lay_out(_np, inputs)
    arrays, args = {}, []
    for name in _INS:
        a = _np.ascontiguousarray(laid[name])
        arrays[f"in_{name}"] = a
        args.append(nc.dram_tensor(f"in_{name}", a.shape, mybir.dt.from_np(a.dtype), kind="ExternalInput").ap())
    for name, shape in _OUTS:
        args.append(nc.dram_tensor(f"out_{name}", shape, F32, kind="ExternalOutput").ap())
    build(nc, *args)
    r = _run(nc, [arrays], core_ids=[0])
    y, vp, vs, st = (_np.asarray(r.results[0][f"out_{n}"]) for n, _ in _OUTS)
    st = st.transpose(2, 1, 0).reshape(OUTC, D)
    return (y[:SEQ].reshape(1, SEQ, D), y[SEQ:].reshape(DB, DS, D),
            st[0].reshape(1, 1, D), st[9:12].reshape(1, 1, 3, D), vp.reshape(1, 1, P, D),
            st[1:9].reshape(1, DB, D), st[12:36].reshape(1, DB, 3, D), vs.reshape(1, DB, DS, D))
```

```python
from contextlib import ExitStack

import concourse.bass as bass
from concourse import mybir

P = 128
D = 1024
KT = D // P
SEQ = 512
NT = SEQ // P
DB, DS = 8, 4
S = DB * DS
TA = SEQ + S
TILES = NT + 1
HEADS = 4
TAPS = 4
NG, EG = 4, 8
NE = NG * EG
NL = NG + NE
LG = 64
FE = 256
CAP = 64
PAIRS = NE // 2
MAXCHUNK = -(-TA // CAP)
EXTRA = 2 * TA // CAP
COLS = PAIRS + EXTRA
EPS = 1e-6
UNITS_V, UNITS_J, UNITS_O = 8, 32, 8
RAW = 4
OUTC = 36
(C_G1, C_W0, C_CB, C_LAM, C_BA, C_BX, C_H0, C_ST, C_G2, C_LG, C_LB) = (0, 1, 5, 6, 7, 8, 9, 17, 41, 42, 43)
NCH = 44
OUT_OF_RANGE = 8192.0
MASKED = 1e30
FIRST = 1

F32 = mybir.dt.float32
F32R = mybir.dt.float32r
BF16 = mybir.dt.bfloat16
I32 = mybir.dt.int32
U32 = mybir.dt.uint32
ALU = mybir.AluOpType
ACT = mybir.ActivationFunctionType
AX = mybir.AxisListType.X

GELU_K = 0.7978845608028654
GELU_C = 0.044715


class Steps:

    def __init__(self, eng, sem):
        self.eng, self.sem, self.base, self.n = eng, sem, 0, 0

    def then(self, ins):
        self.n += 1
        ins.then_inc(self.sem, 1)
        self.eng.wait_ge(self.sem, self.base + self.n)

    def mark(self, ins):
        self.n += 1
        ins.then_inc(self.sem, 1)
        return self.base + self.n

    def upto(self, count):
        self.eng.wait_ge(self.sem, count)

    def enter(self, i, per):
        self.start, self.per = self.base + self.n, per
        self.base, self.n = self.start + i * per, 0

    def leave(self, times):
        assert self.n == self.per, (self.n, self.per)
        self.base, self.n = self.start + times * self.per, 0


def build(nc, x, wmix, wgate, chan, wst, bs, rows, wr, br, wmoe, y, vp, vs, st):
    xnd = nc.dram_tensor("xnd", (TA, D), F32, kind="Internal").ap()
    ytok = nc.dram_tensor("ytok", (2 * TA, D), F32, kind="Internal").ap()

    def at(name, offset, shape, dt=F32):
        return nc.alloc_sbuf_tensor_at(name, shape, dt, offset=BASE + offset)

    K = 1024
    BASE = -(-nc.sbuf_base // 64) * 64
    GU = KT * 512
    EW = GU + 2 * D
    wslot = [[at(f"wslot{q}{s}", (first + s * 24) * K, [P, EW]) for s in range(2)]
             for q, first in enumerate((0, 97, 48))]
    xh = at("xh", 48 * K, [P, KT, SEQ], F32R)
    xl = at("xl", 64 * K, [P, KT, SEQ], F32R)
    zT = at("zT", 80 * K, [P, KT, TA])
    R_V = 161 * K
    v = at("v", 0, [P, TILES, D])
    x1 = at("x1", R_V, [P, TILES, D])
    tw = TA * 4
    XRW = 3 + SEQ + DB * 7
    (XC, A, TR, TI, M, U, U1, GA) = [at(n, R_V + i * tw, [P, TA]) for i, n in
                                     enumerate(("xc", "a", "tr", "ti", "m", "u", "u1", "ga"))]
    XR = at("xr", R_V + 8 * tw, [P, XRW])
    R_M = 97 * K
    mh = at("mh", R_M, [P, KT, SEQ], F32R)
    ml = at("ml", R_M + 16 * K, [P, KT, SEQ], F32R)
    xt = at("xt", R_M, [P, TILES, D])
    lng = at("lng", R_M + 20 * K, [P, D])
    lnb = at("lnb", R_M + 24 * K, [P, D])
    g1r = at("g1r", 80 * K, [P, D])
    junk = at("junk", R_M + 28 * K, [P, D])
    bterm = at("bterm", R_M + 28 * K, [P, KT, P])
    vo = at("vo", R_M, [P, 2, D])
    R_W = 129 * K
    raw = at("raw", R_W, [P, RAW, KT, P])
    wh = at("wh", R_W + 16 * K, [P, 2, D], F32R)
    wl = at("wl", R_W + 24 * K, [P, 2, D], F32R)
    xn2T = at("xn2T", 72 * K, [P, KT, TA])
    junk2 = at("junk2", 89 * K, [P, 512])
    xn2 = at("xn2", 121 * K, [P, TILES, D])
    gy = at("gy", 48 * K, [P, 2, TILES, D])
    nf = at("nf", 88 * K, [P, D])
    junk3 = at("junk3", 92 * K, [P, D])
    R_E = R_W + 16 * K
    xg = at("xg", R_E, [P, D])
    xgT = at("xgT", R_E + 4 * K, [P, KT, P])
    yo = at("yo", R_E + 8 * K, [P, D])
    hs = at("hs", R_E + 12 * K, [P, FE])
    hm = at("hm", R_E + 13 * K, [P, FE])
    hT = at("hT", R_E + 14 * K, [P, 2, P])
    posh = at("posh", R_E + 4 * K, [P, 2 * TILES, P], BF16)
    colh = at("colh", R_E + 7 * K, [P, 2 * TILES, COLS], BF16)
    toks = at("toks", R_E + 8 * K, [P, 2, 2 * TILES, COLS], BF16)
    cmp_ = at("cmp", R_E + 10 * K, [P, 2 * TILES * NE])
    pick2 = at("pick2", R_E + 14 * K + 512, [P, 2 * TILES * NE])
    key17 = at("key17", R_E + 12 * K, [1, EXTRA * NE])
    top = [181 * K]

    def small(name, shape, dt=F32):
        size = 4
        for n in shape[1:]:
            size *= n
        t = at(name, top[0], shape, dt)
        top[0] += -(-size // 32) * 32
        return t

    ch = small("ch", [P, KT, NCH])
    ident = small("ident", [P, P])
    ones = small("ones", [P, P], F32)
    upper = small("upper", [P, P], F32)
    fold = small("fold", [P, S])
    wsT = small("wsT", [P, HEADS, P])
    bdiag = small("bdiag", [S, HEADS, S])
    bsh = small("bsh", [P, HEADS, P])
    gw = small("gw", [P, 2, P])
    xs = small("xs", [P, KT, S])
    ms = small("ms", [P, KT, S])
    sp = small("sp", [P, 512])
    sq = small("sq", [P, 4, S])
    gbs = small("gbs", [P, S])
    so = small("so", [P, KT, OUTC])
    wrt = small("wrt", [P, KT, NL])
    brt = small("brt", [P, NL])
    ss = small("ss", [P, TILES])
    rstd = small("rstd", [P, TILES])
    ssa = small("ssa", [P, TILES])
    bnst = small("bnst", [P, TILES, 2, 6])
    bnag = small("bnag", [P, TILES, 2])
    csp = small("csp", [P, KT, 2])
    hb = small("hb", [P, KT, 2])
    hln = small("hln", [P, KT, 2])
    t8 = small("t8", [P, 5, KT])
    lgg = small("lgg", [P, TILES, NG])
    lge = small("lge", [P, TILES, NE])
    r4 = small("r4", [P, TILES, NG])
    oh = small("oh", [P, TILES, NG])
    r1 = small("r1", [P, 8, TILES])
    key = small("key", [P, TILES, NE])
    ohe = small("ohe", [P, 2, TILES, NE])
    mcnt = small("mcnt", [P, TILES, NE], BF16)
    cum = small("cum", [P, TILES + 1, NE], BF16)
    onesb = small("onesb", [P, P], BF16)
    upperb = small("upperb", [P, P], BF16)
    tokp = small("tokp", [P, 2, 2 * TILES], BF16)
    fold2 = small("fold2", [P, NL])
    lgT = small("lgT", [LG + NL, TA])
    first = small("first", [P, NE])
    iota = small("iota", [P, P])
    epair = small("epair", [P, NE])
    ehalf = small("ehalf", [P, NE])
    tokv = small("tokv", [P, 2, TILES])
    gate = small("gate", [P, 2, TILES])
    T2 = 2 * TILES
    (rk, chk, epr, ehf, ebx, isx, colv, posv) = [small(n, [P, T2]) for n in
                                                 ("rk", "chk", "epr", "ehf", "ebx", "isx", "colv", "posv")]
    is0 = small("is0", [P, T2])
    caps = small("caps", [P, MAXCHUNK - 1])
    xcnt = small("xcnt", [P, 3, NE])
    tab = small("tab", [P, 3, COLS])
    idxg = small("idxg", [P, COLS], U32)
    idxy = small("idxy", [P, COLS], U32)
    colg = small("colg", [P, 1], U32)
    coly = small("coly", [P, 1], U32)
    nxi = small("nxi", [1, 1 + EXTRA], I32)
    assert BASE + top[0] <= nc.sbuf_usable_end, top[0] / K

    with ExitStack() as ctx:
        ps = ctx.enter_context(nc.psum_tensor("ps", [P, 8, 512], F32))

        def sem(name):
            return ctx.enter_context(nc.semaphore(name))

        x_in = [sem(f"x_in{t}") for t in range(TILES)]
        g1_in = sem("g1_in")
        const_in = sem("const_in")
        raw_in = [sem(f"raw_in{s}") for s in range(RAW)]
        part_in = [[[sem(f"part{n}_in{q}{s}") for s in range(2)] for q in range(3)] for n in range(3)]
        gw_in = sem("gw_in")
        xres_in = sem("xres_in")
        bd_in = sem("bd_in")
        masks = sem("masks")
        xg_zero = sem("xg_zero")
        xn_stored = sem("xn_stored")
        xg_in = sem("xg_in")
        y_out = sem("y_out")
        yo_free = sem("yo_free")
        back_in = [sem(f"back_in{n}") for n in range(TILES)]
        rs_mm = sem("rs_mm")
        bt_ready = sem("bt_ready")
        vo_ready = sem("vo_ready")
        v_stored = sem("v_stored")
        done_out = sem("done_out")

        held = sem("held")
        act_s = sem("act_s")
        dve_s = sem("dve_s")
        pool_s = sem("pool_s")

        ss_ready = sem("ss_ready")
        ms_ready = sem("ms_ready")
        sq_ready = sem("sq_ready")
        xn_ready = sem("xn_ready")
        xT_ready = sem("xT_ready")
        xh_ready = sem("xh_ready")
        xl_ready = sem("xl_ready")
        xs_ready = sem("xs_ready")
        hi_ready = sem("hi_ready")
        lo_ready = sem("lo_ready")
        unit_done = sem("unit_done")
        vsum = sem("vsum")
        vfold = sem("vfold")
        v_gelu = sem("v_gelu")
        v_ready = sem("v_ready")
        z_mm = sem("z_mm")
        z_ready = sem("z_ready")
        sproj = sem("sproj")
        sproj_sb = sem("sproj_sb")
        sproj_T = sem("sproj_T")
        sq_sb = sem("sq_sb")
        xr_ev = sem("xr_ev")
        u_ev = sem("u_ev")
        ga_ev = sem("ga_ev")
        gb_ev = sem("gb_ev")
        u_sq = sem("u_sq")
        u_poly = sem("u_poly")
        u_tanh = sem("u_tanh")
        u_free = sem("u_free")
        conv_done = sem("conv_done")
        gates_mm = sem("gates_mm")
        gates_ev = sem("gates_ev")
        a_ready = sem("a_ready")
        m_poly = sem("m_poly")
        m_sqrt = sem("m_sqrt")
        ya_done = sem("ya_done")
        merged = sem("merged")
        x1_ready = sem("x1_ready")
        n2_ms = sem("n2_ms")
        n2_sq = sem("n2_sq")
        xn2_ready = sem("xn2_ready")
        xn2T_mm = sem("xn2T_mm")
        xn2T_sb = [sem("xn2T_even"), sem("xn2T_odd")]
        lg_mm = sem("lg_mm")
        lg_sb = sem("lg_sb")
        lgt_mm = sem("lgt_mm")
        ex_in = sem("ex_in")
        ex_out = sem("ex_out")
        cnt_in = sem("cnt_in")
        rank_mm = sem("rank_mm")
        pos_ready = sem("pos_ready")
        tab_mm = sem("tab_mm")
        tab_ready = sem("tab_ready")
        extra_ready = sem("extra_ready")
        colg_copied = sem("colg_copied")
        coly_copied = sem("coly_copied")
        xgT_mm = sem("xgT_mm")
        xgT_sb = sem("xgT_sb")
        gu_half = sem("gu_half")
        gu_mm = sem("gu_mm")
        silu_done = sem("silu_done")
        hm_ready = sem("hm_ready")
        hT_mm = sem("hT_mm")
        hT_sb = sem("hT_sb")
        pair_mm = sem("pair_mm")
        yo_sb = sem("yo_sb")
        comb = sem("comb")
        fin_ms = sem("fin_ms")
        fin_sq = sem("fin_sq")
        fin_ready = sem("fin_ready")
        so_ready = sem("so_ready")

        block = ctx.enter_context(nc.Block())

        def rowsof(t):
            return S if t == NT else P

        xp_tiles = [x[t * P:t * P + rowsof(t), :] for t in range(TILES)]
        y_tiles = [y[t * P:t * P + rowsof(t), :] for t in range(TILES)]
        NCONST = 16 * 8

        def v_banks(half):
            return ([0, 1, 2, 3], 4, 6) if half == 0 else ([5, 7, 0, 1], 2, 3)

        def o_banks(half):
            return ([0, 1, 2, 5], 6, 4) if half == 0 else ([7, 3, 0, 1], 2, 2)

        TB = (5, 7, 4, 6, 5, 7, 4, 6)
        PARTS = ((0, GU // 2), (GU // 2, GU), (GU, EW))
        ZB = (4, 5, 2, 3)
        XB = (4, 6, 4, 6, 4, 6, 7, 3)

        @block.sync
        def _(sp_):
            e = sp_
            def tile_in(t):
                e.dma_start(xt[0:rowsof(t), t, :], xp_tiles[t]).then_inc(x_in[t], 16)

            def unit_in(n):
                e.dma_start(raw[:, n, :, :], wmix[n]).then_inc(raw_in[n], 16)

            tile_in(0)
            e.dma_start(g1r[:], rows[3:4, :].broadcast_to([P, D])).then_inc(g1_in, 16)
            tile_in(1)
            unit_in(0)
            for t in range(2, TILES):
                tile_in(t)
            e.dma_start(ch[:], chan).then_inc(const_in, 16)
            for n in range(1, 4):
                unit_in(n)
            e.dma_start(lng[:], rows[0:1, :].broadcast_to([P, D])).then_inc(const_in, 16)
            e.dma_start(lnb[:], rows[1:2, :].broadcast_to([P, D])).then_inc(const_in, 16)
            e.dma_start(wsT[:], wst).then_inc(const_in, 16)
            e.dma_start(bsh[:], bs.broadcast_to([P, HEADS * P]).rearrange("p (h t) -> p h t", h=HEADS)).then_inc(const_in, 16)
            e.dma_start(wrt[:], wr).then_inc(const_in, 16)
            e.dma_start(brt[:], br.broadcast_to([P, NL])).then_inc(const_in, 16)
            e.wait_ge(masks, 1)
            for b in range(DB):
                e.dma_start(bdiag[4 * b:4 * b + 4, :, 4 * b:4 * b + 4],
                            wst[0:4, :, 0:4]).then_inc(bd_in, 16)
            for n in range(4, 12):
                e.wait_ge(lo_ready, n - 3)
                e.wait_ge(unit_done, n - 3)
                e.dma_start(raw[:, n % RAW, :, :], wmix[n]).then_inc(raw_in[n % RAW], 16)
            def expert(q, s, n):
                for part, (lo, hi) in enumerate(PARTS):
                    e.dma_start(wslot[q][s][:, lo:hi], wmoe[n][:, lo:hi]).then_inc(part_in[part][q][s], 16)

            def next_units(j):
                for p in range(4):
                    e.wait_ge(lo_ready, j * 4 + (8 + p + 1))
                    e.sem_inc(held, 1)
                    e.wait_ge(sproj, j + 1)
                    e.sem_inc(held, 1)
                    e.dma_start(raw[:, p, :, :], wmix[bass.ds(j * 4 + (12 + p), 1)].rearrange("a p k c -> (a p) k c")).then_inc(raw_in[p], 16)

            next_units(0)
            e.wait_ge(z_mm, KT + 1)
            e.wait_ge(vo_ready, 2)
            expert(0, 0, 0)
            expert(0, 1, 1)
            with e.Fori(1, KT) as j:
                next_units(j)
            e.wait_ge(merged, FIRST + KT)
            for t in range(TILES):
                e.dma_start(x1[0:rowsof(t), t, :], xp_tiles[t]).then_inc(xres_in, 16)
            for n in range(44, 48):
                e.wait_ge(lo_ready, n - 3)
                e.wait_ge(unit_done, n - 3)
                e.dma_start(raw[:, n % RAW, :, :], wmix[n]).then_inc(raw_in[n % RAW], 16)
                if n == 45:
                    expert(2, 0, 4)
            e.wait_ge(unit_done, 48)
            expert(1, 0, 2)
            e.wait_ge(lg_mm, 1)
            expert(2, 1, 5)
            e.wait_ge(xn_stored, 16 * TILES)
            e.wait_ge(xg_in, 16)
            expert(1, 1, 3)

            def refill(q, count, number, before, landed):
                for part, used in enumerate((gu_half, gu_mm, pair_mm)):
                    last, reached = (part_in[part - 1][q], landed[1]) if part else (part_in[2][before], landed[0])
                    lo, hi = PARTS[part]
                    e.wait_ge(used, count)
                    e.sem_inc(held, 1)
                    for s in range(2):
                        e.wait_ge(last[s], reached)
                        e.sem_inc(held, 1)
                        e.dma_start(wslot[q][s][:, lo:hi], wmoe[bass.ds(number + s, 1), :, lo:hi].rearrange(
                            "a p c -> (a p) c")).then_inc(part_in[part][q][s], 16)

            with e.Fori(0, 4) as i:
                for q in range(3):
                    refill(q, i * 3 + (q + 1), i * 6 + (6 + 2 * q), (q - 1) % 3,
                           (i * 16 + (16 if q == 0 else 32), i * 16 + 32))
            refill(0, PAIRS - 3, NE - 2, 2, (16 * 5, 16 * 6))
            e.wait_ge(extra_ready, 1)
            nx = e.value_load(nxi[0:1, 0:1], min_val=0, max_val=EXTRA)

            def further(count, m):
                ex = e.value_load(nxi[0:1, bass.ds(m + 1, 1)], min_val=0, max_val=NE - 1)
                for part, used in enumerate((gu_half, gu_mm, pair_mm)):
                    lo, hi = PARTS[part]
                    e.wait_ge(used, count)
                    e.sem_inc(held, 1)
                    e.dma_start(wslot[1][0][:, lo:hi], wmoe[bass.ds(ex, 1), :, lo:hi].rearrange(
                        "a p c -> (a p) c")).then_inc(part_in[part][1][0], 16)

            with e.If(nx > 0):
                e.wait_ge(part_in[2][0][0], 16 * 6)
                further(PAIRS - 2, 0)
                with e.If(nx > 1):
                    with e.Fori(1, nx) as m:
                        further(m + PAIRS, m)
            e.wait_ge(pair_mm, PAIRS - 1)
            e.dma_start(nf[:], rows[2:3, :].broadcast_to([P, D])).then_inc(const_in, 16)
            e.wait_ge(yo_free, FIRST + nx + PAIRS)
            e.sem_inc(held, 1)
            for t in range(TILES):
                r = rowsof(t)
                for s in range(2):
                    e.dma_start(gy[0:r, s, t, :], ytok[s * TA + t * P:s * TA + t * P + r, :]).then_inc(back_in[t], 16)
            for t in range(TILES):
                e.wait_ge(fin_ready, t + 1)
                e.dma_start(y_tiles[t], xn2[0:rowsof(t), t, :]).then_inc(done_out, 16)
            e.wait_ge(v_stored, 32)
            e.wait_ge(done_out, 16 * (TILES + 1))

        @block.gpsimd
        def _(g):
            own = Steps(g, pool_s)
            g.memset(bdiag[:], 0.0).then_inc(masks, 1)
            own.then(g.memset(ident[:], 0.0))
            g.affine_select(out=ident[:], in_=ident[:], compare_op=ALU.not_equal, fill=1.0, base=0,
                            pattern=[[-1, P]], channel_multiplier=1).then_inc(masks, 1)
            own.then(g.memset(fold[:], 0.0))
            for q in range(4):
                i = g.affine_select(out=fold[:], in_=fold[:], compare_op=ALU.not_equal, fill=1.0,
                                    base=-S * q, pattern=[[-1, S]], channel_multiplier=1)
                if q < 3:
                    own.then(i)
            i.then_inc(masks, 1)
            g.memset(ones[:], 1.0).then_inc(masks, 1)
            own.then(g.memset(upper[:], 1.0))
            g.affine_select(out=upper[:], in_=upper[:], compare_op=ALU.is_gt, fill=0.0, base=0,
                            pattern=[[1, P]], channel_multiplier=-1).then_inc(masks, 1)
            own.then(g.memset(fold2[:], 0.0))
            own.then(g.affine_select(out=fold2[:], in_=fold2[:], compare_op=ALU.not_equal, fill=1.0, base=0,
                                     pattern=[[-1, NL]], channel_multiplier=1))
            own.then(g.affine_select(out=fold2[:], in_=fold2[:], compare_op=ALU.not_equal, fill=1.0, base=-LG,
                                     pattern=[[-1, NL]], channel_multiplier=1))
            g.wait_ge(const_in, NCONST - 16)
            g.affine_select(out=wsT[:], in_=wsT[:], compare_op=ALU.is_ge, fill=0.0, base=0,
                            pattern=[[0, HEADS], [1, P]], channel_multiplier=-1).then_inc(masks, 1)
            g.wait_ge(bd_in, 16 * DB)
            g.affine_select(out=bdiag[:], in_=bdiag[:], compare_op=ALU.is_ge, fill=0.0, base=0,
                            pattern=[[0, HEADS], [1, S]], channel_multiplier=-1).then_inc(masks, 1)
            for n in range(NE):
                g.memset(first[:, n:n + 1], float(NE - n))
            own.then(g.memset(ehalf[:], 0.0))
            g.memset(ehalf[:].rearrange("p (e a) -> p e a", a=2)[:, :, 1:2], float(CAP)).then_inc(masks, 1)
            g.wait_ge(v_ready, 1 + TILES)
            g.wait_ge(const_in, NCONST - 16)
            g.tensor_tensor(vo[:, 0, :], v[:, NT - 1, :], lng[:], ALU.mult).then_inc(vo_ready, 1)
            g.tensor_tensor(vo[0:S, 1, :], v[0:S, NT, :], lng[0:S, :], ALU.mult).then_inc(vo_ready, 1)
            g.wait_ge(vo_ready, 2)
            g.tensor_tensor(vo[:, 0, :], vo[:, 0, :], lnb[:], ALU.add).then_inc(vo_ready, 1)
            g.tensor_tensor(vo[0:S, 1, :], vo[0:S, 1, :], lnb[0:S, :], ALU.add).then_inc(vo_ready, 1)
            g.wait_ge(vo_ready, 4)
            g.dma_start(vp, vo[:, 0, :]).then_inc(v_stored, 16)
            g.dma_start(vs, vo[0:S, 1, :]).then_inc(v_stored, 16)
            with g.Fori(0, KT) as j:
                g.wait_ge(gates_mm, FIRST + j)
                g.dma_start(gw[:], wgate[bass.ds(j, 1)].rearrange("a p w c -> (a p) w c")).then_inc(gw_in, 16)
            g.wait_ge(unit_done, 48)
            g.memset(xg[:], 0.0).then_inc(xg_zero, 1)
            g.wait_ge(xn_stored, 16 * TILES)
            g.wait_ge(tab_ready, 1)
            g.wait_ge(xg_zero, 1)

            def gather(column, count):
                g.tensor_copy(colg[:], idxg[:, column]).then_inc(colg_copied, 1)
                g.wait_ge(colg_copied, count)
                g.sem_inc(held, 1)
                g.indirect_dma_start(
                    out=xg[:, :], out_offset=None, in_=xnd,
                    in_offset=bass.IndirectOffsetOnAxis(ap=colg[:, 0:1], axis=0),
                    bounds_check=TA - 1, oob_is_err=False).then_inc(xg_in, 16)

            def scatter(column, count, total):
                g.tensor_copy(coly[:], idxy[:, column]).then_inc(coly_copied, 1)
                g.wait_ge(coly_copied, count)
                g.sem_inc(held, 1)
                g.indirect_dma_start(
                    out=ytok, out_offset=bass.IndirectOffsetOnAxis(ap=coly[:, 0:1], axis=0),
                    in_=yo[:, :], in_offset=None, bounds_check=2 * TA - 1, oob_is_err=False).then_inc(y_out, 16)
                g.wait_ge(y_out, total)
                g.sem_inc(yo_free, 1)

            g.wait_ge(extra_ready, 1)
            nx = g.value_load(nxi[0:1, 0:1], min_val=0, max_val=EXTRA)
            gather(slice(0, 1), 1)
            g.wait_ge(xgT_mm, FIRST + 1)
            gather(slice(1, 2), 2)
            with g.Fori(0, nx + (PAIRS - 2)) as G:
                g.wait_ge(xgT_mm, FIRST + G + 2)
                g.sem_inc(held, 1)
                gather(bass.ds(G + 2, 1), G + 3)
                g.wait_ge(yo_sb, FIRST + G + 1)
                g.sem_inc(held, 1)
                scatter(bass.ds(G, 1), G + 1, G * 16 + 16)
            for n in (2, 1):
                last = nx + (PAIRS - n)
                g.wait_ge(yo_sb, FIRST + last + 1)
                g.sem_inc(held, 1)
                scatter(bass.ds(last, 1), last + 1, last * 16 + 16)

        @block.scalar
        def _(a):
            own = Steps(a, act_s)
            for first_one in (sproj_sb, xr_ev, u_ev, ga_ev, gates_ev, yo_sb, yo_free, hT_sb):
                a.sem_inc(first_one, FIRST)

            def split_hi(n, slot, hslot, count):
                a.wait_ge(raw_in[slot], count)
                if n is not None and n >= 2:
                    a.wait_ge(unit_done, n - 1)
                a.activation(wh[:, hslot, :], raw[:, slot, :, :].rearrange("p k c -> p (k c)"),
                             ACT.Copy).then_inc(hi_ready, 1)

            a.wait_ge(ss_ready, 1)
            own.then(a.activation(rstd[:], ss[:], ACT.Sqrt))
            def x_hi(t):
                for b in range(2):
                    a.wait_ge(xT_ready, 2 * t + b + 1)
                    a.activation(xh[:, 4 * b:4 * b + 4, t * P:(t + 1) * P],
                                 ps[:, TB[2 * t + b], :].rearrange("p (k c) -> p k c", k=4), ACT.Copy).then_inc(xh_ready, 1)

            for t in range(TILES):
                r = rowsof(t)
                a.wait_ge(x_in[t], 16)
                a.activation(junk[0:r, :], xt[0:r, t, :], ACT.Square, accum_out=ss[0:r, t:t + 1]).then_inc(sq_ready, 1)
                a.wait_ge(sq_ready, 2 * t + 1)
                a.wait_ge(ms_ready, t + 1)
                a.activation(rstd[0:r, t:t + 1], ss[0:r, t:t + 1], ACT.Sqrt).then_inc(sq_ready, 1)
                if t == 1:
                    split_hi(0, 0, 0, 16)
                if t:
                    x_hi(t - 1)
            split_hi(1, 1, 1, 16)
            a.wait_ge(v_ready, 1)
            a.activation(t8[:, 1, :], t8[:, 0, :], ACT.Exp, scale=-1.0).then_inc(ex_out, 1)
            for half in range(2):
                banks, sbank, fbank = v_banks(half)
                c = slice(half * 512, half * 512 + 512)
                for u in range(4):
                    n = half * 4 + u
                    a.wait_ge(unit_done, n + 1)
                    split_hi(n + 2, (n + 2) % RAW, n % 2, 16 * ((n + 2) // RAW + 1))
                    if n == 4:
                        a.wait_ge(vfold, 1)
                        a.activation(v[0:S, NT, 0:512], ps[0:S, v_banks(0)[2], :], ACT.Gelu_apprx_tanh).then_inc(v_gelu, 1)
                a.activation(sp[:], ps[:, sbank, :], ACT.Copy).then_inc(vsum, 1)
                for t in range(NT):
                    a.activation(v[:, t, c], ps[:, banks[t], :], ACT.Gelu_apprx_tanh).then_inc(v_gelu, 1)
            a.wait_ge(vfold, 2)
            a.activation(v[0:S, NT, 512:1024], ps[0:S, v_banks(1)[2], :], ACT.Gelu_apprx_tanh).then_inc(v_gelu, 1)
            a.wait_ge(ms_ready, TILES + 1)
            a.activation(rstd[:], ss[:], ACT.Sqrt).then_inc(sq_ready, 1)

            with a.Fori(0, KT) as j:
                smp = lambda t: t[:, SEQ:TA]
                def raw_count(extra):
                    return j * 16 + 16 * (2 + extra + 1)
                a.wait_ge(sproj, j + 1)
                a.wait_ge(sproj_T, FIRST + j)
                a.activation(sp[:], ps[:, 6, :], ACT.Copy).then_inc(sproj_sb, 1)
                a.wait_ge(unit_done, j * 4 + 9)
                split_hi(None, 2, 0, raw_count(0))
                a.wait_ge(conv_done, FIRST + j)
                a.activation(XR[:, 3:3 + SEQ], ps[:, 0, :], ACT.Copy).then_inc(xr_ev, 1)
                a.wait_ge(sproj_T, FIRST + j + 1)
                a.activation(sq[:].rearrange("p u s -> p (u s)"), ps[:, 7, 0:4 * S], ACT.Copy).then_inc(sq_sb, 1)
                a.wait_ge(sq_sb, j + 1)
                a.activation(XR[:, 3 + SEQ:XRW].rearrange("p (b s) -> p b s", b=DB)[:, :, 3:7],
                             sq[:, 0, :].rearrange("p (b s) -> p b s", b=DB), ACT.Copy).then_inc(xr_ev, 1)
                a.wait_ge(unit_done, j * 4 + 10)
                split_hi(None, 3, 1, raw_count(0))
                a.wait_ge(ya_done, FIRST + j)
                a.activation(U[:, 0:SEQ], ps[:, 1, :], ACT.Copy).then_inc(u_ev, 1)
                a.activation(smp(U), sq[:, 1, :], ACT.Copy).then_inc(u_ev, 1)
                a.wait_ge(u_ev, FIRST + j * 2 + 2)
                a.activation(U1[:], U[:], ACT.Square).then_inc(u_sq, 1)
                a.wait_ge(unit_done, j * 4 + 11)
                split_hi(None, 0, 0, raw_count(1))
                a.wait_ge(merged, FIRST + j)
                a.activation(GA[:, 0:SEQ], ps[:, 2, :], ACT.Tanh, scale=0.5).then_inc(ga_ev, 1)
                a.activation(smp(GA), sq[:, 2, :], ACT.Tanh, scale=0.5).then_inc(ga_ev, 1)
                a.wait_ge(u_poly, j + 1)
                a.activation(U1[:], U1[:], ACT.Tanh, scale=GELU_K).then_inc(u_tanh, 1)
                a.wait_ge(gates_mm, FIRST + j + 1)
                for w, T in ((0, TR), (1, TI)):
                    b = hb[:, bass.ds(j, 1), w]
                    a.activation(T[:, 0:SEQ], ps[:, 4 + w, :], ACT.Tanh, scale=0.5, bias=b).then_inc(gates_ev, 1)
                    a.activation(smp(T), ps[:, 7, (4 + w) * S:(5 + w) * S], ACT.Tanh, scale=0.5, bias=b).then_inc(gates_ev, 1)
                cp, cn = csp[:, bass.ds(j, 1), 0], csp[:, bass.ds(j, 1), 1]
                a.wait_ge(gates_ev, FIRST + j * 4 + 4)
                a.activation(A[:], TR[:], ACT.Exp, scale=cp, bias=cp).then_inc(a_ready, 1)
                a.activation(TR[:], TR[:], ACT.Tanh, scale=cn, bias=cn).then_inc(a_ready, 1)
                a.wait_ge(a_ready, j * 3 + 1)
                a.activation(M[:], A[:], ACT.Square).then_inc(a_ready, 1)
                a.wait_ge(unit_done, j * 4 + 12)
                split_hi(None, 1, 1, raw_count(1))
                a.activation(ps[:, 3, :], ps[:, 3, :], ACT.Tanh, scale=0.5).then_inc(gb_ev, 1)
                a.activation(gbs[:], sq[:, 3, :], ACT.Tanh, scale=0.5).then_inc(gb_ev, 1)
                a.wait_ge(m_poly, j + 1)
                a.activation(M[:], M[:], ACT.Sqrt).then_inc(m_sqrt, 1)

            def squares(h):
                for t in range(TILES):
                    r = rowsof(t)
                    a.wait_ge(x1_ready, h * TILES + t + 1)
                    if h * TILES + t:
                        a.wait_ge(n2_sq, h * TILES + t)
                    a.activation(junk2[0:r, 0:512], x1[0:r, t, h * 512:h * 512 + 512], ACT.Square,
                                 accum_out=(ssa, ss)[h][0:r, t:t + 1]).then_inc(n2_sq, 1)

            def x1T_copy(k):
                a.wait_ge(xn2T_mm, k + 1)
                a.activation(xn2T[:, k, 0:SEQ], ps[:, XB[k], :], ACT.Copy, scale=ch[:, k, C_G2:C_G2 + 1]).then_inc(xn2T_sb[0], 1)

            for half in range(2):
                banks, sbank, fbank = o_banks(half)
                for u in range(4):
                    n = UNITS_V + UNITS_J + half * 4 + u
                    a.wait_ge(unit_done, n + 1)
                    if n + 2 < 48:
                        split_hi(n + 2, (n + 2) % RAW, n % 2, 16 * ((n + 2) // RAW + 1))
                    if half and u == 1:
                        a.wait_ge(so_ready, 1)
                        squares(0)
                    if half and u == 2:
                        x1T_copy(0)
                    if half and u == 3:
                        x1T_copy(2)
                if half:
                    a.wait_ge(vfold, 3)
                a.activation(sp[:], ps[:, sbank, :], ACT.Copy).then_inc(vsum, 1)
            squares(1)
            a.wait_ge(n2_ms, 1)
            a.activation(rstd[:], ss[:], ACT.Sqrt).then_inc(n2_sq, 1)
            for k in (4, 6):
                x1T_copy(k)
            a.wait_ge(lg_mm, 1)
            a.activation(lgT[LG:LG + NL, 0:SEQ], ps[LG:LG + NL, 5, :], ACT.Copy).then_inc(lg_sb, 1)
            a.wait_ge(n2_ms, 2)
            for t in range(TILES):
                r = rowsof(t)
                a.activation(xn2[0:r, t, :], x1[0:r, t, :], ACT.Copy, scale=rstd[0:r, t:t + 1]).then_inc(xn2_ready, 1)
                a.wait_ge(xn2_ready, t + 1)
                a.dma_start(xnd[t * P:t * P + r, :], xn2[0:r, t, :]).then_inc(xn_stored, 16)
            a.wait_ge(ex_in, 1)
            a.activation(r4[:], r4[:], ACT.Exp).then_inc(ex_out, 1)
            a.wait_ge(ex_in, 2)
            a.activation(r1[:, 3, :], r1[:, 2, :], ACT.Exp).then_inc(ex_out, 1)

            a.wait_ge(extra_ready, 1)
            nx = a.value_load(nxi[0:1, 0:1], min_val=0, max_val=EXTRA)
            with a.Fori(0, nx + PAIRS) as G:
                a.wait_ge(gu_mm, G + 1)
                a.activation(hs[:], ps[:, 2, 0:FE], ACT.Silu).then_inc(silu_done, 1)
                a.wait_ge(hT_mm, G + 1)
                a.activation(hT[:].rearrange("p f c -> p (f c)"), ps[:, 3, 0:2 * P], ACT.Copy).then_inc(hT_sb, 1)
                a.wait_ge(pair_mm, G + 1)
                a.wait_ge(yo_free, FIRST + G)
                a.activation(yo[:], ps[:, 6:8, :].rearrange("p b c -> p (b c)"), ACT.Copy).then_inc(yo_sb, 1)
            a.dma_start(st, so[:]).then_inc(done_out, 16)
            for t in range(TILES):
                r = rowsof(t)
                a.wait_ge(comb, 2 * t + 2)
                a.wait_ge(n2_sq, 2 * TILES + 1 + t)
                a.activation(junk3[0:r, :], x1[0:r, t, :], ACT.Square, accum_out=ss[0:r, t:t + 1]).then_inc(n2_sq, 1)
                a.wait_ge(fin_ms, t + 1)
                a.activation(rstd[0:r, t:t + 1], ss[0:r, t:t + 1], ACT.Sqrt).then_inc(fin_sq, 1)

        @block.vector
        def _(d):
            own = Steps(d, dve_s)
            for first_one in (conv_done, ya_done, merged, xgT_sb, hm_ready):
                d.sem_inc(first_one, FIRST)

            def split_lo(hslot, slot, count):
                d.wait_ge(hi_ready, count)
                d.tensor_tensor(wl[:, hslot, :], raw[:, slot, :, :].rearrange("p k c -> p (k c)"),
                                wh[:, hslot, :].bitcast(F32), ALU.subtract).then_inc(lo_ready, 1)

            d.memset(ss[:], float(D)).then_inc(ss_ready, 1)
            def x_lo(t):
                for b in range(2):
                    d.wait_ge(xh_ready, 2 * t + b + 1)
                    part = slice(4 * b, 4 * b + 4), slice(t * P, t * P + P)
                    d.tensor_tensor(xl[:, part[0], part[1]], ps[:, TB[2 * t + b], :].rearrange("p (k c) -> p k c", k=4),
                                    xh[:, part[0], part[1]].bitcast(F32), ALU.subtract).then_inc(xl_ready, 1)

            d.wait_ge(g1_in, 16)
            for t in range(TILES):
                r = rowsof(t)
                d.wait_ge(sq_ready, 2 * t + 1)
                d.tensor_scalar(ss[0:r, t:t + 1], ss[0:r, t:t + 1], 1.0 / D, EPS, ALU.mult, ALU.add).then_inc(ms_ready, 1)
                d.wait_ge(sq_ready, 2 * t + 2)
                own.then(d.reciprocal(rstd[0:r, t:t + 1], rstd[0:r, t:t + 1]))
                d.scalar_tensor_tensor(out=xt[0:r, t, :], in0=xt[0:r, t, :], scalar=rstd[0:r, t:t + 1], in1=g1r[0:r, :],
                                       op0=ALU.mult, op1=ALU.mult).then_inc(xn_ready, 1)
                if t == 1:
                    split_lo(0, 0, 1)
                if t:
                    x_lo(t - 1)
            split_lo(1, 1, 2)
            d.wait_ge(xT_ready, 2 * NT + 1)
            d.tensor_copy(xs[:].rearrange("p k s -> p (k s)"), ps[:, 3, 0:KT * S]).then_inc(xs_ready, 1)
            d.wait_ge(const_in, NCONST - 16)
            own.then(d.tensor_scalar(hb[:], ch[:, :, C_BA:C_BA + 2], 0.5, None, ALU.mult))
            own.then(d.tensor_scalar(bsh[:], bsh[:], 0.5, None, ALU.mult))
            own.then(d.tensor_scalar(hln[:], ch[:, :, C_LG:C_LG + 2], 0.5, None, ALU.mult))
            lam = ch[:, :, C_LAM]
            d.scalar_tensor_tensor(out=t8[:, 0, :], in0=lam, scalar=-1.0, in1=lam, op0=ALU.mult, op1=ALU.max).then_inc(v_ready, 1)
            d.wait_ge(ex_out, 1)
            own.then(d.tensor_scalar(t8[:, 2, :], t8[:, 1, :], 2.0, None, ALU.add))
            own.then(d.reciprocal(t8[:, 2, :], t8[:, 2, :]))
            own.then(d.tensor_tensor(t8[:, 1, :], t8[:, 1, :], t8[:, 2, :], ALU.mult))
            own.then(d.tensor_tensor(t8[:, 2, :], t8[:, 1, :], t8[:, 1, :], ALU.mult))
            own.then(d.tensor_scalar(t8[:, 3, :], t8[:, 2, :], 1.0 / 17, 1.0 / 15, ALU.mult, ALU.add))
            for n in (13, 11, 9, 7, 5, 3, 1):
                own.then(d.tensor_tensor(t8[:, 3, :], t8[:, 3, :], t8[:, 2, :], ALU.mult))
                own.then(d.tensor_scalar(t8[:, 3, :], t8[:, 3, :], 1.0 / n, None, ALU.add))
            own.then(d.tensor_tensor(t8[:, 3, :], t8[:, 3, :], t8[:, 1, :], ALU.mult))
            own.then(d.tensor_scalar(t8[:, 4, :], lam, -1.0, 0.0, ALU.mult, ALU.max))
            own.then(d.scalar_tensor_tensor(out=t8[:, 3, :], in0=t8[:, 3, :], scalar=2.0, in1=t8[:, 4, :],
                                            op0=ALU.mult, op1=ALU.add))
            own.then(d.tensor_scalar(csp[:, :, 0], t8[:, 3, :], -4.0, None, ALU.mult))
            own.then(d.tensor_scalar(csp[:, :, 1], t8[:, 3, :], 4.0, None, ALU.mult))
            d.wait_ge(rs_mm, 1)
            for j in range(KT):
                h = j // 2
                d.scalar_tensor_tensor(out=bterm[:, j, :], in0=ps[:, 7, h * P:(h + 1) * P], scalar=hln[:, j, 1:2],
                                       in1=bsh[:, h, :], op0=ALU.mult, op1=ALU.add).then_inc(bt_ready, 1)
            def router_constants():
                d.wait_ge(masks, 8)
                own.then(d.tensor_tensor_scan(iota[:], ones[:], ones[:], 0.0, ALU.mult, ALU.add))
                own.then(d.tensor_scalar(iota[:], iota[:], -1.0, None, ALU.add))
                own.then(d.tensor_scalar(caps[:], iota[:, 1:MAXCHUNK], float(CAP), None, ALU.mult))
                own.then(d.reduce_sum(r1[:, 7, 0:1], upper[:], axis=AX))
                for s in range(2):
                    for t in range(TILES):
                        own.then(d.tensor_scalar(tokv[:, s, t:t + 1], r1[:, 7, 0:1], -1.0, float(P + s * TA + t * P), ALU.mult, ALU.add))
                own.then(d.tensor_copy(epair[:].rearrange("p (e a) -> p e a", a=2),
                                       iota[:, 0:PAIRS].rearrange("p (e a) -> p e a", a=1).broadcast_to([P, PAIRS, 2])))
                own.then(d.memset(cum[:, 0, :], 0.0))
                own.then(d.memset(mcnt[:], 0.0))
                own.then(d.memset(lgT[:], 0.0))
                d.tensor_copy(onesb[:], ones[:])
                own.then(d.tensor_copy(upperb[:], upper[:]))
                tv = tokv[:].rearrange("p s t -> p (s t)")
                own.then(d.tensor_copy(tokp[:, 0, :], tv))
                own.then(d.tensor_tensor(tokp[:, 1, :], tv, tokp[:, 0, :], ALU.subtract))
                d.memset(ssa[:], float(D) / 2).then_inc(so_ready, 1)

            own.then(d.memset(bnag[:], 1.0))
            for n in range(UNITS_V):
                split_lo(n % 2, (n + 2) % RAW, n + 3)
                if n == 4:
                    for t in range(TILES):
                        d.wait_ge(v_gelu, t + 1)
                        own.then(d.bn_stats(bnst[0:rowsof(t), t, 0, :], v[0:rowsof(t), t, 0:512]))
                if n == 5:
                    router_constants()
            for t in range(TILES):
                r = rowsof(t)
                d.wait_ge(v_gelu, TILES + t + 1)
                own.then(d.bn_stats(bnst[0:r, t, 1, :], v[0:r, t, 512:1024]))
                i = d.bn_aggr(bnag[0:r, t, :], bnst[0:r, t, :, :])
            own.then(i)
            d.tensor_scalar(ss[:], bnag[:, :, 1], EPS, None, ALU.add).then_inc(ms_ready, 1)
            d.wait_ge(sq_ready, 2 * TILES + 1)
            own.then(d.reciprocal(rstd[:], rstd[:]))
            for t in range(TILES):
                r = rowsof(t)
                d.tensor_scalar(v[0:r, t, :], v[0:r, t, :], bnag[0:r, t, 0:1], rstd[0:r, t:t + 1],
                                ALU.subtract, ALU.mult).then_inc(v_ready, 1)
            split_lo(0, 2, UNITS_V + 3)
            d.wait_ge(bt_ready, KT)
            for j in range(KT):
                d.wait_ge(z_mm, j + 1)
                d.scalar_tensor_tensor(
                    out=zT[:, j, 0:SEQ].rearrange("p (c t) -> p c t", c=NT),
                    in0=ps[:, ZB[j % 4], :].rearrange("p (c t) -> p c t", c=NT), scalar=hln[:, j, 0:1],
                    in1=bterm[:, j:j + 1, :].broadcast_to([P, NT, P]), op0=ALU.mult, op1=ALU.add).then_inc(z_ready, 1)
            for j in range(KT):
                d.wait_ge(z_mm, KT + 1)
                d.scalar_tensor_tensor(
                    out=zT[:, j, SEQ:TA].rearrange("p (b s) -> p b s", b=DB),
                    in0=ps[:, ZB[0], j * S:(j + 1) * S].rearrange("p (b s) -> p b s", b=DB), scalar=hln[:, j, 0:1],
                    in1=bterm[:, j:j + 1, 0:DS].broadcast_to([P, DB, DS]), op0=ALU.mult, op1=ALU.add).then_inc(z_ready, 1)
            own.then(d.memset(XR[:, 0:3], 0.0))
            xrs = XR[:, 3 + SEQ:XRW].rearrange("p (b s) -> p b s", b=DB)
            smp = lambda t: t[:, SEQ:TA].rearrange("p (b s) -> p b s", b=DB)
            with d.Fori(0, KT) as j:
                own.enter(j, 25)
                col = lambda c, n=1: ch[:, bass.ds(j, 1), c:c + n].rearrange("p a c -> p (a c)")
                n0 = UNITS_V
                d.wait_ge(gates_mm, FIRST + j)
                own.then(d.tensor_copy(xrs[:, :, 0:3], col(C_ST, 24).rearrange("p (b s) -> p b s", b=DB)))
                d.wait_ge(xr_ev, FIRST + j * 2 + 2)
                own.then(d.tensor_scalar(XC[:, 0:SEQ], XR[:, 3:3 + SEQ], col(C_W0 + 3), col(C_CB), ALU.mult, ALU.add))
                own.then(d.tensor_scalar(smp(XC), xrs[:, :, 3:7], col(C_W0 + 3), col(C_CB), ALU.mult, ALU.add))
                for t in range(3):
                    own.then(d.scalar_tensor_tensor(out=XC[:, 0:SEQ], in0=XR[:, t:t + SEQ], scalar=col(C_W0 + t),
                                                    in1=XC[:, 0:SEQ], op0=ALU.mult, op1=ALU.add))
                    i = d.scalar_tensor_tensor(out=smp(XC), in0=xrs[:, :, t:t + 4], scalar=col(C_W0 + t),
                                               in1=smp(XC), op0=ALU.mult, op1=ALU.add)
                    if t < 2:
                        own.then(i)
                own.then(i)
                sj = so[:, bass.ds(j, 1), :].rearrange("p a c -> p (a c)")
                d.tensor_copy(sj[:, 9:12], XR[:, SEQ:SEQ + 3])
                d.tensor_copy(sj[:, 12:36].rearrange("p (b s) -> p b s", b=DB), xrs[:, :, 4:7]).then_inc(conv_done, 1)
                split_lo(1, 3, j * 4 + (n0 + 4))
                d.wait_ge(u_sq, j + 1)
                own.then(d.tensor_scalar(U1[:], U1[:], GELU_C, 1.0, ALU.mult, ALU.add))
                d.tensor_tensor(U1[:], U1[:], U[:], ALU.mult).then_inc(u_poly, 1)
                split_lo(0, 0, j * 4 + (n0 + 5))
                d.wait_ge(u_tanh, j + 1)
                own.then(d.scalar_tensor_tensor(out=U1[:], in0=U1[:], scalar=1.0, in1=U[:], op0=ALU.add, op1=ALU.mult))
                d.tensor_tensor(U1[:], U1[:], zT[:, bass.ds(j, 1), :].rearrange("p a t -> p (a t)"), ALU.mult).then_inc(u_free, 1)
                d.wait_ge(u_free, j + 1)
                d.wait_ge(ga_ev, FIRST + j * 2 + 2)
                d.scalar_tensor_tensor(out=GA[:], in0=GA[:], scalar=1.0, in1=U1[:], op0=ALU.add, op1=ALU.mult).then_inc(ya_done, 1)
                d.wait_ge(a_ready, j * 3 + 3)
                d.scalar_tensor_tensor(out=M[:], in0=M[:], scalar=1.0, in1=TR[:], op0=ALU.add, op1=ALU.mult).then_inc(m_poly, 1)
                own.then(d.scalar_tensor_tensor(out=TI[:], in0=TI[:], scalar=1.0, in1=XC[:], op0=ALU.add, op1=ALU.mult))
                split_lo(1, 1, j * 4 + (n0 + 6))
                d.wait_ge(m_sqrt, j + 1)
                own.then(d.memset(M[:, 0:1], 1.0))
                own.then(d.scalar_tensor_tensor(out=TI[:], in0=TI[:], scalar=0.5, in1=M[:], op0=ALU.mult, op1=ALU.mult))
                own.then(d.tensor_tensor(TR[:, 0:DB], smp(A)[:, :, 0], col(C_H0, DB), ALU.mult))
                own.then(d.tensor_tensor(smp(TI)[:, :, 0], smp(TI)[:, :, 0], TR[:, 0:DB], ALU.add))
                own.then(d.memset(smp(A)[:, :, 0], 0.0))
                own.then(d.tensor_tensor_scan(XC[:], A[:], TI[:], 0.0, ALU.mult, ALU.add))
                own.then(d.tensor_copy(sj[:, 0:1], XC[:, SEQ - 1:SEQ]))
                own.then(d.tensor_copy(sj[:, 1:9], smp(XC)[:, :, DS - 1]))
                d.wait_ge(gb_ev, j * 2 + 2)
                own.then(d.scalar_tensor_tensor(out=M[:, 0:SEQ], in0=ps[:, 3, :], scalar=1.0, in1=XC[:, 0:SEQ],
                                                op0=ALU.add, op1=ALU.mult))
                own.then(d.scalar_tensor_tensor(out=M[:, SEQ:TA], in0=gbs[:], scalar=1.0, in1=XC[:, SEQ:TA],
                                                op0=ALU.add, op1=ALU.mult))
                own.then(d.tensor_tensor(M[:], M[:], GA[:], ALU.add))
                d.wait_ge(v_stored, 32)
                own.then(d.tensor_copy(mh[:, bass.ds(j, 1), :].rearrange("p a t -> p (a t)"), M[:, 0:SEQ]))
                own.then(d.tensor_copy(ms[:, bass.ds(j, 1), :].rearrange("p a t -> p (a t)"), M[:, SEQ:TA]))
                d.tensor_tensor(ml[:, bass.ds(j, 1), :].rearrange("p a t -> p (a t)"), M[:, 0:SEQ],
                                mh[:, bass.ds(j, 1), :].rearrange("p a t -> p (a t)").bitcast(F32),
                                ALU.subtract).then_inc(merged, 1)
                split_lo(0, 2, j * 4 + (n0 + 7))
                own.leave(KT)
            def add_rows(half, t):
                banks, _, fbank = o_banks(half)
                c = slice(half * 512, half * 512 + 512)
                r = rowsof(t)
                bank = banks[t] if t < NT else fbank
                d.scalar_tensor_tensor(out=x1[0:r, t, c], in0=ps[0:r, bank, :], scalar=0.5, in1=x1[0:r, t, c],
                                       op0=ALU.mult, op1=ALU.add).then_inc(x1_ready, 1)

            def x1T_copy(k):
                d.wait_ge(xn2T_mm, k + 1)
                d.tensor_scalar(xn2T[:, k, 0:SEQ], ps[:, XB[k], :], ch[:, k, C_G2:C_G2 + 1], None, ALU.mult).then_inc(xn2T_sb[1], 1)

            for half in range(2):
                for u in range(4):
                    n = UNITS_V + UNITS_J + half * 4 + u
                    if half + u and n + 2 < 48:
                        split_lo(n % 2, (n + 2) % RAW, n + 3)
                    if half and u == 0:
                        d.wait_ge(vfold, 3)
                        add_rows(0, NT)
                    if half and u == 2:
                        x1T_copy(1)
                    if half and u == 3:
                        x1T_copy(3)
                d.wait_ge(unit_done, 44 + 4 * half)
                d.wait_ge(xres_in, 16 * TILES)
                for t in range(NT):
                    add_rows(half, t)
            d.wait_ge(vfold, 4)
            add_rows(1, NT)
            d.wait_ge(so_ready, 1)
            d.wait_ge(n2_sq, 2 * TILES)
            own.then(d.tensor_tensor(ss[:], ss[:], ssa[:], ALU.add))
            d.tensor_scalar(ss[:], ss[:], 1.0 / D, EPS, ALU.mult, ALU.add).then_inc(n2_ms, 1)
            d.wait_ge(n2_sq, 2 * TILES + 1)
            d.reciprocal(rstd[:], rstd[:]).then_inc(n2_ms, 1)
            for k in (5, 7):
                x1T_copy(k)
            d.wait_ge(xn2T_mm, KT + 1)
            d.tensor_tensor(xn2T[:, :, SEQ:TA], ps[:, 0, 0:KT * S].rearrange("p (k s) -> p k s", k=KT),
                            ch[:, :, C_G2:C_G2 + 1].broadcast_to([P, KT, S]), ALU.mult).then_inc(xn2T_sb[1], 1)

            def bc(t, n):
                return t.rearrange("p (t a) -> p t a", a=1).broadcast_to([P, t.shape[1], n])

            def row(t, m):
                return t.rearrange("p (a n) -> p a n", a=1).broadcast_to([P, m, t.shape[1]])

            def first_max(out, keys, maxv, n, mv):
                own.then(d.reduce_max(maxv, keys, axis=AX))
                own.then(d.tensor_tensor(out, keys, bc(maxv, n), ALU.is_ge))
                own.then(d.tensor_tensor(out, out, row(first[:, 0:n], TILES), ALU.mult))
                own.then(d.reduce_max(mv, out, axis=AX))
                own.then(d.tensor_tensor(out, out, bc(mv, n), ALU.is_equal))

            d.wait_ge(lg_mm, 1)
            d.wait_ge(n2_ms, 2)
            d.tensor_copy(lgT[0:NL, 0:SEQ], ps[0:NL, 5, :]).then_inc(lg_sb, 1)
            d.tensor_copy(lgT[0:NL, SEQ:TA], ps[0:NL, 1, 0:S]).then_inc(lg_sb, 1)
            d.wait_ge(lgt_mm, 1)
            lps = ps[:, 0, 0:TILES * NL].rearrange("p (t n) -> p t n", t=TILES)
            g_done = own.mark(d.tensor_tensor(lgg[:], lps[:, :, 0:NG], bc(rstd[:], NG), ALU.mult))
            e_done = own.mark(d.tensor_tensor(lge[:], lps[:, :, NG:NL], bc(rstd[:], NE), ALU.mult))
            own.upto(g_done)
            g_done = own.mark(d.tensor_tensor(lgg[:], lgg[:], row(brt[:, 0:NG], TILES), ALU.add))
            own.upto(e_done)
            own.mark(d.tensor_tensor(lge[:], lge[:], row(brt[:, NG:NL], TILES), ALU.add))
            own.upto(g_done)
            first_max(oh[:], lgg[:], r1[:, 0, :], NG, r1[:, 1, :])
            d.tensor_tensor(r4[:], lgg[:], bc(r1[:, 0, :], NG), ALU.subtract).then_inc(ex_in, 1)
            own.then(d.tensor_scalar(oh[:], oh[:], MASKED, -MASKED, ALU.mult, ALU.add))
            own.then(d.tensor_tensor(lge[:].rearrange("p t (g e) -> p (t g) e", e=EG), lge[:].rearrange("p t (g e) -> p (t g) e", e=EG),
                                     bc(oh[:].rearrange("p t g -> p (t g)"), EG), ALU.add))
            first_max(ohe[:, 0], lge[:], r1[:, 0, :], NE, r1[:, 1, :])
            own.then(d.scalar_tensor_tensor(out=key[:], in0=ohe[:, 0], scalar=-2 * MASKED, in1=lge[:], op0=ALU.mult, op1=ALU.add))
            first_max(ohe[:, 1], key[:], r1[:, 4, :], NE, r1[:, 1, :])
            d.tensor_tensor(mcnt[:, 0:NT, :], ohe[:, 0, 0:NT, :], ohe[:, 1, 0:NT, :], ALU.add)
            own.then(d.tensor_tensor(mcnt[0:S, NT, :], ohe[0:S, 0, NT, :], ohe[0:S, 1, NT, :], ALU.add))
            for t in range(TILES):
                i = d.tensor_tensor(cum[:, t + 1, :], cum[:, t, :], mcnt[:, t, :], ALU.add)
                if t < NT:
                    own.then(i)
            i.then_inc(cnt_in, 1)
            oh10 = ohe[:].rearrange("p s t e -> p (s t) e")
            pick = cmp_[:].rearrange("p (t e) -> p t e", e=NE)

            pick_b = pick2[:].rearrange("p (t e) -> p t e", e=NE)
            one = own.mark(d.tensor_tensor(pick, oh10, row(epair[:], T2), ALU.mult))
            two = own.mark(d.tensor_tensor(pick_b, oh10, row(ehalf[:], T2), ALU.mult))
            own.upto(one)
            own.mark(d.reduce_sum(epr[:], pick, axis=AX))
            own.upto(two)
            own.then(d.reduce_sum(ehf[:], pick_b, axis=AX))
            d.tensor_tensor(r1[:, 2, :], r1[:, 4, :], r1[:, 0, :], ALU.subtract).then_inc(ex_in, 1)
            d.wait_ge(rank_mm, 1)
            nck = MAXCHUNK - 1
            c8 = cmp_[:, 0:NE * nck].rearrange("p (e c) -> p e c", c=nck)
            c10 = pick2[:, 0:T2 * nck].rearrange("p (e c) -> p e c", c=nck)
            a_ = own.mark(d.tensor_tensor(c8, bc(ps[:, 0, TILES * NE:(TILES + 1) * NE], nck), row(caps[:], NE), ALU.is_gt))
            b_ = own.mark(d.tensor_tensor(pick2[:].rearrange("p (s n) -> p s n", s=2), ohe[:].rearrange("p s t e -> p s (t e)"),
                                          row(ps[:, 0, 0:TILES * NE], 2), ALU.mult))
            own.upto(a_)
            a_ = own.mark(d.reduce_sum(xcnt[:, 0, :], c8, axis=AX))
            own.upto(b_)
            b_ = own.mark(d.reduce_sum(rk[:], pick_b, axis=AX))
            own.upto(a_)
            a_ = own.mark(d.tensor_tensor_scan(xcnt[:, 1, :], ones[:, 0:NE], xcnt[:, 0, :], 0.0, ALU.mult, ALU.add))
            own.upto(b_)
            b_ = own.mark(d.tensor_tensor(c10, bc(rk[:], nck), row(caps[:], T2), ALU.is_ge))
            own.upto(a_)
            a_ = own.mark(d.scalar_tensor_tensor(out=xcnt[:, 2, :], in0=xcnt[:, 1, :], scalar=float(PAIRS - 1), in1=xcnt[:, 0, :],
                                                 op0=ALU.add, op1=ALU.subtract))
            own.upto(b_)
            b_ = own.mark(d.reduce_sum(chk[:], c10, axis=AX))
            own.upto(a_)
            a_ = own.mark(d.tensor_tensor(pick, oh10, row(xcnt[:, 2, :], T2), ALU.mult))
            own.upto(b_)
            own.mark(d.tensor_scalar(isx[:], chk[:], 1.0, None, ALU.is_ge))
            own.mark(d.tensor_scalar(is0[:], chk[:], 1.0, None, ALU.is_lt))
            own.mark(d.scalar_tensor_tensor(out=posv[:], in0=chk[:], scalar=-float(CAP), in1=rk[:], op0=ALU.mult, op1=ALU.add))
            b_ = own.mark(d.tensor_tensor(colv[:], chk[:], epr[:], ALU.subtract))
            own.upto(a_)
            a_ = own.mark(d.reduce_sum(ebx[:], pick, axis=AX))
            own.upto(b_)
            b_ = own.mark(d.tensor_tensor(ehf[:], ehf[:], is0[:], ALU.mult))
            own.upto(a_)
            a_ = own.mark(d.tensor_tensor(ebx[:], ebx[:], colv[:], ALU.add))
            own.upto(b_)
            b_ = own.mark(d.tensor_tensor(posv[:], posv[:], ehf[:], ALU.add))
            own.upto(a_)
            a_ = own.mark(d.tensor_tensor(ebx[:], ebx[:], isx[:], ALU.mult))
            own.upto(b_)
            d.tensor_tensor(posh[:, 0:TILES, :], row(iota[:], TILES), bc(posv[:, 0:TILES], P), ALU.is_equal).then_inc(pos_ready, 1)
            own.upto(a_)
            a_ = own.mark(d.tensor_tensor(colv[:], ebx[:], epr[:], ALU.add))
            d.tensor_tensor(posh[:, TILES:T2, :], row(iota[:], TILES), bc(posv[:, TILES:T2], P), ALU.is_equal).then_inc(pos_ready, 1)
            own.upto(a_)
            own.then(d.tensor_tensor(colh[:], row(iota[:, 0:COLS], T2), bc(colv[:], COLS), ALU.is_equal))
            for n in range(2):
                d.tensor_tensor(toks[:, n], colh[:], bc(tokp[:, n, :], COLS), ALU.mult).then_inc(pos_ready, 1)
            own.then(d.tensor_copy(nxi[0:1, 0:1], xcnt[0:1, 1, NE - 1:NE]))
            c17 = key17[0:1, :].rearrange("p (m e) -> p m e", e=NE)
            own.then(d.tensor_tensor(c17, xcnt[0:1, 1:2, :].broadcast_to([1, EXTRA, NE]),
                                     iota[0:1, 0:EXTRA].rearrange("p (m a) -> p m a", a=1).broadcast_to([1, EXTRA, NE]), ALU.is_le))
            own.then(d.reduce_sum(tab[0:1, 1, 0:EXTRA], c17, axis=AX))
            d.tensor_copy(nxi[0:1, 1:1 + EXTRA], tab[0:1, 1, 0:EXTRA]).then_inc(extra_ready, 1)
            d.wait_ge(tab_mm, 1)
            own.then(d.tensor_scalar(tab[:, 0, :], ps[:, 1, 0:COLS], 0.5, OUT_OF_RANGE, ALU.is_lt, ALU.mult))
            own.then(d.tensor_scalar(tab[:, 1, :], ps[:, 1, 0:COLS], TA + 0.5, float(-TA), ALU.is_gt, ALU.mult))
            own.then(d.scalar_tensor_tensor(out=tab[:, 2, :], in0=tab[:, 0, :], scalar=-1.0, in1=ps[:, 1, 0:COLS], op0=ALU.add, op1=ALU.add))
            own.then(d.tensor_copy(idxy[:], tab[:, 2, :]))
            d.tensor_tensor(idxg[:], tab[:, 2, :], tab[:, 1, :], ALU.add).then_inc(tab_ready, 1)
            d.wait_ge(ex_out, 3)
            own.then(d.reduce_sum(r1[:, 1, :], r4[:], axis=AX))
            own.then(d.reciprocal(r1[:, 5, :], r1[:, 1, :]))
            own.then(d.tensor_scalar(r1[:, 6, :], r1[:, 3, :], 1.0, None, ALU.add))
            own.then(d.reciprocal(r1[:, 6, :], r1[:, 6, :]))
            own.then(d.tensor_tensor(gate[:, 0, :], r1[:, 6, :], r1[:, 5, :], ALU.mult))
            own.then(d.tensor_tensor(gate[:, 1, :], gate[:, 0, :], r1[:, 3, :], ALU.mult))

            nx = d.value_load(nxi[0:1, 0:1], min_val=0, max_val=EXTRA)

            def rows_T(G):
                d.wait_ge(xgT_mm, FIRST + G + 1)
                d.tensor_tensor(xgT[:], ps[:, 0:2, :].rearrange("p b (k c) -> p (b k) c", c=P),
                                ch[:, :, C_G2:C_G2 + 1].broadcast_to([P, KT, P]), ALU.mult).then_inc(xgT_sb, 1)

            def gated(G):
                d.wait_ge(silu_done, G + 1)
                d.tensor_tensor(hm[:], hs[:], ps[:, 2, FE:2 * FE], ALU.mult).then_inc(hm_ready, 1)

            rows_T(0)
            with d.Fori(0, nx + (PAIRS - 1)) as G:
                gated(G)
                rows_T(G + 1)
            gated(nx + (PAIRS - 1))
            def mean_square(t):
                r = rowsof(t)
                d.wait_ge(n2_sq, 2 * TILES + 2 + t)
                d.tensor_scalar(ss[0:r, t:t + 1], ss[0:r, t:t + 1], 1.0 / D, EPS, ALU.mult, ALU.add).then_inc(fin_ms, 1)

            def final(t):
                r = rowsof(t)
                d.wait_ge(fin_sq, t + 1)
                own.then(d.reciprocal(rstd[0:r, t:t + 1], rstd[0:r, t:t + 1]))
                d.scalar_tensor_tensor(out=xn2[0:r, t, :], in0=x1[0:r, t, :], scalar=rstd[0:r, t:t + 1], in1=nf[0:r, :],
                                       op0=ALU.mult, op1=ALU.mult).then_inc(fin_ready, 1)

            d.wait_ge(const_in, NCONST)
            for t in range(TILES):
                r = rowsof(t)
                d.wait_ge(back_in[t], 32)
                for s in range(2):
                    d.scalar_tensor_tensor(out=x1[0:r, t, :], in0=gy[0:r, s, t, :], scalar=gate[0:r, s, t:t + 1],
                                           in1=x1[0:r, t, :], op0=ALU.mult, op1=ALU.add).then_inc(comb, 1)
                    if s == 0:
                        d.wait_ge(comb, 2 * t + 1)
                if t >= 1:
                    mean_square(t - 1)
                if t >= 2:
                    final(t - 2)
            final(NT - 1)
            mean_square(NT)
            final(NT)

        @block.tensor
        def _(pe):
            for first_one in (sproj_T, gates_mm, xgT_mm):
                pe.sem_inc(first_one, FIRST)
            def product(out, sh, sl, mh_, ml_, start, stop):
                pe.matmul(out, sh, mh_, start=start, stop=False)
                pe.matmul(out, sl, mh_, start=False, stop=False)
                return pe.matmul(out, sh, ml_, start=False, stop=stop)

            def token_rows(base, half, banks_of, sth, stl, sts, before, after_unit):
                banks, sbank, fbank = banks_of(half)
                for u in range(4):
                    n = base + half * 4 + u
                    slot = n % RAW
                    pe.wait_ge(hi_ready, n + 1)
                    pe.wait_ge(lo_ready, n + 1)
                    wr_ = raw[:, slot, :, :].rearrange("p k c -> p (k c)")
                    for t in range(NT):
                        before(u, t)
                        for kk in range(2):
                            k = 2 * u + kk
                            c = slice(kk * 512, kk * 512 + 512)
                            tok = slice(t * P, t * P + P)
                            product(ps[:, banks[t], :], sth[:, k, tok], stl[:, k, tok], wh[:, n % 2, c], wl[:, n % 2, c],
                                    k == 0, k == KT - 1)
                    before(u, NT)
                    for kk in range(2):
                        k = 2 * u + kk
                        q = k % 4
                        last = pe.matmul(ps[S * q:S * q + S, sbank, :], sts[:, k, :], wr_[:, kk * 512:kk * 512 + 512],
                                         start=k < 4, stop=k >= 4, tile_position=(0, S * q), skip_group_check=True)
                    last.then_inc(unit_done, 1)
                    after_unit(u)

            def fold_rows(bank, count):
                pe.wait_ge(vsum, count)
                pe.matmul(ps[0:S, bank, :], fold[:], sp[:], start=True, stop=True).then_inc(vfold, 1)

            def nothing(*_):
                pass

            def xT(t):
                pe.wait_ge(xn_ready, t + 1)
                if t == NT:
                    for k in range(KT):
                        i = pe.transpose(ps[:, 3, k * S:(k + 1) * S], xt[0:S, NT, k * P:(k + 1) * P], ident[0:S, 0:S])
                    i.then_inc(xT_ready, 1)
                    return
                for b in range(2):
                    if t >= 2:
                        pe.wait_ge(xl_ready, 2 * (t - 2) + b + 1)
                    for k in range(4):
                        i = pe.transpose(ps[:, TB[2 * t + b], k * P:(k + 1) * P],
                                         xt[:, t, (4 * b + k) * P:(4 * b + k + 1) * P], ident[:])
                    i.then_inc(xT_ready, 1)

            def v_before0(u, t):
                if u == 0 and t < NT:
                    xT(t + 1)
                    pe.wait_ge(xl_ready, 2 * t + 2)
                    if t == NT - 1:
                        pe.wait_ge(xs_ready, 1)
                if u == 0 and t == NT:
                    pe.wait_ge(xl_ready, 2 * NT)
                    pe.wait_ge(masks, 6)
                    pe.matmul(ps[:, 7, :], ones[:], wsT[:].rearrange("p h t -> p (h t)"), start=True, stop=True).then_inc(rs_mm, 1)

            pe.wait_ge(masks, 2)
            xT(0)
            token_rows(0, 0, v_banks, xh, xl, xs, v_before0, nothing)

            def v_before(u, t):
                if u == 0 and t == 1:
                    pe.wait_ge(bt_ready, KT)
                if u == 0 and t == 2:
                    pe.wait_ge(v_gelu, 1)
                if u == 0 and t == 3:
                    pe.wait_ge(v_gelu, 2)
                if u == 0 and t == NT:
                    pe.wait_ge(v_gelu, 3)

            def v_after(u):
                if u == 0:
                    fold_rows(v_banks(0)[2], 1)

            token_rows(0, 1, v_banks, xh, xl, xs, v_before, v_after)
            pe.wait_ge(v_gelu, 4)
            fold_rows(v_banks(1)[2], 2)
            def z_mixing():
                pe.wait_ge(masks, 7)
                pe.wait_ge(v_gelu, 2 * TILES)
                pe.wait_ge(v_ready, 1 + TILES)
                for c8 in range(KT):
                    if c8 >= 4:
                        pe.wait_ge(z_ready, c8 - 3)
                    for c in range(NT):
                        i = pe.matmul(ps[:, ZB[c8 % 4], c * P:(c + 1) * P], v[:, c, c8 * P:(c8 + 1) * P], wsT[:, c8 // 2, :],
                                      start=True, stop=True)
                    i.then_inc(z_mm, 1)
                pe.wait_ge(z_ready, 5)
                for c8 in range(KT):
                    i = pe.matmul(ps[:, ZB[0], c8 * S:(c8 + 1) * S], v[0:S, NT, c8 * P:(c8 + 1) * P], bdiag[:, c8 // 2, :],
                                  start=True, stop=True)
                i.then_inc(z_mm, 1)
                pe.wait_ge(z_ready, KT)

            def channel_tile(j, z_here):
                for s in range(RAW):
                    pe.wait_ge(raw_in[s], j * 16 + 48)
                pe.wait_ge(sproj_sb, FIRST + j)
                for k in range(KT):
                    q = k % 4
                    i = pe.matmul(ps[S * q:S * q + S, 6, :].rearrange("p (u c) -> p u c", u=4), xs[:, k, :], raw[:, :, k, :],
                                  start=k < 4, stop=k >= 4, tile_position=(0, S * q), skip_group_check=True)
                i.then_inc(sproj, 1)
                for p, freed in enumerate((xr_ev, u_ev, ga_ev, None)):
                    pe.wait_ge(hi_ready, j * 4 + (UNITS_V + p + 1))
                    pe.wait_ge(lo_ready, j * 4 + (UNITS_V + p + 1))
                    if z_here and p < 2:
                        pe.wait_ge(v_gelu, 2 * TILES - 2 + p)
                    if freed is not None:
                        pe.wait_ge(freed, FIRST + j * 2)
                    else:
                        pe.wait_ge(merged, FIRST + j)
                    for k in range(KT):
                        c = slice(k * P, k * P + P)
                        i = product(ps[:, p, :], wh[:, p % 2, c], wl[:, p % 2, c], xh[:, k, :], xl[:, k, :], k == 0, k == KT - 1)
                    i.then_inc(unit_done, 1)
                    if p == 1 and z_here:
                        z_mixing()
                    if p == 0:
                        pe.wait_ge(sproj_sb, FIRST + j + 1)
                        pe.wait_ge(gates_ev, FIRST + j * 4)
                        for u in range(4):
                            i = pe.matmul(ps[:, 7, u * S:(u + 1) * S], sp[:, u * P:(u + 1) * P], fold[:], start=True, stop=True)
                        i.then_inc(sproj_T, 1)
                    if p == 2:
                        pe.wait_ge(conv_done, FIRST + j + 1)
                        pe.wait_ge(gw_in, j * 16 + 16)
                        pe.wait_ge(sq_sb, j + 1)
                        pe.wait_ge(z_ready, 2 * KT)
                        pe.wait_ge(gates_ev, FIRST + j * 4)
                        for w in range(2):
                            pe.matmul(ps[:, 4 + w, :], gw[:, w, :], XC[:, 0:SEQ], start=True, stop=True)
                            i = pe.matmul(ps[:, 7, (4 + w) * S:(5 + w) * S], gw[:, w, :], XC[:, SEQ:TA], start=True, stop=True)
                        i.then_inc(gates_mm, 1)
            channel_tile(0, True)
            with pe.Fori(1, KT) as j:
                channel_tile(j, False)
            def o_before0(u, t):
                if t == 0:
                    pe.wait_ge(merged, FIRST + 2 * u + 2)
                if u == 0:
                    last = KT * 2 + FIRST
                    for sem_, count in (((xr_ev, last),), ((u_ev, last),), ((ga_ev, last),),
                                        ((gates_ev, 4 * KT + FIRST),), ((sproj_sb, KT + FIRST),))[t]:
                        pe.wait_ge(sem_, count)

            token_rows(UNITS_V + UNITS_J, 0, o_banks, mh, ml, ms, o_before0, nothing)

            def o_before1(u, t):
                if u == 0 and t >= 2:
                    pe.wait_ge(x1_ready, t - 1)

            def x1T(k):
                if k >= 2 and k < 6:
                    pe.wait_ge(xn2T_sb[k % 2], k // 2)
                for t in range(NT):
                    i = pe.transpose(ps[:, XB[k], t * P:(t + 1) * P], x1[:, t, k * P:(k + 1) * P], ident[:])
                i.then_inc(xn2T_mm, 1)

            def logits(k):
                pe.wait_ge(xn2T_sb[k % 2], k // 2 + 1)
                g0 = LG * (k % 2)
                return pe.matmul(ps[g0:g0 + NL, 5, :], wrt[:, k, :], xn2T[:, k, 0:SEQ], start=k < 2, stop=k >= KT - 2,
                                 tile_position=(0, g0), skip_group_check=True)

            def o_after1(u):
                if u == 0:
                    pe.wait_ge(gates_ev, 4 * KT + FIRST)
                    fold_rows(o_banks(0)[2], 3)
                if u == 1:
                    pe.wait_ge(x1_ready, TILES)
                    x1T(0)
                    x1T(1)
                if u == 2:
                    x1T(2)
                    x1T(3)
                    logits(0)
                    logits(1)

            token_rows(UNITS_V + UNITS_J, 1, o_banks, mh, ml, ms, o_before1, o_after1)
            fold_rows(o_banks(1)[2], 4)
            logits(2)
            logits(3)
            pe.wait_ge(x1_ready, TILES + NT)
            for k in range(4, KT):
                x1T(k)
            pe.wait_ge(x1_ready, 2 * TILES)
            for k in range(KT):
                i = pe.transpose(ps[:, 0, k * S:(k + 1) * S], x1[0:S, NT, k * P:(k + 1) * P], ident[0:S, 0:S])
            i.then_inc(xn2T_mm, 1)
            for k in range(4, KT):
                logits(k)
            pe.wait_ge(xn2T_sb[1], KT // 2 + 1)
            for k in range(KT):
                i = pe.matmul(ps[0:NL, 1, 0:S], wrt[:, k, :], xn2T[:, k, SEQ:TA], start=k == 0, stop=k == KT - 1)
            i.then_inc(lg_mm, 1)
            pe.wait_ge(lg_sb, 3)
            for t in range(TILES):
                r = rowsof(t)
                i = pe.matmul(ps[0:r, 0, t * NL:(t + 1) * NL], lgT[0:LG + NL, t * P:t * P + r], fold2[0:LG + NL, :], start=True, stop=True)
            i.then_inc(lgt_mm, 1)
            pe.wait_ge(cnt_in, 1)
            pe.matmul(ps[:, 0, 0:(TILES + 1) * NE], onesb[:], cum[:].rearrange("p t e -> p (t e)"), start=True, stop=False)
            pe.matmul(ps[:, 0, 0:TILES * NE], upperb[:], mcnt[:].rearrange("p t e -> p (t e)"), start=False, stop=True).then_inc(rank_mm, 1)
            for n in range(2 * TILES):
                if n == 0:
                    pe.wait_ge(pos_ready, 4)
                r = rowsof(n % TILES)
                for part in range(2):
                    i = pe.matmul(ps[:, 1, 0:COLS], posh[0:r, n, :], toks[0:r, part, n, :], start=n + part == 0,
                                  stop=n + part == 2 * TILES)
            i.then_inc(tab_mm, 1)

            def transposes(G):
                pe.wait_ge(xg_in, G * 16 + 16)
                pe.wait_ge(xgT_sb, FIRST + G)
                for c in range(KT):
                    l = pe.transpose(ps[:, c // 4, (c % 4) * P:(c % 4 + 1) * P], xg[:, c * P:(c + 1) * P], ident[:])
                l.then_inc(xgT_mm, 1)

            def pair(G, q, halves, weights_in, next_rows):
                pe.wait_ge(xgT_sb, FIRST + G + 1)
                pe.wait_ge(hm_ready, FIRST + G)
                for c in range(KT):
                    if c % 4 == 0:
                        for s in halves:
                            pe.wait_ge(part_in[c // 4][q][s], weights_in)
                    for s in halves:
                        l = pe.matmul(ps[CAP * s:CAP * s + CAP, 2, :], xgT[:, c, CAP * s:CAP * s + CAP],
                                      wslot[q][s][:, c * 512:(c + 1) * 512], start=c == 0, stop=c == KT - 1,
                                      tile_position=(0, CAP * s), skip_group_check=True)
                    if c == 3:
                        l.then_inc(gu_half, 1)
                l.then_inc(gu_mm, 1)
                if next_rows:
                    transposes(G + 1)
                pe.wait_ge(hm_ready, FIRST + G + 1)
                pe.wait_ge(hT_sb, FIRST + G)
                for f in range(2):
                    l = pe.transpose(ps[:, 3, f * P:(f + 1) * P], hm[:, f * P:(f + 1) * P], ident[:])
                l.then_inc(hT_mm, 1)
                pe.wait_ge(hT_sb, FIRST + G + 1)
                for s in halves:
                    pe.wait_ge(part_in[2][q][s], weights_in)
                pe.wait_ge(yo_sb, FIRST + G)
                for f in range(2):
                    for h in range(2):
                        for s in halves:
                            o = GU + f * D + h * 512
                            l = pe.matmul(ps[CAP * s:CAP * s + CAP, 6 + h, :], hT[:, f, CAP * s:CAP * s + CAP],
                                          wslot[q][s][:, o:o + 512], start=f == 0, stop=f == 1,
                                          tile_position=(0, CAP * s), skip_group_check=True)
                l.then_inc(pair_mm, 1)

            transposes(0)
            with pe.Fori(0, PAIRS // 3) as i:
                for q in range(3):
                    pair(i * 3 + q, q, (0, 1), i * 16 + 16, True)
            pair(PAIRS - 1, 0, (0, 1), 16 * (PAIRS // 3 + 1), False)
            pe.wait_ge(extra_ready, 1)
            nx = pe.value_load(nxi[0:1, 0:1], min_val=0, max_val=EXTRA)
            with pe.If(nx > 0):
                with pe.Fori(0, nx) as m:
                    transposes(m + PAIRS)
                    pair(m + PAIRS, 1, (0,), m * 16 + 16 * (PAIRS // 3 + 1), False)


_INS = ["x", "wmix", "wgate", "chan", "wst", "bs", "rows", "wr", "br", "wmoe"]
_OUTS = [("y", (TA, D)), ("vp", (P, D)), ("vs", (S, D)), ("st", (P, KT, OUTC))]


def lay_out(np, i):
    f = lambda n: np.asarray(i[n])
    cat = np.concatenate
    x = cat([f("x_prompt").reshape(SEQ, D), f("x_sample").reshape(S, D)])
    w_in = f("w_in")[0].reshape(KT, P, 5, D)

    def token_units(w):
        return w.reshape(4, 2, P, 2, 512).transpose(3, 0, 2, 1, 4).reshape(8, P, KT, P)

    order = [2, 0, 3, 4]
    jw = w_in[:, :, order, :].reshape(KT, P, 4, KT, P).transpose(3, 2, 1, 0, 4).reshape(UNITS_J, P, KT, P)
    wmix = cat([token_units(w_in[:, :, 1, :]), jw, token_units(f("w_out")[0].reshape(KT, P, D))])
    wgate = np.stack([f("w_rg_a")[0], f("w_rg_x")[0]], axis=2)
    per = lambda a: a.reshape(-1, KT, P).transpose(2, 1, 0)
    chan = cat([per(f("norm1")[0]), per(f("conv_w")[0]), per(f("conv_b")[0]), per(f("lru_lambda")[0]),
                per(f("b_rg_a")[0].reshape(-1)), per(f("b_rg_x")[0].reshape(-1)), per(f("state_lru_h")[0]),
                per(f("state_conv")[0].reshape(-1, D)),
                per(f("norm2")[0]), per(f("ln_g")[0]), per(f("ln_b")[0])], axis=2)
    wst = f("w_s")[0].transpose(2, 0, 1)
    bs = f("b_s")[0].reshape(1, HEADS * P)
    rows = np.stack([f("ln_g")[0], f("ln_b")[0], f("norm_f"), f("norm1")[0]])
    wr = cat([f("w_route_group")[0], f("w_route_expert")[0]], axis=1).reshape(KT, P, NL).transpose(1, 0, 2)
    br = cat([f("b_route_group")[0], f("b_route_expert")[0]]).reshape(1, NL)
    gu = cat([f("w_gate")[0], f("w_up")[0]], axis=2).reshape(NE, KT, P, 512).transpose(0, 2, 1, 3).reshape(NE, P, KT * 512)
    wd = f("w_down")[0].reshape(NE, 2, P, D).transpose(0, 2, 1, 3).reshape(NE, P, 2 * D)
    wmoe = cat([gu, wd], axis=2)
    return dict(x=x, wmix=wmix, wgate=wgate, chan=chan, wst=wst, bs=bs, rows=rows, wr=wr, br=br, wmoe=wmoe)


def kernel(**inputs):
    import numpy as _np
    import concourse.bacc as _bacc
    from concourse.bass_utils import run_bass_kernel_spmd as _run

    nc = _bacc.Bacc("TRN2", target_bir_lowering=False, num_devices=1)
    laid = lay_out(_np, inputs)
    arrays, args = {}, []
    for name in _INS:
        a = _np.ascontiguousarray(laid[name])
        arrays[f"in_{name}"] = a
        args.append(nc.dram_tensor(f"in_{name}", a.shape, mybir.dt.from_np(a.dtype), kind="ExternalInput").ap())
    for name, shape in _OUTS:
        args.append(nc.dram_tensor(f"out_{name}", shape, F32, kind="ExternalOutput").ap())
    build(nc, *args)
    r = _run(nc, [arrays], core_ids=[0])
    y, vp, vs, st = (_np.asarray(r.results[0][f"out_{n}"]) for n, _ in _OUTS)
    st = st.transpose(2, 1, 0).reshape(OUTC, D)
    return (y[:SEQ].reshape(1, SEQ, D), y[SEQ:].reshape(DB, DS, D),
            st[0].reshape(1, 1, D), st[9:12].reshape(1, 1, 3, D), vp.reshape(1, 1, P, D),
            st[1:9].reshape(1, DB, D), st[12:36].reshape(1, DB, 3, D), vs.reshape(1, DB, DS, D))
```
